# Optimizing a Trainium2 kernel written in Bass

```python
import jax, jax.numpy as jnp
from jax import lax
import numpy as np

D_MODEL = 1024
BATCH = 1
SEQ = 512
DEPTH = 1
DEC_BATCH = 8
DEC_SEQ = 8
PAST_LEN = 4096
PAGE_SIZE = 128

PLE_DIM = 256
CONV_CH = D_MODEL // 2
CONV_K = 31
RET_WIDTH = D_MODEL - CONV_CH
RET_HEADS = 4
RET_HEAD_DIM = RET_WIDTH // RET_HEADS
CHUNK = 128
ROPE_BASE = 10000.0
N_GROUPS = 4
EXPERTS_PER_GROUP = 8
N_EXPERTS = N_GROUPS * EXPERTS_PER_GROUP
TOP_K = 2
EXPERT_FF = D_MODEL // 4
IN_COLS = 2 * CONV_CH + 4 * RET_WIDTH
EPS = 1e-6

kernel_name = "hymba_conformer_retnet_hmoe_step"

def rmsnorm(x, g):
    xf = x.astype(jnp.float32)
    y = xf * lax.rsqrt(jnp.mean(xf * xf, axis=-1, keepdims=True) + EPS)
    return (y * g.astype(jnp.float32)).astype(x.dtype)

def layernorm(x, g, b):
    xf = x.astype(jnp.float32)
    mu = jnp.mean(xf, axis=-1, keepdims=True)
    var = jnp.mean(jnp.square(xf - mu), axis=-1, keepdims=True)
    y = (xf - mu) * lax.rsqrt(var + EPS)
    return (y * g.astype(jnp.float32) + b.astype(jnp.float32)).astype(x.dtype)

def rope(x, pos0):
    l, d = x.shape[1], x.shape[-1]
    half = d // 2
    inv = ROPE_BASE ** (-jnp.arange(half, dtype=jnp.float32) / half)
    pos = jnp.arange(l, dtype=jnp.float32) + jnp.float32(pos0)
    ang = pos[:, None] * inv[None, :]
    cos = jnp.cos(ang)[None, :, None, :]
    sin = jnp.sin(ang)[None, :, None, :]
    xf = x.astype(jnp.float32)
    x1, x2 = xf[..., :half], xf[..., half:]
    return jnp.concatenate([x1 * cos - x2 * sin, x1 * sin + x2 * cos], axis=-1).astype(x.dtype)

def causal_depthwise_conv(u, buf, w, b):
    ext = jnp.concatenate([buf.astype(u.dtype), u], axis=1)
    out = lax.conv_general_dilated(
        ext, w[:, None, :].astype(u.dtype), window_strides=(1,), padding='VALID',
        dimension_numbers=('NWC', 'WIO', 'NWC'), feature_group_count=u.shape[-1])
    return out + b, ext[:, -(CONV_K - 1):]

def retention(q, k, v, r0):
    n, l, hh, dk = q.shape
    dv = v.shape[-1]
    c = CHUNK if l % CHUNK == 0 else l
    nc = l // c

    def blocks(x):
        return x.astype(jnp.float32).reshape(n, nc, c, hh, x.shape[-1]).transpose(1, 0, 3, 2, 4)

    lg = jnp.log(1.0 - 2.0 ** (-5.0 - jnp.arange(hh, dtype=jnp.float32)))
    idx = jnp.arange(c, dtype=jnp.float32)
    rel = idx[:, None] - idx[None, :]
    dmat = jnp.where(rel[None] >= 0, jnp.exp(jnp.maximum(rel, 0.0)[None] * lg[:, None, None]), 0.0)
    xi = jnp.exp((idx + 1.0)[None, :] * lg[:, None])
    zeta = jnp.exp((c - 1.0 - idx)[None, :] * lg[:, None])
    gc = jnp.exp(c * lg)

    def step(r, blk):
        qc, kc, vc = blk
        s = jnp.einsum('nhid,nhjd->nhij', qc, kc) * dmat
        o = (jnp.einsum('nhij,nhje->nhie', s, vc)
             + jnp.einsum('nhid,nhde->nhie', qc, r) * xi[:, :, None])
        r = r * gc[:, None, None] + jnp.einsum('nhjd,nhje->nhde', kc * zeta[:, :, None], vc)
        return r, o

    r, o = lax.scan(step, r0.astype(jnp.float32), (blocks(q), blocks(k), blocks(v)))
    o = o.transpose(1, 0, 3, 2, 4).reshape(n, l, hh, dv)
    return o, r

def token_mix(h, conv_buf, ret_state, pos0, w_in, conv_w, conv_b, conv_ln_g, conv_ln_b, w_out):
    n, l, _ = h.shape
    z = h @ w_in
    a, b, q, k, v, g = jnp.split(
        z, [CONV_CH, 2 * CONV_CH, 2 * CONV_CH + RET_WIDTH, 2 * CONV_CH + 2 * RET_WIDTH,
            2 * CONV_CH + 3 * RET_WIDTH], axis=-1)
    u = a * jax.nn.sigmoid(b)
    c, new_buf = causal_depthwise_conv(u, conv_buf, conv_w, conv_b)
    c = jax.nn.silu(layernorm(c, conv_ln_g, conv_ln_b))
    q = rope(q.reshape(n, l, RET_HEADS, RET_HEAD_DIM), pos0)
    k = rope(k.reshape(n, l, RET_HEADS, RET_HEAD_DIM), pos0) * (RET_HEAD_DIM ** -0.5)
    v = v.reshape(n, l, RET_HEADS, RET_HEAD_DIM)
    o, new_state = retention(q, k, v, ret_state)
    mu = jnp.mean(o, axis=-1, keepdims=True)
    var = jnp.mean(jnp.square(o - mu), axis=-1, keepdims=True)
    o = ((o - mu) * lax.rsqrt(var + EPS)).reshape(n, l, RET_WIDTH).astype(g.dtype)
    o = jax.nn.silu(g) * o
    y = jnp.concatenate([c, o], axis=-1) @ w_out
    return y, new_buf, new_state

def hier_moe(h, rg_w, rg_b, re_w, re_b, w_gate, w_up, w_down):
    n, l, d = h.shape
    t = h.reshape(n * l, d)
    g_prob = jax.nn.softmax((t @ rg_w + rg_b).astype(jnp.float32), axis=-1)
    g_top, g_idx = lax.top_k(g_prob, 1)
    e_logit = (t @ re_w + re_b).astype(jnp.float32).reshape(-1, N_GROUPS, EXPERTS_PER_GROUP)
    e_logit = jnp.take_along_axis(e_logit, g_idx[:, :, None], axis=1)[:, 0]
    e_top, e_idx = lax.top_k(jax.nn.softmax(e_logit, axis=-1), TOP_K)
    e_top = e_top / jnp.sum(e_top, axis=-1, keepdims=True)
    gate = g_top * e_top
    eid = g_idx * EXPERTS_PER_GROUP + e_idx
    combine = jnp.sum(jax.nn.one_hot(eid, N_EXPERTS, dtype=jnp.float32) * gate[..., None], axis=1)
    hid = jax.nn.silu(jnp.einsum('td,edf->tef', t, w_gate)) * jnp.einsum('td,edf->tef', t, w_up)
    hid = hid * combine[..., None].astype(hid.dtype)
    y = jnp.einsum('tef,efd->td', hid, w_down)
    return y.reshape(n, l, d)

def layer(x, p, conv_buf, ret_state, pos0, w_in, conv_w, conv_b, conv_ln_g, conv_ln_b, w_out,
          norm1_g, norm2_g, rg_w, rg_b, re_w, re_b, w_gate, w_up, w_down, w_ple, ple_norm_g, w_ple_gate):
    mix, new_buf, new_state = token_mix(rmsnorm(x, norm1_g), conv_buf, ret_state, pos0,
                                        w_in, conv_w, conv_b, conv_ln_g, conv_ln_b, w_out)
    x = x + mix
    x = x + hier_moe(rmsnorm(x, norm2_g), rg_w, rg_b, re_w, re_b, w_gate, w_up, w_down)
    ple = rmsnorm(p @ w_ple, ple_norm_g)
    x = x + ple * jax.nn.sigmoid(x @ w_ple_gate)
    return x, new_buf, new_state

def setup_inputs(seed: int = 0) -> dict:
    key = jax.random.key(seed)
    ks = jax.random.split(key, 32)
    f32 = jnp.float32
    nrm = lambda k, shape, s: jax.random.normal(k, shape, f32) * s
    return {
        "x_prompt": nrm(ks[0], (BATCH, SEQ, D_MODEL), 1.0),
        "x_sample": nrm(ks[1], (DEC_BATCH, DEC_SEQ, D_MODEL), 1.0),
        "p_prompt": nrm(ks[2], (DEPTH, BATCH, SEQ, PLE_DIM), 1.0),
        "p_sample": nrm(ks[3], (DEPTH, DEC_BATCH, DEC_SEQ, PLE_DIM), 1.0),
        "state_conv": nrm(ks[4], (DEPTH, DEC_BATCH, CONV_K - 1, CONV_CH), 0.5),
        "state_ret": nrm(ks[5], (DEPTH, DEC_BATCH, RET_HEADS, RET_HEAD_DIM, RET_HEAD_DIM), 0.1),
        "w_in": nrm(ks[6], (DEPTH, D_MODEL, IN_COLS), D_MODEL ** -0.5),
        "conv_w": nrm(ks[7], (DEPTH, CONV_K, CONV_CH), CONV_K ** -0.5),
        "conv_b": nrm(ks[8], (DEPTH, CONV_CH), 0.01),
        "conv_ln_g": 1.0 + nrm(ks[9], (DEPTH, CONV_CH), 0.01),
        "conv_ln_b": nrm(ks[10], (DEPTH, CONV_CH), 0.01),
        "w_out": nrm(ks[11], (DEPTH, D_MODEL, D_MODEL), D_MODEL ** -0.5),
        "norm1_g": 1.0 + nrm(ks[12], (DEPTH, D_MODEL), 0.01),
        "norm2_g": 1.0 + nrm(ks[13], (DEPTH, D_MODEL), 0.01),
        "router_group_w": nrm(ks[14], (DEPTH, D_MODEL, N_GROUPS), D_MODEL ** -0.5),
        "router_group_b": nrm(ks[15], (DEPTH, N_GROUPS), 0.01),
        "router_expert_w": nrm(ks[16], (DEPTH, D_MODEL, N_EXPERTS), D_MODEL ** -0.5),
        "router_expert_b": nrm(ks[17], (DEPTH, N_EXPERTS), 0.01),
        "w_expert_gate": nrm(ks[18], (DEPTH, N_EXPERTS, D_MODEL, EXPERT_FF), D_MODEL ** -0.5),
        "w_expert_up": nrm(ks[19], (DEPTH, N_EXPERTS, D_MODEL, EXPERT_FF), D_MODEL ** -0.5),
        "w_expert_down": nrm(ks[20], (DEPTH, N_EXPERTS, EXPERT_FF, D_MODEL), EXPERT_FF ** -0.5),
        "w_ple": nrm(ks[21], (DEPTH, PLE_DIM, D_MODEL), PLE_DIM ** -0.5),
        "ple_norm_g": 1.0 + nrm(ks[22], (DEPTH, D_MODEL), 0.01),
        "w_ple_gate": nrm(ks[23], (DEPTH, D_MODEL, D_MODEL), D_MODEL ** -0.5),
        "final_norm_g": 1.0 + nrm(ks[24], (D_MODEL,), 0.01),
    }

def reference(x_prompt, x_sample, p_prompt, p_sample, state_conv, state_ret,
              w_in, conv_w, conv_b, conv_ln_g, conv_ln_b, w_out, norm1_g, norm2_g,
              router_group_w, router_group_b, router_expert_w, router_expert_b,
              w_expert_gate, w_expert_up, w_expert_down, w_ple, ple_norm_g, w_ple_gate,
              final_norm_g):
    hp = x_prompt
    hs = x_sample
    conv_p, ret_p, conv_s, ret_s = [], [], [], []
    for i in range(DEPTH):
        w = (w_in[i], conv_w[i], conv_b[i], conv_ln_g[i], conv_ln_b[i], w_out[i], norm1_g[i], norm2_g[i],
             router_group_w[i], router_group_b[i], router_expert_w[i], router_expert_b[i],
             w_expert_gate[i], w_expert_up[i], w_expert_down[i], w_ple[i], ple_norm_g[i], w_ple_gate[i])
        buf0 = jnp.zeros((hp.shape[0], CONV_K - 1, CONV_CH), hp.dtype)
        st0 = jnp.zeros((hp.shape[0], RET_HEADS, RET_HEAD_DIM, RET_HEAD_DIM), jnp.float32)
        hp, nb, ns = layer(hp, p_prompt[i], buf0, st0, 0, *w)
        conv_p.append(nb)
        ret_p.append(ns)
        hs, nb, ns = layer(hs, p_sample[i], state_conv[i], state_ret[i], PAST_LEN, *w)
        conv_s.append(nb)
        ret_s.append(ns)
    y_prompt = rmsnorm(hp, final_norm_g)
    y_sample = rmsnorm(hs, final_norm_g)
    return (y_prompt, y_sample, jnp.stack(conv_p), jnp.stack(ret_p), jnp.stack(conv_s), jnp.stack(ret_s))


_drawn_inputs = setup_inputs


def setup_inputs(seed=0):
    import zlib

    import numpy as np

    out = dict(_drawn_inputs(seed))
    spreads = {}
    factors = {'conv_b': 3.106,
     'conv_ln_g': 35.256,
     'conv_ln_b': 26.472,
     'norm1_g': 11.351,
     'router_group_b': 47.689,
     'router_expert_b': 23.04,
     'ple_norm_g': 200.0,
     'final_norm_g': 186.458,
     'norm2_g': 6.416,
     'state_ret': 4.308}
    for name, (base, spread) in spreads.items():
        noise = np.random.default_rng([zlib.crc32(name.encode()), seed]).standard_normal(out[name].shape)
        drawn = base * np.exp(spread * noise) if base else spread * noise
        out[name] = __import__('jax').numpy.asarray(drawn.astype(out[name].dtype))
    for name, factor in factors.items():
        out[name] = (out[name] * factor).astype(out[name].dtype)
    return out
```

```python
from contextlib import ExitStack

import numpy as np

import concourse.bass as bass
from concourse import mybir

F32 = mybir.dt.float32
I32 = mybir.dt.int32
ALU = mybir.AluOpType
ACT = mybir.ActivationFunctionType
AX = mybir.AxisListType

P = 128
D = 1024
KT = D // P
SEQ = 512
NB, NL = 8, 8
NS = NB * NL
T = SEQ + NS
TT = 5
CH, CT = 512, 4
TAPS = 31
HIST = TAPS - 1
NH, HD = 4, 128
PLE = 256
NG, NEG = 4, 8
NE = NG * NEG
FF = 256
EPS = 1e-6
SLOTS = 128
DEEP = -(-T // SLOTS)
NOV = (2 * T - NE) // SLOTS if SLOTS < 128 else 8
NBLK = NE + NOV
RING = 6
CHUNK = 2048
GAMMA = [1.0 - 2.0 ** (-5.0 - h) for h in range(NH)]

COLS = {}
_at = 0
for _name, _n in (("ident", P), ("ones", P), ("before", P), ("decay", NH * P), ("xi", NH * P), ("zeta", NH),
                  ("decay_s", NH * NS), ("zeta_s", NH), ("eye8", NB * NB), ("row8", NB), ("rope", TT * 2 * 64),
                  ("lane", P), ("block", NBLK), ("expert", NE), ("code", TT * 2), ("rev", NEG), ("ovj", NOV)):
    COLS[_name] = (_at, _n)
    _at += _n
NCONST = _at


def rows(i):
    return P if i < TT - 1 else NS


def constants():
    c = np.zeros((P, NCONST), np.float64)

    def put(name, value):
        a, n = COLS[name]
        v = np.asarray(value, np.float64)
        c[: v.shape[0], a:a + n] = v.reshape(v.shape[0], n)

    lg = np.array([np.log(g) for g in GAMMA])
    p = np.arange(P)
    put("ident", np.eye(P))
    put("ones", np.ones((P, P)))
    put("before", p[:, None] < p[None, :])
    scale = HD ** -0.5
    rel = p[None, :] - p[:, None]
    put("decay", np.stack([np.where(rel >= 0, np.exp(np.maximum(rel, 0) * g), 0.0) * scale for g in lg], 1))
    put("xi", np.broadcast_to(np.stack([np.exp((p + 1) * g) for g in lg])[None], (P, NH, P)))
    put("zeta", np.stack([np.exp((P - 1 - p) * g) * scale for g in lg], 1))
    s = np.arange(NS)
    rs = s[None, :] - s[:, None]
    same = (s[None, :] // NL == s[:, None] // NL) & (rs >= 0)
    put("decay_s", np.stack([np.where(same, np.exp(np.maximum(rs, 0) * g), 0.0) * scale for g in lg], 1))
    put("zeta_s", np.stack([np.exp((NL - 1 - s % NL) * g) * scale for g in lg], 1))
    put("eye8", np.broadcast_to(np.eye(NB).reshape(1, -1), (P, NB * NB)))
    put("row8", (s[:, None] // NL == np.arange(NB)[None, :]))
    inv = (10000.0 ** (-np.arange(64, dtype=np.float64) / 64)).astype(np.float32)
    pos = np.zeros((P, TT), np.float32)
    for i in range(TT - 1):
        pos[:, i] = i * P + p
    pos[:NS, TT - 1] = 4096 + s % NL
    ang = (pos[:, :, None] * inv[None, None, :]).astype(np.float64)
    put("rope", np.stack([np.cos(ang), np.sin(ang)], 2))
    put("lane", np.broadcast_to(p[None].astype(float), (P, P)))
    put("block", np.broadcast_to(np.arange(NBLK)[None].astype(float), (P, NBLK)))
    put("expert", np.broadcast_to(np.arange(NE)[None].astype(float), (P, NE)))
    tok = np.arange(TT)[None, :] * P + p[:, None]
    put("code", np.stack([2 * tok + 1, 2 * tok + 2], 2))
    put("rev", np.broadcast_to((NEG - np.arange(NEG))[None].astype(float), (P, NEG)))
    put("ovj", np.broadcast_to(np.arange(NOV)[None].astype(float), (P, NOV)))
    return c.astype(np.float32)


def bc(ap, axis, n):
    a = ap.unsqueeze(axis)
    shape = list(a.shape)
    shape[axis] = n
    return a.to_broadcast(shape)


def build(nc, ins, outs):
    (x_prompt, x_sample, p_prompt, p_sample, state_conv, state_ret, w_in, conv_w, conv_b, conv_ln_g, conv_ln_b,
     w_out, norm1_g, norm2_g, rg_w, rg_b, re_w, re_b, w_gate, w_up, w_down, w_ple, ple_norm_g, w_ple_gate,
     final_norm_g, consts_d) = ins
    y_prompt, y_sample, conv_p, ret_p, conv_s, ret_s = outs
    h2_d = nc.dram_tensor("h2_rows", (T, D), F32, kind="Internal").ap()
    moe_d = nc.dram_tensor("expert_rows", (2 * T, D), F32, kind="Internal").ap()

    with ExitStack() as ctx:
        def sb(name, shape, dt=F32):
            return ctx.enter_context(nc.sbuf_tensor(name, shape, dt))

        def sem(name):
            return ctx.enter_context(nc.semaphore(name))

        ring = sb("ring", [P, RING, CHUNK])
        const = sb("const", [P, NCONST])
        hT = sb("hT", [P, KT, T])
        front = sb("front", [P, TT * D])
        scratch = sb("scratch", [P, CT * T])
        z = sb("z", [P, TT, 4, 512])
        uext = sb("uext", [P, CT, HIST + SEQ])
        sext = sb("sext", [P, CT, NB, HIST + NL])
        cv = sb("cv", [P, CT * T])
        catT = sb("catT", [P, KT, T])
        kz = sb("kz", [P, 512])
        Rst = sb("Rst", [P, NH, HD])
        qTs = sb("qTs", [P, NH, P])
        qTx = sb("qTx", [P, NH, P])
        kTs = sb("kTs", [P, NH, P])
        Sm = sb("Sm", [P, NH, P])
        gbc = sb("gbc", [P, D])
        g1c = sb("g1c", [P, KT])
        cpar = sb("cpar", [P, CT, TAPS + 3])
        ssq = sb("ssq", [P, TT])
        rst = sb("rst", [P, TT])
        ssq2 = sb("ssq2", [P, TT])
        rst2 = sb("rst2", [P, TT])
        ssq3 = sb("ssq3", [P, TT, 2])
        rst3 = sb("rst3", [P, TT])
        ssq4 = sb("ssq4", [P, TT])
        rst4 = sb("rst4", [P, TT])
        bns = sb("bns", [P, NH, 6])
        mv = sb("mv", [P, NH, 2])
        grs = sb("grs", [P, NH])
        half = sb("half", [P, NH])
        epsb = sb("epsb", [P, 1])
        tokidx = sb("tokidx", [P, NBLK], I32)
        codes = sb("codes", [P, NBLK], I32)
        cur_tok = sb("cur_tok", [P, 2], I32)
        cur_code = sb("cur_code", [P, 2], I32)
        ovinfo = sb("ovinfo", [1, NOV + 1], I32)
        gates = sb("gates", [P, TT, 2])
        wr = sb("wr", [P, KT, NG + NE])
        rbias = sb("rbias", [P, NG + NE])

        def view(t, off, dims):
            n = int(np.prod(dims))
            flat = t[:, off:off + n]
            if len(dims) == 1:
                return flat
            names = "abcd"[: len(dims)]
            return flat.rearrange("p (" + " ".join(names) + ") -> p " + " ".join(names),
                                  **{k: v for k, v in zip(names[1:], dims[1:])})

        flat_cat = catT[:, :, :].rearrange("p k t -> p (k t)")
        flat_u = uext[:, :, :].rearrange("p c t -> p (c t)")
        flat_s = sext[:, :, :, :].rearrange("p c b t -> p (c b t)")
        flat_z = z[:, :, :, :].rearrange("p i j n -> p (i j n)")
        flat_h = hT[:, :, :].rearrange("p k t -> p (k t)")
        x_sb = view(front, 0, (TT, D))
        states = view(front, 0, (NB, NH, HD))
        xn = view(scratch, 0, (2, D))
        squares = view(scratch, 0, (CT, T))
        conv = view(cv, 0, (CT, T))
        p_sb = view(cv, 0, (TT, PLE))
        cpar_rows = flat_z[0:TAPS + 3, 0:CH]
        hist_rows = flat_z[0:120, CH:3 * CH].rearrange("p (a c) -> p a c", a=2)
        sig = flat_cat[:, 0:2 * T].rearrange("p (a t) -> p a t", a=2)
        tails = flat_cat[:, 4 * T:4 * T + 2 * CH].rearrange("p (a c) -> p a c", a=2)
        qmask = flat_u[:, 0:NH * NB * NS].rearrange("p (h b t) -> p h b t", h=NH, b=NB)
        vmask = flat_s[0:NS, 0:NB * HD].rearrange("p (b e) -> p b e", b=NB)
        pT = flat_u[:, 0:2 * T].rearrange("p (k t) -> p k t", k=2)
        pbc = flat_s[:, 0:D]
        rt = [0]

        def work(n):
            rt[0] += n
            return flat_cat[:, rt[0] - n:rt[0]]

        logit = work(TT * 36).rearrange("p (i n) -> p i n", i=TT)
        gmx, gsum, m1, m2, e2, t1 = (work(TT) for _ in range(6))
        gexp = work(TT * NG).rearrange("p (i n) -> p i n", i=TT)
        gval = work(TT * NG).rearrange("p (i n) -> p i n", i=TT)
        gone = work(TT * NG).rearrange("p (i n) -> p i n", i=TT)
        sel = work(TT * NE).rearrange("p (i g e) -> p i g e", i=TT, g=NG)
        el = work(TT * NEG).rearrange("p (i n) -> p i n", i=TT)
        eval_ = work(TT * NEG).rearrange("p (i n) -> p i n", i=TT)
        one1 = work(TT * NEG).rearrange("p (i n) -> p i n", i=TT)
        one2 = work(TT * NEG).rearrange("p (i n) -> p i n", i=TT)
        M = [work(TT * NE).rearrange("p (i n) -> p i n", i=TT) for _ in range(2)]
        both = work(TT * NE).rearrange("p (i n) -> p i n", i=TT)
        rank = work((TT + 1) * NE).rearrange("p (i n) -> p i n", i=TT + 1)
        deep = work(TT * NE).rearrange("p (i n) -> p i n", i=TT)
        flag = work(TT * NE).rearrange("p (i n) -> p i n", i=TT)
        blk = work(TT * NE).rearrange("p (i n) -> p i n", i=TT)
        lane = work(TT * NE).rearrange("p (i n) -> p i n", i=TT)
        prod = work(TT * NE).rearrange("p (i n) -> p i n", i=TT)
        ov = work(NE)
        ovi = work(NE)
        ovb = work(NE)
        ovw = work(NE)
        zero32 = work(NE)
        posb = work(2 * TT).rearrange("p (a i) -> p a i", a=2)
        posl = work(2 * TT).rearrange("p (a i) -> p a i", a=2)
        laneone = work(2 * P).rearrange("p (a n) -> p a n", a=2)
        blockone = work(2 * NBLK).rearrange("p (a n) -> p a n", a=2)
        tabf = work(NBLK)
        tabz = work(NBLK)
        ovt = work(2 * NOV * NE).rearrange("p (a j e) -> p a j e", a=2, j=NOV)
        ovf = work(NOV + 1)
        assert rt[0] <= KT * T, rt[0]
        junk = view(front, 4 * D, (D,))
        X = view(scratch, 0, (2, D))
        XT = flat_h[:, 0:2 * D].rearrange("p (a k s) -> p a k s", a=2, k=KT)
        hid = view(cv, 0, (2, FF))
        gat = view(cv, 2 * FF, (2, FF))
        hidT = view(cv, 4 * FF, (2, 2, P))
        yout = view(front, 0, (2, D))
        yin = flat_u[:, 0:2 * D].rearrange("p (a n) -> p a n", a=2)
        yin2 = flat_cat[:, 0:2 * D].rearrange("p (a n) -> p a n", a=2)
        yins = [yin, yin2]
        sg = view(scratch, 0, (2, D))
        yo = view(front, 0, (2, D))
        xt = view(front, 2 * D, (2, D))

        def C(name, r=P):
            a, n = COLS[name]
            return const[0:r, a:a + n]

        ident = C("ident")
        rope_t = C("rope").rearrange("p (i c n) -> p i c n", i=TT, c=2)

        bank = [ctx.enter_context(nc.psum_tensor(f"bank{i}", [P, 512], F32)) for i in range(8)]

        def pair(b):
            return [bank[b], bank[b + 1]]

        names = """const_in params_in hist_in states_in router_in gbc_in final_in pbc_in p_in cpar_T hist_T xT_ps
            ab_done mean_done var_done z_done qk_T s_done o_done kvs_done oT_done tail_T wo_done pT_ps
            ple_done h2T_ps logit_done rank_done table_done gu_done xt_ps hT_ps d_done cpar_sb hist_sb hT_sb
            u_done sig_done convp convs cmean csq cstd crstd cdone z_sb rope_done qT_sb qTx_sb kT_sb s_sb
            kz_done gn_var gn_rstd on_done og_done oT_sb r_upd tail_u tail_sb tail_out qm_done vm_done
            rs_upd rs_out rp_out x1_sum x1_sq x1_std x1_rstd h2_done h2T_sb xsq xstd xrstd xn_done zeroed
            dve_order pool_order pT_sb ple_sq ple_var ple_std ple_rstd ple_sb logit_sb gexp_done picks_done
            laneone_done table_sb idx_done xt_sb sil_done hid_done hT_ev y_ready zero_x cur_done pool_codes
            ticks moe_out ov_load ov_gather ov_cur ov_xt ov_xtsb ov_gu ov_sil ov_hid ov_hT ov_hTsb ov_d ov_y
            ov_out ov_end x2_done x2T_ps x2T_low x2T_high pg_done sg_done x3_done x3_sq x3_std x3_rstd
            out_done cs_copy x2_order""".split()
        S = {n: sem(n) for n in names}
        x_in = [sem(f"x_in{i}") for i in range(TT)]
        x_back = [sem(f"x_back{i}") for i in range(TT)]
        slot_in = [sem(f"slot_in{i}") for i in range(RING)]
        h2_out = [sem(f"h2_out{i}") for i in range(2)]
        y_stored = [sem(f"y_stored{i}") for i in range(2)]
        gathered = [sem(f"gathered{i}") for i in range(2)]
        scattered = [sem(f"scattered{i}") for i in range(2)]
        moe_in = [sem(f"moe_in{i}") for i in range(2)]
        block = ctx.enter_context(nc.Block())

        def x_rows(i):
            return x_prompt[0, i * P:(i + 1) * P, :] if i < TT - 1 else x_sample.rearrange("b t d -> (b t) d")

        def p_rows(i):
            return p_prompt[0, 0, i * P:(i + 1) * P, :] if i < TT - 1 else p_sample[0].rearrange("b t d -> (b t) d")

        def y_rows(i):
            return y_prompt[0, i * P:(i + 1) * P, :] if i < TT - 1 else y_sample.rearrange("b t d -> (b t) d")

        def tok(i):
            return slice(i * P, i * P + rows(i))

        def w_cols(w, n):
            return w.rearrange("(p k) n -> p k n", k=KT)[:, :, n * 256:(n + 1) * 256]

        def w_cols_k(w, n):
            return w.rearrange("(k p) n -> p k n", p=P)[:, :, n * 256:(n + 1) * 256]

        def slot8(s):
            return ring[:, s, :].rearrange("p (k n) -> p k n", k=KT)

        def slots8(s):
            return ring[:, s:s + 2, :].rearrange("p a (k n) -> p k a n", k=KT)

        def slot2(s):
            return ring[:, s, :].rearrange("p (k n) -> p k n", k=2)

        def gate_rows(e):
            return w_gate[0, e, :, :].rearrange("(p k) f -> p (k f)", k=KT)

        @block.sync
        def _(sp):
            W = w_in[0]

            def load(s, view_, src):
                sp.dma_start(view_, src).then_inc(slot_in[s], 16)

            for i in range(TT):
                sp.dma_start(x_sb[0:rows(i), i, :], x_rows(i)).then_inc(x_in[i], 16)
            for s, n in enumerate((0, 2, 1, 3, 4, 5)):
                load(s, slot8(s), w_cols(W, n))
            sp.wait_ge(S["ab_done"], 2)
            load(0, slot8(0), w_cols(W, 6))
            load(1, slot8(1), w_cols(W, 7))
            sp.wait_ge(S["ab_done"], 4)
            load(2, slot8(2), w_cols(W, 8))
            load(3, slot8(3), w_cols(W, 9))
            sp.wait_ge(S["z_done"], TT)
            load(4, slot8(4), w_cols(W, 10))
            load(5, slot8(5), w_cols(W, 11))
            sp.wait_ge(S["z_done"], 2 * TT)
            load(0, slot8(0), w_cols_k(w_out[0], 0))
            load(1, slot8(1), w_cols_k(w_out[0], 1))
            sp.wait_ge(S["z_done"], 3 * TT)
            load(2, slot8(2), w_cols_k(w_out[0], 2))
            load(3, slot8(3), w_cols_k(w_out[0], 3))
            for i in range(TT):
                sp.wait_ge(S["og_done"], i + 1)
                sp.dma_start(z[0:rows(i), i, 0:2, :].rearrange("p a n -> p (a n)"), x_rows(i)).then_inc(x_back[i], 16)
            load(4, ring[:, 4, :], w_ple[0].rearrange("(p k) n -> p (k n)", k=2))
            sp.wait_ge(S["wo_done"], TT)
            load(0, ring[:, 0, :], gate_rows(0))
            load(1, ring[:, 1, :], w_up[0, 0, :, :].rearrange("(p k) f -> p (k f)", k=KT))
            load(2, ring[:, 2, :], w_down[0, 0, :, :].rearrange("(p k) n -> p (k n)", k=2))
            load(3, ring[:, 3, :], gate_rows(1))
            load(5, ring[:, 5, :], w_down[0, 1, :, :].rearrange("(p k) n -> p (k n)", k=2))
            sp.wait_ge(S["ple_done"], TT)
            load(4, ring[:, 4, :], w_up[0, 1, :, :].rearrange("(p k) f -> p (k f)", k=KT))
            wg3 = w_gate[0].rearrange("e (p k) f -> e p (k f)", k=KT)
            wu3 = w_up[0].rearrange("e (p k) f -> e p (k f)", k=KT)
            wd3 = w_down[0].rearrange("e (p k) n -> e p (k n)", k=2)
            with sp.Fori(1, NE // 2) as i:
                for par in range(2):
                    for m, w3 in ((0, wg3), (1, wu3), (2, wd3)):
                        s = 3 * par + m
                        if m != 1:
                            sp.wait_ge(S["gu_done" if m == 0 else "d_done"], 2 * i - 1 + par)
                        src = w3[bass.ds(2 * i + par, 1), :, :].rearrange("e p n -> (e p) n")
                        load(s, ring[:, s, :], src)
            sp.wait_ge(S["idx_done"], 3)
            n_ov = sp.value_load(ovinfo[0:1, NOV:NOV + 1], min_val=0, max_val=NOV)
            sp.wait_ge(S["d_done"], NE)
            with sp.If(n_ov > 0):
                with sp.Fori(0, NOV) as j:
                    e = sp.value_load(ovinfo[0:1, bass.ds(j, 1)], min_val=0, max_val=NE - 1)
                    sp.wait_ge(S["ov_end"], j + 1)
                    for s, w3 in ((0, wg3), (1, wu3), (2, wd3)):
                        src = w3[bass.ds(e, 1), :, :].rearrange("e p n -> (e p) n")
                        sp.dma_start(ring[:, s, :], src).then_inc(S["ov_load"], 16)
                sp.wait_ge(S["ov_end"], NOV + 1)
            sp.nop()
            for s in range(4):
                load(s, slot8(s), w_cols(w_ple_gate[0], s))

        @block.tensor
        def _(pe):
            def mm(out, lhsT, rhs, start, stop):
                return nc.tensor.matmul(out, lhsT, rhs, start=start, stop=stop, skip_group_check=True)

            def tr(out, in_):
                k = in_.shape[0]
                return nc.tensor.transpose(out, in_, ident[0:k, 0:k])

            def slot_ready(s, use):
                pe.wait_ge(slot_in[s], 16 * use)

            pe.wait_ge(S["const_in"], 16)
            pe.wait_ge(S["params_in"], 80)
            for c in range(CT):
                m = tr(bank[6][:, c * 34:(c + 1) * 34], cpar_rows[:, c * P:(c + 1) * P])
            m.then_inc(S["cpar_T"], 1)
            pe.wait_ge(S["hist_in"], 32)
            for a in range(2):
                for c in range(CT):
                    m = tr(bank[4 + a][:, c * 120:(c + 1) * 120], hist_rows[:, a, c * P:(c + 1) * P])
                m.then_inc(S["hist_T"], 1)

            def rows_T(src, i, banks, done):
                r = rows(i)
                for k in range(KT):
                    m = tr(banks[k // 4][:, (k % 4) * P:(k % 4) * P + r], src[0:r, k:D:KT])
                m.then_inc(done, 1)

            for i in range(TT):
                pe.wait_ge(S["xn_done"], i + 1)
                if i >= 2:
                    pe.wait_ge(S["hT_sb"], 2 * (i - 1))
                rows_T(xn[:, i % 2, :], i, pair(2 * (i % 2)), S["xT_ps"])

            for c in range(CT):
                if c == 0:
                    pe.wait_ge(S["hT_sb"], 2 * TT)
                    pe.wait_ge(S["hist_sb"], 2)
                    pe.wait_ge(S["cpar_sb"], 1)
                if c >= 2:
                    pe.wait_ge(S["u_done"], 2 * (c - 1))
                for n in range(2):
                    s = 2 * (c // 2) + n
                    slot_ready(s, 1)
                    for k in range(KT):
                        w = slot8(s)[:, k, (c % 2) * P:(c % 2 + 1) * P]
                        mm(bank[2 + 2 * (c % 2) + n][:, :], w, hT[:, k, 0:SEQ], k == 0, k == KT - 1)
                    for k in range(KT):
                        w = slot8(s)[:, k, (c % 2) * P:(c % 2 + 1) * P]
                        m = mm(bank[(6, 1)[c % 2]][:, n * NS:(n + 1) * NS], w, hT[:, k, SEQ:T], k == 0, k == KT - 1)
                m.then_inc(S["ab_done"], 1)

            def z_part(j, i, k0, k1):
                n = j * TT + i
                s = (4, 0, 2, 4)[j]
                if k0 == 0:
                    if n == 1:
                        pe.wait_ge(S["u_done"], 2 * CT)
                    if n >= 2:
                        pe.wait_ge(S["z_sb"], n - 1)
                    if i == 0:
                        for t in (s, s + 1):
                            slot_ready(t, (1, 2, 2, 2)[j])
                r = rows(i)
                for k in range(k0, k1):
                    m = mm(bank[n % 2][0:r, :], hT[:, k, tok(i)], slots8(s)[:, k, :, :], k == 0, k == KT - 1)
                if k1 == KT:
                    m.then_inc(S["z_done"], 1)

            for j in range(2):
                for i in range(TT):
                    z_part(j, i, 0, KT)
            z_part(2, 0, 0, KT)
            z_part(2, 1, 0, KT)

            def channel_sum(src, b, done):
                for c in range(CT):
                    mm(bank[b][:, :], C("ones"), src[:, c, 0:SEQ], c == 0, c == CT - 1)
                for c in range(CT):
                    m = mm(bank[b - 1][:, 0:NS], C("ones"), src[:, c, SEQ:T], c == 0, c == CT - 1)
                m.then_inc(done, 1)

            pe.wait_ge(S["convp"], CT * TAPS)
            pe.wait_ge(S["convs"], CT * TAPS)
            channel_sum(conv, 7, S["mean_done"])
            pe.wait_ge(S["tail_u"], CT)
            for c in range(CT):
                tr(bank[4][0:HIST, c * P:(c + 1) * P], uext[:, c, SEQ:SEQ + HIST])
            for c in range(CT):
                m = tr(bank[5][0:NS, c * P:(c + 1) * P], kTs[:, c, 0:NS])
            m.then_inc(S["tail_T"], 1)
            for i in range(2, TT):
                z_part(2, i, 0, KT)
            pe.wait_ge(S["csq"], 1)
            pe.wait_ge(S["tail_sb"], 2)
            channel_sum(squares, 5, S["var_done"])

            def retention_scores(i):
                r = rows(i)
                pe.wait_ge(S["qT_sb"], i + 1)
                pe.wait_ge(S["kT_sb"], i + 1)
                for h in range(NH):
                    m = mm(bank[4][0:r, h * P:h * P + r], kTs[:, h, 0:r], qTs[:, h, 0:r], True, True)
                m.then_inc(S["s_done"], 1)

            def retention_out(i):
                r = rows(i)
                pe.wait_ge(S["s_sb"], i + 1)
                pe.wait_ge(S["qTx_sb"], i + 1)
                if 0 < i < TT - 1:
                    pe.wait_ge(S["r_upd"], 1 + NH * (i - 1))
                if i == TT - 1:
                    pe.wait_ge(S["qm_done"], NH)
                    pe.wait_ge(S["states_in"], 16)
                if i >= 1:
                    pe.wait_ge(S["on_done"], NH * i)
                for h in range(NH):
                    o = bank[5][0:r, h * HD:(h + 1) * HD]
                    v = z[0:r, i, 2, h * HD:(h + 1) * HD]
                    if i == TT - 1:
                        for b in range(NB):
                            mm(o, qmask[:, h, b, :], states[:, b, h, :], b == 0, False)
                    elif i:
                        mm(o, qTx[:, h, 0:r], Rst[:, h, :], True, False)
                    m = mm(o, Sm[0:r, h, 0:r], v, i == 0, True)
                pe.wait_ge(S["kz_done"], i + 1)
                if i < TT - 1:
                    for h in range(NH):
                        m = mm(bank[6][:, h * HD:(h + 1) * HD], kz[:, h * HD:(h + 1) * HD],
                               z[:, i, 2, h * HD:(h + 1) * HD], True, True)
                m.then_inc(S["o_done"], 1)

            def gated_T(i):
                r = rows(i)
                pe.wait_ge(S["og_done"], i + 1)
                if i >= 1:
                    pe.wait_ge(S["oT_sb"], i)
                for h in range(NH):
                    m = tr(bank[7][:, h * P:h * P + r], z[0:r, i, 3, h * HD:(h + 1) * HD])
                m.then_inc(S["oT_done"], 1)

            for i in range(TT):
                r = rows(i)
                pe.wait_ge(S["rope_done"], TT + i + 1)
                if i == 0:
                    pe.wait_ge(S["cmean"], 2 * CT)
                for j, b in ((0, 2), (1, 3)):
                    for h in range(NH):
                        m = tr(bank[b][:, h * P:h * P + r], z[0:r, i, j, h * HD:(h + 1) * HD])
                m.then_inc(S["qk_T"], 1)
                z_part(3, i, 0, KT // 2)
                if i == 0:
                    pe.wait_ge(S["cstd"], 2)
                retention_scores(i)
                z_part(3, i, KT // 2, KT)
                retention_out(i)
                if i >= 1:
                    gated_T(i - 1)

            def sample_states():
                for n in range(2 * NH):
                    h, a = n // 2, n % 2
                    pe.wait_ge(S["vm_done"], h + 1)
                    if n == 0:
                        pe.wait_ge(S["r_upd"], 1 + NH * (TT - 2))
                    if n >= 2:
                        pe.wait_ge(S["rs_upd"], n - 1)
                    mm(bank[(6, 4)[n % 2]][:, :], kz[0:NS, h * HD:(h + 1) * HD], vmask[:, 4 * a:4 * a + 4, :],
                       True, True).then_inc(S["kvs_done"], 1)

            def w_out_tile(i):
                r = rows(i)
                if i == 0:
                    pe.wait_ge(S["cdone"], CT)
                    pe.wait_ge(S["z_sb"], 4 * TT)
                    for s in range(4):
                        slot_ready(s, (3, 3, 3, 3)[s])
                pe.wait_ge(S["oT_sb"], i + 1)
                if i >= 2:
                    pe.wait_ge(S["x1_sum"], 2 * (i - 1))
                for a in range(2):
                    for k in range(KT):
                        m = mm(pair(2 * (i % 2))[a][0:r, :], catT[:, k, tok(i)], slots8(2 * a)[:, k, :, :],
                               k == 0, k == KT - 1)
                m.then_inc(S["wo_done"], 1)

            sample_states()
            w_out_tile(0)
            gated_T(TT - 1)
            for i in range(1, TT):
                w_out_tile(i)
            pe.wait_ge(S["p_in"], 16 * TT)
            pe.wait_ge(S["oT_sb"], TT)
            for i in range(TT):
                r = rows(i)
                if i >= 2:
                    pe.wait_ge(S["pT_sb"], i - 1)
                if i == 1:
                    pe.wait_ge(S["rs_upd"], 2 * NH)
                for k in range(2):
                    m = tr(bank[7 - i % 2][:, P * k:P * k + r], p_sb[0:r, i, k:PLE:2])
                m.then_inc(S["pT_ps"], 1)
            slot_ready(4, 3)
            for i in range(TT):
                r = rows(i)
                pe.wait_ge(S["pT_sb"], TT if i == 1 else i + 1)
                if i >= 2:
                    pe.wait_ge(S["ple_sb"], 2 * (i - 1))
                for a in range(2):
                    for k in range(2):
                        m = mm(pair(4 + 2 * (i % 2))[a][0:r, :], pT[:, k, tok(i)],
                               slot2(4)[:, k, a * 512:(a + 1) * 512], k == 0, k == 1)
                m.then_inc(S["ple_done"], 1)
            pe.wait_ge(S["router_in"], 64)
            for i in range(TT):
                r = rows(i)
                pe.wait_ge(S["h2_done"], i + 1)
                if i == 0:
                    pe.wait_ge(S["x1_sum"], 2 * TT)
                if i >= 2:
                    pe.wait_ge(S["h2T_sb"], 2 * (i - 1))
                rows_T(xn[:, i % 2, :], i, pair(2 * (i % 2)), S["h2T_ps"])
                pe.wait_ge(S["h2T_sb"], 2 * (i + 1))
                if i == 0:
                    pe.wait_ge(S["ple_sb"], 2 * TT)
                for k in range(KT):
                    m = mm(bank[6][0:r, i * 36:(i + 1) * 36], hT[:, k, tok(i)], wr[:, k, :], k == 0, k == KT - 1)
                m.then_inc(S["logit_done"], 1)
            pe.wait_ge(S["picks_done"], 1)
            for i in range(TT):
                for j in range(i + 1):
                    r = rows(j)
                    w = C("before", r) if j == i else C("ones", r)
                    mm(bank[7][0:rows(i), i * NE:(i + 1) * NE], w[:, 0:rows(i)], both[0:r, j, :], j == 0, j == i)
            for j in range(TT):
                r = rows(j)
                m = mm(bank[7][:, TT * NE:(TT + 1) * NE], C("ones", r), both[0:r, j, :], j == 0, j == TT - 1)
            m.then_inc(S["rank_done"], 1)
            for n in range(2 * TT):
                i, r = n // 2, rows(n // 2)
                pe.wait_ge(S["laneone_done"], 2 * (n + 1))
                mm(bank[5][:, 0:NBLK], laneone[0:r, n % 2, :], blockone[0:r, n % 2, :], n == 0,
                   n == 2 * TT - 1).then_inc(S["table_done"], 1)

            def x_T(i, par):
                pe.wait_ge(gathered[par], 16 * i + 16)
                for k in range(KT):
                    m = tr(bank[2 + k // 4][:, (k % 4) * P:(k % 4 + 1) * P], X[:, par, k:D:KT])
                m.then_inc(S["xt_ps"], 1)

            def gate_up(i, par):
                pe.wait_ge(S["xt_sb"], 2 * (2 * i + par) + 2)
                for s in (3 * par, 3 * par + 1):
                    pe.wait_ge(slot_in[s], 16 * i + 64)
                for k in range(KT):
                    m = mm(bank[par][:, :], XT[:, par, k, :], slots8(3 * par)[:, k, :, :], k == 0, k == KT - 1)
                m.then_inc(S["gu_done"], 1)

            def hid_T(i, par):
                pe.wait_ge(S["hid_done"], 2 * i + par + 1)
                for k in range(2):
                    m = tr(bank[4][:, k * P:(k + 1) * P], hid[:, par, k:FF:2])
                m.then_inc(S["hT_ps"], 1)

            def down(i, par):
                pe.wait_ge(S["hT_ev"], 2 * i + par + 1)
                pe.wait_ge(slot_in[3 * par + 2], 16 * i + (64, 48)[par])
                if not (isinstance(i, int) and i == 0 and par == 0):
                    pe.wait_ge(S["y_ready"], 2 * (2 * i + par))
                for a in range(2):
                    for k in range(2):
                        m = mm(bank[5 + a][:, :], hidT[:, par, k, :],
                               slot2(3 * par + 2)[:, k, a * 512:(a + 1) * 512], k == 0, k == 1)
                m.then_inc(S["d_done"], 1)

            def before(i, par):
                return (i, 0) if par else (i - 1, 1)

            def after(i, par):
                return (i + 1, 0) if par else (i, 1)

            def step(i, par, first=False, last=False):
                gate_up(i, par)
                if not last:
                    x_T(*after(i, par))
                if not first:
                    down(*before(i, par))
                hid_T(i, par)

            pe.wait_ge(S["h2T_sb"], 2 * TT)
            pe.wait_ge(S["table_sb"], 1)
            x_T(0, 0)
            step(0, 0, first=True)
            step(0, 1)
            step(1, 0)
            step(1, 1)
            with pe.Fori(2, NE // 2 - 1) as i:
                step(i, 0)
                step(i, 1)
            step(NE // 2 - 1, 0)
            step(NE // 2 - 1, 1, last=True)
            down(NE // 2 - 1, 1)

            pe.wait_ge(S["idx_done"], 3)
            n_ov = pe.value_load(ovinfo[0:1, NOV:NOV + 1], min_val=0, max_val=NOV)
            with pe.If(n_ov > 0):
                with pe.Fori(0, NOV) as j:
                    pe.wait_ge(S["ov_gather"], 16 * j + 16)
                    for k in range(KT):
                        m = tr(bank[2 + k // 4][:, (k % 4) * P:(k % 4 + 1) * P], X[:, 0, k:D:KT])
                    m.then_inc(S["ov_xt"], 1)
                    pe.wait_ge(S["ov_xtsb"], 2 * j + 2)
                    pe.wait_ge(S["ov_load"], 48 * j + 48)
                    for k in range(KT):
                        m = mm(bank[0][:, :], XT[:, 0, k, :], slots8(0)[:, k, :, :], k == 0, k == KT - 1)
                    m.then_inc(S["ov_gu"], 1)
                    pe.wait_ge(S["ov_hid"], j + 1)
                    for k in range(2):
                        m = tr(bank[4][:, k * P:(k + 1) * P], hid[:, 0, k:FF:2])
                    m.then_inc(S["ov_hT"], 1)
                    pe.wait_ge(S["ov_hTsb"], j + 1)
                    for a in range(2):
                        for k in range(2):
                            m = mm(bank[5 + a][:, :], hidT[:, 0, k, :], slot2(2)[:, k, a * 512:(a + 1) * 512],
                                   k == 0, k == 1)
                    m.then_inc(S["ov_d"], 1)
            pe.nop()

            for i in range(TT + 1):
                if i < TT:
                    r = rows(i)
                    pe.wait_ge(S["x2_done"], i + 1)
                    if i >= 2:
                        pe.wait_ge(S["x2T_low"], i - 1)
                        pe.wait_ge(S["x2T_high"], i - 1)
                    else:
                        pe.wait_ge(S["y_ready"], 2 * NE)
                    rows_T(z[:, i, 0:2, :].rearrange("p a n -> p (a n)"), i, pair(2 * (i % 2)), S["x2T_ps"])
                if i >= 1:
                    t = i - 1
                    r = rows(t)
                    pe.wait_ge(S["x2T_low"], t + 1)
                    pe.wait_ge(S["x2T_high"], t + 1)
                    if t == 0:
                        for s in range(4):
                            slot_ready(s, 4 + NE // 2)
                    if t >= 2:
                        pe.wait_ge(S["sg_done"], 2 * (t - 1))
                    for a in range(2):
                        for k in range(KT):
                            m = mm(pair(4 + 2 * (t % 2))[a][0:r, :], hT[:, k, tok(t)], slots8(2 * a)[:, k, :, :],
                                   k == 0, k == KT - 1)
                    m.then_inc(S["pg_done"], 1)

        @block.vector
        def _(dve):
            V = nc.vector
            order = [0]

            def then(ins):
                order[0] += 1
                ins.then_inc(S["dve_order"], 1)
                dve.wait_ge(S["dve_order"], order[0])

            for t in (ssq, ssq2, ssq4):
                V.memset(t[:, :], 1.0).then_inc(S["zeroed"], 1)
            V.memset(ssq3[:, :, :], 1.0).then_inc(S["zeroed"], 1)
            V.memset(epsb[:, :], EPS).then_inc(S["zeroed"], 1)
            V.memset(half[:, :], -0.5).then_inc(S["zeroed"], 1)
            V.memset(mv[:, :, :], 1.0).then_inc(S["zeroed"], 1)
            dve.wait_ge(S["cpar_T"], 1)
            V.tensor_copy(cpar[:, :, :], bank[6][:, 0:CT * 34].rearrange("p (c n) -> p c n", c=CT)).then_inc(S["cpar_sb"], 1)
            dve.wait_ge(S["xstd"], 1)
            V.reciprocal(rst[:, :], rst[:, :]).then_inc(S["xrstd"], 1)

            def quads(i, a):
                return bank[2 * (i % 2) + a][:, :].rearrange("p (k t) -> p k t", k=4)[:, :, 0:rows(i)]

            for i in range(TT):
                dve.wait_ge(S["xT_ps"], i + 1)
                for a in range(2):
                    g = bc(g1c[:, 4 * a:4 * a + 4], 2, rows(i))
                    V.tensor_tensor(hT[:, 4 * a:4 * a + 4, tok(i)], quads(i, a), g, ALU.mult).then_inc(S["hT_sb"], 1)

            dve.wait_ge(S["cpar_sb"], 1)
            dve.wait_ge(S["zero_x"], 1)
            dve.wait_ge(S["hist_sb"], 2)
            def glu(c):
                dve.wait_ge(S["sig_done"], 2 * (c + 1))
                V.tensor_tensor(uext[:, c, HIST:HIST + SEQ], bank[2 + 2 * (c % 2)][:, :], sig[:, c % 2, 0:SEQ],
                                ALU.mult).then_inc(S["u_done"], 1)
                V.tensor_tensor(sext[:, c, :, HIST:HIST + NL],
                                bank[(6, 1)[c % 2]][:, 0:NS].rearrange("p (b t) -> p b t", b=NB),
                                sig[:, c % 2, SEQ:T].rearrange("p (b t) -> p b t", b=NB),
                                ALU.mult).then_inc(S["u_done"], 1)

            ahead = (15, 6, 2)
            glu(0)
            for c in range(CT):
                dve.wait_ge(S["u_done"], 2 * (c + 1))
                cs = conv[:, c, SEQ:T].rearrange("p (b t) -> p b t", b=NB)
                for t in range(TAPS):
                    tap = cpar[:, c, t:t + 1]
                    out = bank[7][:, :] if t < TAPS - 1 else conv[:, c, 0:SEQ]
                    if t == 0:
                        if c:
                            dve.wait_ge(S["convp"], c * TAPS)
                        bias = cpar[:, c, TAPS:TAPS + 1]
                        V.tensor_scalar(out, uext[:, c, 0:SEQ], tap, bias, ALU.mult, ALU.add).then_inc(S["convp"], 1)
                        V.tensor_scalar(cs, sext[:, c, :, 0:NL], tap, bias, ALU.mult, ALU.add).then_inc(S["convs"], 1)
                    else:
                        dve.wait_ge(S["convp"], c * TAPS + t)
                        V.scalar_tensor_tensor(out, uext[:, c, t:t + SEQ], tap, bank[7][:, :], ALU.mult,
                                               ALU.add).then_inc(S["convp"], 1)
                        dve.wait_ge(S["convs"], c * TAPS + t)
                        V.scalar_tensor_tensor(cs, sext[:, c, :, t:t + NL], tap, cs, ALU.mult,
                                               ALU.add).then_inc(S["convs"], 1)
                    if c < CT - 1 and t == ahead[c]:
                        glu(c + 1)
            dve.wait_ge(S["convp"], CT * TAPS)
            dve.wait_ge(S["convs"], CT * TAPS)
            dve.wait_ge(S["mean_done"], 1)
            for c in range(CT):
                for b, cols in ((7, slice(0, SEQ)), (6, slice(SEQ, T))):
                    v = conv[:, c, cols]
                    V.scalar_tensor_tensor(v, bank[b][:, 0:v.shape[1]], -1.0 / CH, v, ALU.mult,
                                           ALU.add).then_inc(S["cmean"], 1)
            dve.wait_ge(S["cstd"], 2)
            cst = squares[:, 0, :]
            then(V.reciprocal(cst, cst))
            V.tensor_tensor(conv, conv, bc(cst, 1, CT), ALU.mult).then_inc(S["crstd"], 1)

            for i in range(TT):
                r = rows(i)
                dve.wait_ge(S["qT_sb"], i + 1)
                if i == 0:
                    dve.wait_ge(S["rope_done"], 2 * TT)
                if i < TT - 1:
                    V.tensor_tensor(qTx[:, :, :], qTs[:, :, :],
                                    C("xi").rearrange("p (h t) -> p h t", h=NH), ALU.mult).then_inc(S["qTx_sb"], 1)
                    decay = C("decay").rearrange("p (h t) -> p h t", h=NH)
                else:
                    for h in range(NH):
                        m = V.tensor_tensor(qTx[:, h, 0:NS].rearrange("p (b t) -> p b t", b=NB),
                                            qTs[:, h, 0:NS].rearrange("p (b t) -> p b t", b=NB),
                                            bc(C("xi")[:, h * P:h * P + NL], 1, NB), ALU.mult)
                        if h == NH - 1:
                            m.then_inc(S["qTx_sb"], 1)
                    decay = C("decay_s", NS).rearrange("p (h t) -> p h t", h=NH)
                dve.wait_ge(S["s_done"], i + 1)
                V.tensor_tensor(Sm[0:r, :, 0:r], bank[4][0:r, :].rearrange("p (h t) -> p h t", h=NH)[:, :, 0:r],
                                decay, ALU.mult).then_inc(S["s_sb"], 1)
                dve.wait_ge(S["o_done"], i + 1)
                if i == 0:
                    V.tensor_copy(Rst[:, :, :], bank[6][:, :].rearrange("p (h e) -> p h e", h=NH)).then_inc(S["r_upd"], 1)
                elif i < TT - 1:
                    for h in range(NH):
                        V.scalar_tensor_tensor(Rst[:, h, :], Rst[:, h, :], float(np.exp(P * np.log(GAMMA[h]))),
                                               bank[6][:, h * HD:(h + 1) * HD], ALU.mult, ALU.add).then_inc(S["r_upd"], 1)
                for h in range(NH):
                    m = V.bn_stats(bns[0:r, h, :], bank[5][0:r, h * HD:(h + 1) * HD])
                then(m)
                for h in range(NH):
                    m = V.bn_aggr(mv[0:r, h, :], bns[0:r, h, :])
                then(m)
                V.tensor_scalar(mv[0:r, :, 1], mv[0:r, :, 1], EPS, None, ALU.add).then_inc(S["gn_var"], 1)
                dve.wait_ge(S["gn_rstd"], i + 1)
                for h in range(NH):
                    V.tensor_scalar(z[0:r, i, 0, h * HD:(h + 1) * HD], bank[5][0:r, h * HD:(h + 1) * HD],
                                    mv[0:r, h, 0:1], grs[0:r, h:h + 1], ALU.subtract, ALU.mult).then_inc(S["on_done"], 1)

            for n in range(2 * NH):
                h, a = n // 2, n % 2
                dve.wait_ge(S["kvs_done"], n + 1)
                st = states[:, 4 * a:4 * a + 4, h, :]
                V.scalar_tensor_tensor(st, st, float(np.exp(NL * np.log(GAMMA[h]))),
                                       bank[(6, 4)[n % 2]][:, :].rearrange("p (b e) -> p b e", b=4), ALU.mult,
                                       ALU.add).then_inc(S["rs_upd"], 1)

            def x1(i, a=None):
                v = z[0:rows(i), i, 0:2, :]
                return v.rearrange("p a n -> p (a n)") if a is None else v[:, a, :]

            def ple(i, a=None):
                v = z[0:rows(i), i, 2:4, :]
                return v.rearrange("p a n -> p (a n)") if a is None else v[:, a, :]

            def norm2(i):
                r = rows(i)
                dve.wait_ge(S["x1_std"], i + 1)
                V.reciprocal(rst2[0:r, i:i + 1], rst2[0:r, i:i + 1]).then_inc(S["x1_rstd"], 1)
                dve.wait_ge(S["x1_rstd"], i + 1)
                if i == 0:
                    dve.wait_ge(S["gbc_in"], 16)
                if i >= 2:
                    dve.wait_ge(S["h2T_ps"], i - 1)
                    dve.wait_ge(h2_out[i % 2], 16 * (i // 2))
                V.scalar_tensor_tensor(xn[0:r, i % 2, :], x1(i), rst2[0:r, i:i + 1], gbc[0:r, :], ALU.mult,
                                       ALU.mult).then_inc(S["h2_done"], 1)

            for i in range(TT):
                dve.wait_ge(x_back[i], 16)
                dve.wait_ge(S["wo_done"], i + 1)
                for a in range(2):
                    V.tensor_tensor(x1(i, a), pair(2 * (i % 2))[a][0:rows(i), :], x1(i, a), ALU.add).then_inc(S["x1_sum"], 1)
                if i in (1, 2):
                    norm2(i - 1)

            def ple_norm(i):
                r = rows(i)
                dve.wait_ge(S["ple_sq"], 2 * (i + 1))
                V.tensor_tensor(rst3[0:r, i:i + 1], ssq3[0:r, i, 0:1], ssq3[0:r, i, 1:2], ALU.add).then_inc(S["ple_var"], 1)
                dve.wait_ge(S["ple_std"], i + 1)
                V.reciprocal(rst3[0:r, i:i + 1], rst3[0:r, i:i + 1]).then_inc(S["ple_rstd"], 1)
                dve.wait_ge(S["ple_rstd"], i + 1)
                if i == 0:
                    dve.wait_ge(S["pbc_in"], 16)
                for a in range(2):
                    V.scalar_tensor_tensor(ple(i, a), pair(4 + 2 * (i % 2))[a][0:r, :], rst3[0:r, i:i + 1],
                                           pbc[0:r, a * 512:(a + 1) * 512], ALU.mult, ALU.mult).then_inc(S["ple_sb"], 1)

            for i in range(TT):
                ple_norm(i)
            for i in range(TT):
                if i >= 2:
                    norm2(i)
                dve.wait_ge(S["h2T_ps"], i + 1)
                V.tensor_copy(hT[:, 4:8, tok(i)], quads(i, 1)).then_inc(S["h2T_sb"], 1)

            dve.wait_ge(S["wo_done"], TT)
            then(V.memset(logit, 0.0))
            V.memset(tabz, 0.0).then_inc(S["zeroed"], 1)
            V.memset(zero32, 0.0).then_inc(S["zeroed"], 1)
            dve.wait_ge(S["logit_done"], TT)
            dve.wait_ge(S["router_in"], 64)
            ps = bank[6][:, 0:TT * 36].rearrange("p (i n) -> p i n", i=TT)
            V.tensor_tensor(logit[:, 0:TT - 1, :], ps[:, 0:TT - 1, :], bc(rbias[:, :], 1, TT - 1), ALU.add).then_inc(S["logit_sb"], 1)
            V.tensor_tensor(logit[0:NS, TT - 1, :], ps[0:NS, TT - 1, :], rbias[0:NS, :], ALU.add).then_inc(S["logit_sb"], 1)
            dve.wait_ge(S["logit_sb"], 2)
            lg = logit[:, :, 0:NG]
            then(V.tensor_reduce(gmx, lg, AX.X, ALU.max))
            V.tensor_tensor(gexp, lg, bc(gmx, 2, NG), ALU.subtract).then_inc(S["logit_sb"], 1)

            def first_of(one, values, mx, tmp, n):
                then(V.tensor_tensor(one, values, bc(mx, 2, n), ALU.is_equal))
                then(V.tensor_tensor(tmp, one, bc(C("rev")[:, 0:n], 1, TT), ALU.mult))
                then(V.tensor_reduce(t1, tmp, AX.X, ALU.max))
                then(V.tensor_tensor(one, tmp, bc(t1, 2, n), ALU.is_equal))

            first_of(gone, lg, gmx, gval, NG)
            then(V.tensor_tensor(sel, logit[:, :, NG:].rearrange("p i (g e) -> p i g e", g=NG),
                                 bc(gone, 3, NEG), ALU.mult))
            then(V.tensor_reduce(el, sel.rearrange("p i g e -> p i e g"), AX.X, ALU.add))
            then(V.tensor_reduce(m1, el, AX.X, ALU.max))
            first_of(one1, el, m1, eval_, NEG)
            then(V.tensor_scalar(eval_, one1, -3.0e38, None, ALU.mult))
            then(V.tensor_tensor(el, el, eval_, ALU.add))
            then(V.tensor_reduce(m2, el, AX.X, ALU.max))
            V.tensor_tensor(e2, m2, m1, ALU.subtract).then_inc(S["logit_sb"], 1)
            first_of(one2, el, m2, eval_, NEG)
            for k, one in ((0, one1), (1, one2)):
                for i in range(TT):
                    m = V.tensor_tensor(M[k][:, i, :].rearrange("p (g e) -> p g e", g=NG), bc(gone[:, i, :], 2, NEG),
                                        bc(one[:, i, :], 1, NG), ALU.mult)
                then(m)
            V.tensor_tensor(both, M[0], M[1], ALU.add).then_inc(S["picks_done"], 1)
            dve.wait_ge(S["gexp_done"], 2)
            then(V.tensor_reduce(gsum, gexp, AX.X, ALU.add))
            then(V.tensor_scalar(t1, e2, 1.0, None, ALU.add))
            then(V.tensor_tensor(t1, t1, gsum, ALU.mult))
            then(V.reciprocal(gates[:, :, 0], t1))
            then(V.tensor_tensor(gates[:, :, 1], gates[:, :, 0], e2, ALU.mult))
            dve.wait_ge(S["rank_done"], 1)
            then(V.memset(rank, 0.0))
            rp = bank[7][:, 0:(TT + 1) * NE].rearrange("p (i n) -> p i n", i=TT + 1)
            V.tensor_copy(rank[:, 0:TT - 1, :], rp[:, 0:TT - 1, :])
            V.tensor_copy(rank[0:NS, TT - 1, :], rp[0:NS, TT - 1, :])
            then(V.tensor_copy(rank[:, TT, :], rp[:, TT, :]))
            total = rank[:, TT, :]
            then(V.tensor_scalar(ov, total, float(SLOTS), None, ALU.is_gt))
            for n in range(2, DEEP):
                then(V.scalar_tensor_tensor(ov, total, float(SLOTS * n), ov, ALU.is_gt, ALU.add))
            then(V.tensor_tensor_scan(ovi, zero32, ov, 0.0, ALU.add, ALU.add))
            then(V.tensor_tensor(ovb, ovi, ov, ALU.subtract))
            then(V.tensor_tensor(ovw, ovb, C("expert"), ALU.subtract))
            then(V.tensor_scalar(ovw, ovw, float(NE - 1), None, ALU.add))
            rk = rank[:, 0:TT, :]
            then(V.tensor_scalar(flag, rk, float(SLOTS), None, ALU.is_ge))
            then(V.tensor_copy(deep, flag))
            for n in range(2, DEEP):
                then(V.scalar_tensor_tensor(deep, rk, float(SLOTS * n), deep, ALU.is_ge, ALU.add))
            then(V.tensor_tensor(blk, deep, bc(ovw, 1, TT), ALU.add))
            then(V.tensor_tensor(blk, blk, flag, ALU.mult))
            then(V.tensor_tensor(blk, blk, bc(C("expert"), 1, TT), ALU.add))
            then(V.scalar_tensor_tensor(lane, deep, -float(SLOTS), rk, ALU.mult, ALU.add))
            for k in range(2):
                for pos, what in ((posb, blk), (posl, lane)):
                    then(V.tensor_tensor(prod, what, M[k], ALU.mult))
                    then(V.tensor_reduce(pos[:, k, :], prod, AX.X, ALU.add))
            code = C("code").rearrange("p (i k) -> p i k", i=TT)
            for n in range(2 * TT):
                i, k = n // 2, n % 2
                if n >= 2:
                    dve.wait_ge(S["table_done"], n - 1)
                V.tensor_scalar(laneone[:, n % 2, :], C("lane"), posl[:, k, i:i + 1], None,
                                ALU.is_equal).then_inc(S["laneone_done"], 1)
                V.tensor_scalar(blockone[:, n % 2, :], C("block"), posb[:, k, i:i + 1], code[:, i, k:k + 1],
                                ALU.is_equal, ALU.mult).then_inc(S["laneone_done"], 1)
            dve.wait_ge(S["table_done"], 2 * TT)
            V.tensor_copy(tabf, bank[5][:, 0:NBLK]).then_inc(S["table_sb"], 1)
            dve.wait_ge(S["table_sb"], 1)
            then(V.tensor_scalar(tabz, tabf, 0.0, float(1 << 20), ALU.is_equal, ALU.mult))
            then(V.scalar_tensor_tensor(tabf, tabf, -1.0, tabz, ALU.add, ALU.add))
            V.tensor_copy(codes[:, :], tabf).then_inc(S["idx_done"], 1)
            dve.wait_ge(S["idx_done"], 1)
            V.tensor_scalar(tokidx[:, :], codes[:, :], 1, None, ALU.arith_shift_right).then_inc(S["idx_done"], 1)
            jj = bc(C("ovj", 1), 2, NE)
            then(V.tensor_tensor(ovt[0:1, 0, :, :], bc(ovb[0:1, :], 1, NOV), jj, ALU.is_le))
            then(V.tensor_tensor(ovt[0:1, 1, :, :], bc(ovi[0:1, :], 1, NOV), jj, ALU.is_le))
            then(V.tensor_tensor(ovt[0:1, 0, :, :], ovt[0:1, 0, :, :], ovt[0:1, 1, :, :], ALU.subtract))
            then(V.tensor_tensor(ovt[0:1, 0, :, :], ovt[0:1, 0, :, :], bc(C("expert", 1), 1, NOV), ALU.mult))
            then(V.tensor_reduce(ovf[0:1, 0:NOV], ovt[0:1, 0, :, :], AX.X, ALU.add))
            then(V.tensor_copy(ovf[0:1, NOV:NOV + 1], ovi[0:1, NE - 1:NE]))
            V.tensor_copy(ovinfo[:, :], ovf[0:1, :]).then_inc(S["idx_done"], 1)

            def xt_half(par):
                return XT[:, par, 4:8, :], bank[3][:, :].rearrange("p (k s) -> p k s", k=4)

            def x_out(i, par):
                dve.wait_ge(S["xt_ps"], 2 * i + par + 1)
                V.tensor_copy(*xt_half(par)).then_inc(S["xt_sb"], 1)

            def hidden(i, par):
                dve.wait_ge(S["sil_done"], 2 * i + par + 1)
                V.tensor_tensor(hid[:, par, :], bank[par][:, FF:2 * FF], gat[:, par, :], ALU.mult).then_inc(S["hid_done"], 1)

            def hid_out(i, par):
                dve.wait_ge(S["hT_ps"], 2 * i + par + 1)
                V.tensor_copy(hidT[:, par, :, :], bank[4][:, 0:2 * P].rearrange("p (k s) -> p k s", k=2)).then_inc(S["hT_ev"], 1)

            def y_out(i, par):
                dve.wait_ge(S["d_done"], 2 * i + par + 1)
                if isinstance(i, int):
                    if i == 0 and par == 0:
                        dve.wait_ge(S["rs_out"], 16)
                    if i:
                        dve.wait_ge(scattered[par], 16 * i)
                else:
                    dve.wait_ge(scattered[par], 16 * i)
                V.tensor_copy(yout[:, par, 512:1024], bank[6][:, :]).then_inc(S["y_ready"], 1)

            def step(i, par, first=False, last=False):
                hidden(i, par)
                if not last:
                    x_out(*((i + 1, 0) if par else (i, 1)))
                if not first:
                    y_out(*((i, 0) if par else (i - 1, 1)))
                hid_out(i, par)

            x_out(0, 0)
            step(0, 0, first=True)
            step(0, 1)
            step(1, 0)
            step(1, 1)
            with dve.Fori(2, NE // 2 - 1) as i:
                step(i, 0)
                step(i, 1)
            step(NE // 2 - 1, 0)
            step(NE // 2 - 1, 1, last=True)
            y_out(NE // 2 - 1, 1)

            dve.wait_ge(S["idx_done"], 3)
            n_ov = dve.value_load(ovinfo[0:1, NOV:NOV + 1], min_val=0, max_val=NOV)
            with dve.If(n_ov > 0):
                with dve.Fori(0, NOV) as j:
                    dve.wait_ge(S["ov_xt"], j + 1)
                    V.tensor_copy(*xt_half(0)).then_inc(S["ov_xtsb"], 1)
                    dve.wait_ge(S["ov_sil"], j + 1)
                    V.tensor_tensor(hid[:, 0, :], bank[0][:, FF:2 * FF], gat[:, 0, :], ALU.mult).then_inc(S["ov_hid"], 1)
                    dve.wait_ge(S["ov_hT"], j + 1)
                    V.tensor_copy(hidT[:, 0, :, :], bank[4][:, 0:2 * P].rearrange("p (k s) -> p k s", k=2)).then_inc(S["ov_hTsb"], 1)
                    dve.wait_ge(S["ov_d"], j + 1)
                    V.tensor_copy(yout[:, 0, 512:1024], bank[6][:, :]).then_inc(S["ov_y"], 1)
            dve.nop()

            def x2(i):
                r = rows(i)
                dve.wait_ge(moe_in[i % 2], 16 * (i // 2 + 1))
                y = yins[i % 2]
                V.scalar_tensor_tensor(x1(i), y[0:r, 0, :], gates[0:r, i, 0:1], x1(i), ALU.mult,
                                       ALU.add).then_inc(S["x2_order"], 1)
                dve.wait_ge(S["x2_order"], i + 1)
                V.scalar_tensor_tensor(x1(i), y[0:r, 1, :], gates[0:r, i, 1:2], x1(i), ALU.mult,
                                       ALU.add).then_inc(S["x2_done"], 1)
                dve.wait_ge(S["x2T_ps"], i + 1)
                V.tensor_copy(hT[:, 4:8, tok(i)], quads(i, 1)).then_inc(S["x2T_high"], 1)

            def x3(i):
                r = rows(i)
                dve.wait_ge(S["sg_done"], 2 * (i + 1))
                if i >= 2:
                    dve.wait_ge(S["x3_sq"], i - 1)
                t = xt[0:r, i % 2, :]
                then(V.tensor_tensor(t, sg[0:r, i % 2, :], ple(i), ALU.mult))
                V.tensor_tensor(t, t, x1(i), ALU.add).then_inc(S["x3_done"], 1)

            def final(i):
                r = rows(i)
                dve.wait_ge(S["x3_std"], i + 1)
                V.reciprocal(rst4[0:r, i:i + 1], rst4[0:r, i:i + 1]).then_inc(S["x3_rstd"], 1)
                dve.wait_ge(S["x3_rstd"], i + 1)
                if i == 0:
                    dve.wait_ge(S["final_in"], 16)
                if i >= 2:
                    dve.wait_ge(y_stored[i % 2], 16 * (i // 2))
                V.scalar_tensor_tensor(yo[0:r, i % 2, :], xt[0:r, i % 2, :], rst4[0:r, i:i + 1], gbc[0:r, :],
                                       ALU.mult, ALU.mult).then_inc(S["out_done"], 1)

            for i in range(TT + 2):
                if i < TT:
                    x2(i)
                if 1 <= i <= TT:
                    x3(i - 1)
                if i >= 2:
                    final(i - 2)

        @block.scalar
        def _(act):
            A = nc.scalar
            act.dma_start(const[:, :], consts_d).then_inc(S["const_in"], 16)
            act.dma_start(cpar_rows[0:TAPS, :], conv_w[0]).then_inc(S["params_in"], 16)
            for n, v in enumerate((conv_b, conv_ln_g, conv_ln_b)):
                act.dma_start(cpar_rows[TAPS + n:TAPS + n + 1, :], v).then_inc(S["params_in"], 16)
            act.dma_start(g1c[:, :], norm1_g[0].rearrange("(p k) -> p k", k=KT)).then_inc(S["params_in"], 16)
            for a in range(2):
                act.dma_start(hist_rows[:, a, :], state_conv[0, 4 * a:4 * a + 4, :, :].rearrange("b t c -> (b t) c")
                              ).then_inc(S["hist_in"], 16)

            for i in range(TT):
                r = rows(i)
                act.wait_ge(x_in[i], 16)
                if i == 0:
                    act.wait_ge(S["zeroed"], 7)
                else:
                    act.wait_ge(S["xsq"], i)
                A.activation(xn[0:r, 0, :], x_sb[0:r, i, :], ACT.Square, accum_out=ssq[0:r, i:i + 1]).then_inc(S["xsq"], 1)
            act.wait_ge(S["xsq"], TT)
            A.activation(rst[:, :], ssq[:, :], ACT.Sqrt, bias=epsb[:, :], scale=1.0 / D).then_inc(S["xstd"], 1)
            act.wait_ge(S["xrstd"], 1)
            for i in range(TT):
                r = rows(i)
                if i >= 2:
                    act.wait_ge(S["xT_ps"], i - 1)
                A.activation(xn[0:r, i % 2, :], x_sb[0:r, i, :], ACT.Copy, scale=rst[0:r, i:i + 1]).then_inc(S["xn_done"], 1)
                if i < 2:
                    act.wait_ge(S["hist_T"], i + 1)
                    A.activation(sext[:, :, 4 * i:4 * i + 4, 0:HIST],
                                 bank[4 + i][:, 0:CT * 120].rearrange("p (c b t) -> p c b t", c=CT, b=4),
                                 ACT.Copy).then_inc(S["hist_sb"], 1)
            act.wait_ge(S["xn_done"], TT)
            act.dma_start(states, state_ret[0].rearrange("b h d e -> d b h e")).then_inc(S["states_in"], 16)
            act.dma_start(conv_s[0, :, 0:HIST - NL, :], state_conv[0, :, NL:HIST, :]).then_inc(S["cs_copy"], 16)
            act.dma_start(wr[:, :, 0:NG], rg_w[0].rearrange("(p k) n -> p k n", k=KT)).then_inc(S["router_in"], 16)
            act.dma_start(wr[:, :, NG:], re_w[0].rearrange("(p k) n -> p k n", k=KT)).then_inc(S["router_in"], 16)
            act.dma_start(rbias[:, 0:NG], rg_b[0].partition_broadcast(P)).then_inc(S["router_in"], 16)
            act.dma_start(rbias[:, NG:], re_b[0].partition_broadcast(P)).then_inc(S["router_in"], 16)
            act.dma_start(gbc[:, :], norm2_g[0].partition_broadcast(P)).then_inc(S["gbc_in"], 16)

            for c in range(CT):
                act.wait_ge(S["ab_done"], c + 1)
                if c >= 2:
                    act.wait_ge(S["u_done"], 2 * (c - 1))
                A.activation(sig[:, c % 2, 0:SEQ], bank[3 + 2 * (c % 2)][:, :], ACT.Sigmoid).then_inc(S["sig_done"], 1)
                A.activation(sig[:, c % 2, SEQ:T], bank[(6, 1)[c % 2]][:, NS:2 * NS], ACT.Sigmoid).then_inc(S["sig_done"], 1)

            def z_out(n):
                j, i = n // TT, n % TT
                act.wait_ge(S["z_done"], n + 1)
                A.activation(z[0:rows(i), i, j, :], bank[n % 2][0:rows(i), :],
                             ACT.Silu if j == 3 else ACT.Copy).then_inc(S["z_sb"], 1)

            for n in range(12):
                z_out(n)
            act.wait_ge(S["tail_T"], 1)
            A.activation(tails[0:HIST, 0, :], bank[4][0:HIST, :], ACT.Copy).then_inc(S["tail_sb"], 1)
            A.activation(tails[0:NS, 1, :], bank[5][0:NS, :], ACT.Copy).then_inc(S["tail_sb"], 1)
            act.wait_ge(S["cmean"], 2 * CT)
            A.activation(squares, conv, ACT.Square).then_inc(S["csq"], 1)
            act.wait_ge(S["tail_sb"], 2)
            act.dma_start(conv_p[0, 0], tails[0:HIST, 0, :]).then_inc(S["tail_out"], 16)
            for b in range(NB):
                act.dma_start(conv_s[0, b, HIST - NL:HIST, :], tails[b * NL:(b + 1) * NL, 1, :]).then_inc(S["tail_out"], 16)
            for n in range(12, 15):
                z_out(n)
            act.wait_ge(S["var_done"], 1)
            A.activation(squares[:, 0, 0:SEQ], bank[5][:, :], ACT.Sqrt, bias=epsb[:, :], scale=1.0 / CH).then_inc(S["cstd"], 1)
            A.activation(squares[:, 0, SEQ:T], bank[4][:, 0:NS], ACT.Sqrt, bias=epsb[:, :], scale=1.0 / CH).then_inc(S["cstd"], 1)

            def gated_out(i):
                r = rows(i)
                act.wait_ge(S["oT_done"], i + 1)
                if i == 0:
                    act.wait_ge(S["tail_out"], 16 * (1 + NB))
                A.activation(catT[:, 4:8, tok(i)], bank[7][:, :].rearrange("p (h t) -> p h t", h=NH)[:, :, 0:r],
                             ACT.Copy).then_inc(S["oT_sb"], 1)

            for i in range(TT):
                r = rows(i)
                act.wait_ge(S["qk_T"], i + 1)
                for t, b, done in ((kTs, 3, "kT_sb"), (qTs, 2, "qT_sb")):
                    A.activation(t[:, :, 0:r], bank[b][:, :].rearrange("p (h t) -> p h t", h=NH)[:, :, 0:r],
                                 ACT.Copy).then_inc(S[done], 1)
                z_out(15 + i)
                if i == 0:
                    act.wait_ge(S["crstd"], 1)
                    for c in range(CT):
                        A.activation(catT[:, c, :], conv[:, c, :], ACT.Silu, bias=cpar[:, c, TAPS + 2:TAPS + 3],
                                     scale=cpar[:, c, TAPS + 1:TAPS + 2]).then_inc(S["cdone"], 1)
                    act.wait_ge(S["cdone"], CT)
                    for n in range(TT):
                        act.dma_start(p_sb[0:rows(n), n, :], p_rows(n)).then_inc(S["p_in"], 16)
                if i >= 1:
                    gated_out(i - 1)
            act.wait_ge(S["r_upd"], 1 + NH * (TT - 2))
            act.dma_start(ret_p[0, 0].rearrange("h d e -> d h e"), Rst[:, :, :]).then_inc(S["rp_out"], 16)
            act.wait_ge(S["rs_upd"], 2 * NH)
            act.dma_start(pbc, ple_norm_g[0].partition_broadcast(P)).then_inc(S["pbc_in"], 16)
            act.dma_start(ret_s[0].rearrange("b h d e -> d b h e"), states).then_inc(S["rs_out"], 16)
            gated_out(TT - 1)

            def x1_sq(i):
                r = rows(i)
                act.wait_ge(S["x1_sum"], 2 * (i + 1))
                if i >= 1:
                    act.wait_ge(S["x1_sq"], i)
                A.activation(junk[0:r, :], z[0:r, i, 0:2, :].rearrange("p a n -> p (a n)"), ACT.Square,
                             accum_out=ssq2[0:r, i:i + 1]).then_inc(S["x1_sq"], 1)
                act.wait_ge(S["x1_sq"], i + 1)
                A.activation(rst2[0:r, i:i + 1], ssq2[0:r, i:i + 1], ACT.Sqrt, bias=epsb[0:r, :],
                             scale=1.0 / D).then_inc(S["x1_std"], 1)

            def h2_store(i):
                r = rows(i)
                act.wait_ge(S["h2_done"], i + 1)
                act.dma_start(h2_d[i * P:i * P + r, :], xn[0:r, i % 2, :]).then_inc(h2_out[i % 2], 16)

            for i in range(TT):
                x1_sq(i)
                if i in (1, 2):
                    h2_store(i - 1)
            for i in range(TT):
                r = rows(i)
                act.wait_ge(S["pT_ps"], i + 1)
                A.activation(pT[:, :, tok(i)],
                             bank[7 - i % 2][:, 0:256].rearrange("p (k t) -> p k t", k=2)[:, :, 0:r],
                             ACT.Copy).then_inc(S["pT_sb"], 1)
            for i in range(TT):
                r = rows(i)
                act.wait_ge(S["ple_done"], i + 1)
                for a in range(2):
                    act.wait_ge(S["x1_sq"], TT)
                    if 2 * i + a:
                        act.wait_ge(S["ple_sq"], 2 * i + a)
                    A.activation(junk[0:r, 0:512], pair(4 + 2 * (i % 2))[a][0:r, :], ACT.Square,
                                 accum_out=ssq3[0:r, i, a:a + 1]).then_inc(S["ple_sq"], 1)
                act.wait_ge(S["ple_var"], i + 1)
                A.activation(rst3[0:r, i:i + 1], rst3[0:r, i:i + 1], ACT.Sqrt, bias=epsb[0:r, :],
                             scale=1.0 / D).then_inc(S["ple_std"], 1)
            for i in range(TT):
                if i >= 2:
                    h2_store(i)
                act.wait_ge(S["h2T_ps"], i + 1)
                A.activation(hT[:, 0:4, tok(i)], bank[2 * (i % 2)][:, :].rearrange("p (k t) -> p k t", k=4)[:, :, 0:rows(i)],
                             ACT.Copy).then_inc(S["h2T_sb"], 1)
            act.dma_start(gbc[:, :], final_norm_g.partition_broadcast(P)).then_inc(S["final_in"], 16)
            act.wait_ge(S["logit_sb"], 3)
            A.activation(gexp, gexp, ACT.Exp).then_inc(S["gexp_done"], 1)
            act.wait_ge(S["logit_sb"], 4)
            A.activation(e2, e2, ACT.Exp).then_inc(S["gexp_done"], 1)

            def xt_half(par):
                return XT[:, par, 0:4, :], bank[2][:, :].rearrange("p (k s) -> p k s", k=4)

            def x_out(i, par):
                act.wait_ge(S["xt_ps"], 2 * i + par + 1)
                A.activation(*xt_half(par), ACT.Copy).then_inc(S["xt_sb"], 1)

            def silu(i, par):
                act.wait_ge(S["gu_done"], 2 * i + par + 1)
                A.activation(gat[:, par, :], bank[par][:, 0:FF], ACT.Silu).then_inc(S["sil_done"], 1)

            def y_copy(i, par):
                act.wait_ge(S["d_done"], 2 * i + par + 1)
                if isinstance(i, int):
                    if i == 0 and par == 0:
                        act.wait_ge(S["rs_out"], 16)
                    if i:
                        act.wait_ge(scattered[par], 16 * i)
                else:
                    act.wait_ge(scattered[par], 16 * i)
                A.activation(yout[:, par, 0:512], bank[5][:, :], ACT.Copy).then_inc(S["y_ready"], 1)

            def step(i, par, first=False, last=False):
                silu(i, par)
                if not last:
                    x_out(*((i + 1, 0) if par else (i, 1)))
                if not first:
                    y_copy(*((i, 0) if par else (i - 1, 1)))

            x_out(0, 0)
            step(0, 0, first=True)
            step(0, 1)
            step(1, 0)
            step(1, 1)
            with act.Fori(2, NE // 2 - 1) as i:
                step(i, 0)
                step(i, 1)
            step(NE // 2 - 1, 0)
            step(NE // 2 - 1, 1, last=True)
            y_copy(NE // 2 - 1, 1)

            act.wait_ge(S["idx_done"], 3)
            n_ov = act.value_load(ovinfo[0:1, NOV:NOV + 1], min_val=0, max_val=NOV)
            with act.If(n_ov > 0):
                with act.Fori(0, NOV) as j:
                    act.wait_ge(S["ov_xt"], j + 1)
                    A.activation(*xt_half(0), ACT.Copy).then_inc(S["ov_xtsb"], 1)
                    act.wait_ge(S["ov_gu"], j + 1)
                    A.activation(gat[:, 0, :], bank[0][:, 0:FF], ACT.Silu).then_inc(S["ov_sil"], 1)
                    act.wait_ge(S["ov_d"], j + 1)
                    A.activation(yout[:, 0, 0:512], bank[5][:, :], ACT.Copy).then_inc(S["ov_y"], 1)
            act.nop()

            act.wait_ge(S["moe_out"], 1)
            moe2 = moe_d.rearrange("(t k) d -> t k d", k=2)
            for i in range(2):
                act.dma_start(yins[i], moe2[i * P:(i + 1) * P, :, :]).then_inc(moe_in[i], 16)
            for i in range(TT + 1):
                if i < TT:
                    r = rows(i)
                    act.wait_ge(S["x2T_ps"], i + 1)
                    A.activation(hT[:, 0:4, tok(i)],
                                 bank[2 * (i % 2)][:, :].rearrange("p (k t) -> p k t", k=4)[:, :, 0:r],
                                 ACT.Copy).then_inc(S["x2T_low"], 1)
                    if i + 2 < TT:
                        n = i + 2
                        act.wait_ge(S["x2_done"], i + 1)
                        act.dma_start(yins[i % 2][0:rows(n), :, :],
                                      moe2[n * P:n * P + rows(n), :, :]).then_inc(moe_in[i % 2], 16)
                if i >= 1:
                    t = i - 1
                    r = rows(t)
                    act.wait_ge(S["pg_done"], t + 1)
                    if t >= 2:
                        act.wait_ge(S["x3_done"], t - 1)
                    for a in range(2):
                        A.activation(sg[0:r, t % 2, a * 512:(a + 1) * 512], pair(4 + 2 * (t % 2))[a][0:r, :],
                                     ACT.Sigmoid).then_inc(S["sg_done"], 1)
                    act.wait_ge(S["x3_done"], t + 1)
                    if t >= 1:
                        act.wait_ge(S["x3_sq"], t)
                    A.activation(junk[0:r, :], xt[0:r, t % 2, :], ACT.Square,
                                 accum_out=ssq4[0:r, t:t + 1]).then_inc(S["x3_sq"], 1)
                    act.wait_ge(S["x3_sq"], t + 1)
                    A.activation(rst4[0:r, t:t + 1], ssq4[0:r, t:t + 1], ACT.Sqrt, bias=epsb[0:r, :],
                                 scale=1.0 / D).then_inc(S["x3_std"], 1)
                    if t >= 1:
                        act.wait_ge(S["out_done"], t)
                        act.dma_start(y_rows(t - 1), yo[0:rows(t - 1), (t - 1) % 2, :]).then_inc(y_stored[(t - 1) % 2], 16)
            act.wait_ge(S["out_done"], TT)
            act.dma_start(y_rows(TT - 1), yo[0:NS, (TT - 1) % 2, :]).then_inc(y_stored[0], 16)
            act.wait_ge(y_stored[0], 48)
            act.wait_ge(y_stored[1], 32)
            act.wait_ge(S["tail_out"], 16 * (1 + NB))
            act.wait_ge(S["cs_copy"], 16)
            act.wait_ge(S["rp_out"], 16)
            act.wait_ge(S["rs_out"], 16)

        @block.gpsimd
        def _(pool):
            G = nc.gpsimd
            order = [0]

            def then(ins):
                order[0] += 1
                ins.then_inc(S["pool_order"], 1)
                pool.wait_ge(S["pool_order"], order[0])

            G.memset(uext[:, :, 0:HIST], 0.0).then_inc(S["zero_x"], 1)
            pool.wait_ge(S["const_in"], 16)
            ta = Sm[:, :, :]
            tb = qTx[:, :, :]
            for j in range(2):
                for i in range(TT):
                    r = rows(i)
                    pool.wait_ge(S["z_sb"], j * TT + i + 1)
                    v = z[0:r, i, j, :].rearrange("p (h a n) -> p h a n", h=NH, a=2)
                    aa = ta[0:r].rearrange("p h (a n) -> p h a n", a=2)
                    bb = tb[0:r].rearrange("p h (a n) -> p h a n", a=2)
                    cos = bc(bc(rope_t[0:r, i, 0, :], 1, 2), 1, NH)
                    sin = bc(bc(rope_t[0:r, i, 1, :], 1, 2), 1, NH)
                    then(G.tensor_tensor(aa, v, cos, ALU.mult))
                    then(G.tensor_tensor(bb, v, sin, ALU.mult))
                    then(G.tensor_tensor(v[:, :, 0, :], aa[:, :, 0, :], bb[:, :, 1, :], ALU.subtract))
                    G.tensor_tensor(v[:, :, 1, :], bb[:, :, 0, :], aa[:, :, 1, :], ALU.add).then_inc(S["rope_done"], 1)
                    pool.wait_ge(S["rope_done"], j * TT + i + 1)
                if j == 0:
                    pool.wait_ge(S["u_done"], 2 * CT)
                    for c in range(CT):
                        G.tensor_copy(kTs[:, c, 0:NS].rearrange("p (b t) -> p b t", b=NB),
                                      sext[:, c, :, HIST:HIST + NL]).then_inc(S["tail_u"], 1)

            def k_decay(i):
                r = rows(i)
                if i:
                    pool.wait_ge(S["o_done"], i)
                zeta = C("zeta" if i < TT - 1 else "zeta_s", r)
                G.tensor_tensor(kz[0:r, :].rearrange("p (h d) -> p h d", h=NH),
                                z[0:r, i, 1, :].rearrange("p (h d) -> p h d", h=NH), bc(zeta, 2, HD),
                                ALU.mult).then_inc(S["kz_done"], 1)

            def v_masks(h):
                if h:
                    pool.wait_ge(S["kvs_done"], 2 * h)
                G.tensor_tensor(vmask, bc(z[0:NS, TT - 1, 2, h * HD:(h + 1) * HD], 1, NB),
                                bc(C("row8", NS), 2, HD), ALU.mult).then_inc(S["vm_done"], 1)

            k_decay(0)
            for i in range(TT):
                r = rows(i)
                if i == TT - 1:
                    pool.wait_ge(S["qTx_sb"], TT)
                    eye = C("eye8").rearrange("p (b c) -> p b c", b=NB)
                    for h in range(NH):
                        G.tensor_tensor(qmask[:, h, :, :].rearrange("p b (c t) -> p b c t", c=NB),
                                        bc(qTx[:, h, 0:NS].rearrange("p (c t) -> p c t", c=NB), 1, NB),
                                        bc(eye, 3, NL), ALU.mult).then_inc(S["qm_done"], 1)
                    v_masks(0)
                pool.wait_ge(S["gn_var"], i + 1)
                G.tensor_tensor(grs[0:r, :], mv[0:r, :, 1], half[0:r, :], ALU.pow).then_inc(S["gn_rstd"], 1)
                if i < TT - 1:
                    k_decay(i + 1)
                pool.wait_ge(S["on_done"], NH * (i + 1))
                pool.wait_ge(S["z_sb"], 16 + i)
                G.tensor_tensor(z[0:r, i, 3, :], z[0:r, i, 3, :], z[0:r, i, 0, :], ALU.mult).then_inc(S["og_done"], 1)
            for h in range(1, NH):
                v_masks(h)

            pool.wait_ge(S["idx_done"], 2)
            pool.wait_ge(h2_out[0], 48)
            pool.wait_ge(h2_out[1], 32)
            pool.wait_ge(S["h2T_ps"], TT)

            def wait(on, value):
                pool.wait_ge(on, value)
                pool.sem_inc(S["ticks"], 1)

            def column(dst, src, n, done, count):
                G.tensor_copy(dst, src[:, bass.ds(n, 1)]).then_inc(done, 1)
                wait(done, count)

            def gather(i, par):
                if not (isinstance(i, int) and i == 0):
                    wait(S["xt_ps"], 2 * i + par - 1)
                column(cur_tok[:, par:par + 1], tokidx, 2 * i + par, S["cur_done"], 2 * i + par + 1)
                G.indirect_dma_start(X[:, par, :], None, h2_d, bass.IndirectOffsetOnAxis(ap=cur_tok[:, par:par + 1], axis=0),
                                     bounds_check=T - 1, oob_is_err=False).then_inc(gathered[par], 16)

            def scatter(i, par):
                if not (isinstance(i, int) and i == 0):
                    wait(scattered[par], 16 * i)
                column(cur_code[:, par:par + 1], codes, 2 * i + par, S["pool_codes"], 2 * i + par + 1)
                wait(S["y_ready"], 2 * (2 * i + par) + 2)
                G.indirect_dma_start(moe_d, bass.IndirectOffsetOnAxis(ap=cur_code[:, par:par + 1], axis=0),
                                     yout[:, par, :], None, bounds_check=2 * T - 1,
                                     oob_is_err=False).then_inc(scattered[par], 16)

            gather(0, 0)
            gather(0, 1)
            for i in range(2):
                for par in range(2):
                    gather(i + 1, par)
                    scatter(i, par)
            with pool.Fori(2, NE // 2 - 1) as i:
                for par in range(2):
                    gather(i + 1, par)
                    scatter(i, par)
            for par in range(2):
                scatter(NE // 2 - 1, par)

            pool.wait_ge(scattered[0], 8 * NE)
            pool.wait_ge(scattered[1], 8 * NE)
            pool.sem_inc(S["ov_end"], 1)
            pool.wait_ge(S["idx_done"], 3)
            n_ov = pool.value_load(ovinfo[0:1, NOV:NOV + 1], min_val=0, max_val=NOV)
            with pool.If(n_ov > 0):
                with pool.Fori(0, NOV) as j:
                    G.tensor_copy(cur_tok[:, 0:1], tokidx[:, bass.ds(j + NE, 1)]).then_inc(S["ov_cur"], 1)
                    G.tensor_copy(cur_code[:, 0:1], codes[:, bass.ds(j + NE, 1)]).then_inc(S["ov_cur"], 1)
                    wait(S["ov_cur"], 2 * j + 2)
                    G.indirect_dma_start(X[:, 0, :], None, h2_d, bass.IndirectOffsetOnAxis(ap=cur_tok[:, 0:1], axis=0),
                                         bounds_check=T - 1, oob_is_err=False).then_inc(S["ov_gather"], 16)
                    wait(S["ov_y"], 2 * j + 2)
                    G.indirect_dma_start(moe_d, bass.IndirectOffsetOnAxis(ap=cur_code[:, 0:1], axis=0),
                                         yout[:, 0, :], None, bounds_check=2 * T - 1,
                                         oob_is_err=False).then_inc(S["ov_out"], 16)
                    wait(S["ov_out"], 16 * j + 16)
                    pool.sem_inc(S["ov_end"], 1)
            pool.nop()
            pool.sem_inc(S["moe_out"], 1)


_INS = ["x_prompt", "x_sample", "p_prompt", "p_sample", "state_conv", "state_ret", "w_in", "conv_w", "conv_b",
        "conv_ln_g", "conv_ln_b", "w_out", "norm1_g", "norm2_g", "router_group_w", "router_group_b",
        "router_expert_w", "router_expert_b", "w_expert_gate", "w_expert_up", "w_expert_down", "w_ple",
        "ple_norm_g", "w_ple_gate", "final_norm_g"]
_OUTS = [(1, SEQ, D), (NB, NL, D), (1, 1, HIST, CH), (1, 1, NH, HD, HD), (1, NB, HIST, CH), (1, NB, NH, HD, HD)]


def kernel(**inputs):
    import concourse.bacc as _bacc
    from concourse.bass_utils import run_bass_kernel_spmd as _run

    nc = _bacc.Bacc("TRN2", target_bir_lowering=False, num_devices=1)
    arrays, args = {}, []
    for name in _INS:
        a = np.ascontiguousarray(inputs[name])
        arrays[f"in_{name}"] = a
        args.append(nc.dram_tensor(f"in_{name}", a.shape, mybir.dt.from_np(a.dtype), kind="ExternalInput").ap())
    arrays["constants"] = constants()
    args.append(nc.dram_tensor("constants", (P, NCONST), F32, kind="ExternalInput").ap())
    outs = [nc.dram_tensor(f"out_{i}", shape, F32, kind="ExternalOutput").ap() for i, shape in enumerate(_OUTS)]
    build(nc, args, outs)
    r = _run(nc, [arrays], core_ids=[0])
    return tuple(r.results[0][f"out_{i}"] for i in range(len(_OUTS)))
```

```python
from contextlib import ExitStack

import numpy as np

import concourse.bass as bass
from concourse import mybir

F32 = mybir.dt.float32
I32 = mybir.dt.int32
ALU = mybir.AluOpType
ACT = mybir.ActivationFunctionType
AX = mybir.AxisListType

P = 128
D = 1024
KT = D // P
SEQ = 512
NB, NL = 8, 8
NS = NB * NL
T = SEQ + NS
TT = 5
CH, CT = 512, 4
TAPS = 31
HIST = TAPS - 1
NH, HD = 4, 128
PLE = 256
NG, NEG = 4, 8
NE = NG * NEG
FF = 256
EPS = 1e-6
SLOTS = 128
DEEP = -(-T // SLOTS)
NOV = (2 * T - NE) // SLOTS if SLOTS < 128 else 8
NBLK = NE + NOV
RING = 6
NX = 4
LOOPS = NE // NX
CHUNK = 2048
GAMMA = [1.0 - 2.0 ** (-5.0 - h) for h in range(NH)]

COLS = {}
_at = 0
for _name, _n in (("ident", P), ("ones", P), ("before", P), ("decay", NH * P), ("xi", NH * P), ("zeta", NH),
                  ("decay_s", NH * NS), ("zeta_s", NH), ("eye8", NB * NB), ("row8", NB), ("rope", TT * 2 * 64),
                  ("lane", P), ("block", NBLK), ("expert", NE), ("code", TT * 2), ("rev", NEG), ("ovj", NOV)):
    COLS[_name] = (_at, _n)
    _at += _n
NCONST = _at


def rows(i):
    return P if i < TT - 1 else NS


def constants():
    c = np.zeros((P, NCONST), np.float64)

    def put(name, value):
        a, n = COLS[name]
        v = np.asarray(value, np.float64)
        c[: v.shape[0], a:a + n] = v.reshape(v.shape[0], n)

    lg = np.array([np.log(g) for g in GAMMA])
    p = np.arange(P)
    put("ident", np.eye(P))
    put("ones", np.ones((P, P)))
    put("before", p[:, None] < p[None, :])
    scale = HD ** -0.5
    rel = p[None, :] - p[:, None]
    put("decay", np.stack([np.where(rel >= 0, np.exp(np.maximum(rel, 0) * g), 0.0) * scale for g in lg], 1))
    put("xi", np.broadcast_to(np.stack([np.exp((p + 1) * g) for g in lg])[None], (P, NH, P)))
    put("zeta", np.stack([np.exp((P - 1 - p) * g) * scale for g in lg], 1))
    s = np.arange(NS)
    rs = s[None, :] - s[:, None]
    same = (s[None, :] // NL == s[:, None] // NL) & (rs >= 0)
    put("decay_s", np.stack([np.where(same, np.exp(np.maximum(rs, 0) * g), 0.0) * scale for g in lg], 1))
    put("zeta_s", np.stack([np.exp((NL - 1 - s % NL) * g) * scale for g in lg], 1))
    put("eye8", np.broadcast_to(np.eye(NB).reshape(1, -1), (P, NB * NB)))
    put("row8", (s[:, None] // NL == np.arange(NB)[None, :]))
    inv = (10000.0 ** (-np.arange(64, dtype=np.float64) / 64)).astype(np.float32)
    pos = np.zeros((P, TT), np.float32)
    for i in range(TT - 1):
        pos[:, i] = i * P + p
    pos[:NS, TT - 1] = 4096 + s % NL
    ang = (pos[:, :, None] * inv[None, None, :]).astype(np.float64)
    put("rope", np.stack([np.cos(ang), np.sin(ang)], 2))
    put("lane", np.broadcast_to(p[None].astype(float), (P, P)))
    put("block", np.broadcast_to(np.arange(NBLK)[None].astype(float), (P, NBLK)))
    put("expert", np.broadcast_to(np.arange(NE)[None].astype(float), (P, NE)))
    tok = np.arange(TT)[None, :] * P + p[:, None]
    put("code", np.stack([2 * tok + 1, 2 * tok + 2], 2))
    put("rev", np.broadcast_to((NEG - np.arange(NEG))[None].astype(float), (P, NEG)))
    put("ovj", np.broadcast_to(np.arange(NOV)[None].astype(float), (P, NOV)))
    return c.astype(np.float32)


def bc(ap, axis, n):
    a = ap.unsqueeze(axis)
    shape = list(a.shape)
    shape[axis] = n
    return a.to_broadcast(shape)


def build(nc, ins, outs):
    (x_prompt, x_sample, p_prompt, p_sample, state_conv, state_ret, w_in, conv_w, conv_b, conv_ln_g, conv_ln_b,
     w_out, norm1_g, norm2_g, rg_w, rg_b, re_w, re_b, w_gate, w_up, w_down, w_ple, ple_norm_g, w_ple_gate,
     final_norm_g, consts_d) = ins
    y_prompt, y_sample, conv_p, ret_p, conv_s, ret_s = outs
    h2_d = nc.dram_tensor("h2_rows", (T, D), F32, kind="Internal").ap()
    moe_d = nc.dram_tensor("expert_rows", (2 * T, D), F32, kind="Internal").ap()

    with ExitStack() as ctx:
        def sb(name, shape, dt=F32):
            return ctx.enter_context(nc.sbuf_tensor(name, shape, dt))

        def sem(name):
            return ctx.enter_context(nc.semaphore(name))

        ring = sb("ring", [P, RING, CHUNK])
        const = sb("const", [P, NCONST])
        hT = sb("hT", [P, KT, T])
        front = sb("front", [P, TT * D])
        scratch = sb("scratch", [P, CT * T])
        z = sb("z", [P, TT, 4, 512])
        uext = sb("uext", [P, CT, HIST + SEQ])
        sext = sb("sext", [P, CT, NB, HIST + NL])
        cv = sb("cv", [P, CT * T])
        catT = sb("catT", [P, KT, T])
        kz = sb("kz", [P, 512])
        Rst = sb("Rst", [P, NH, HD])
        qTs = sb("qTs", [P, NH, P])
        qTx = sb("qTx", [P, NH, P])
        kTs = sb("kTs", [P, NH, P])
        Sm = sb("Sm", [P, NH, P])
        gbc = sb("gbc", [P, D])
        g1c = sb("g1c", [P, KT])
        cpar = sb("cpar", [P, CT, TAPS + 3])
        ssq = sb("ssq", [P, TT])
        rst = sb("rst", [P, TT])
        ssq2 = sb("ssq2", [P, TT])
        rst2 = sb("rst2", [P, TT])
        ssq3 = sb("ssq3", [P, TT, 2])
        rst3 = sb("rst3", [P, TT])
        ssq4 = sb("ssq4", [P, TT])
        rst4 = sb("rst4", [P, TT])
        bns = sb("bns", [P, NH, 6])
        mv = sb("mv", [P, NH, 2])
        grs = sb("grs", [P, NH])
        half = sb("half", [P, NH])
        epsb = sb("epsb", [P, 1])
        tokidx = sb("tokidx", [P, NBLK], I32)
        codes = sb("codes", [P, NBLK], I32)
        cur_tok = sb("cur_tok", [P, NX], I32)
        cur_code = sb("cur_code", [P, 2], I32)
        ovinfo = sb("ovinfo", [1, NOV + 1], I32)
        gates = sb("gates", [P, TT, 2])
        wr = sb("wr", [P, KT, NG + NE])
        rbias = sb("rbias", [P, NG + NE])

        def view(t, off, dims):
            n = int(np.prod(dims))
            flat = t[:, off:off + n]
            if len(dims) == 1:
                return flat
            names = "abcd"[: len(dims)]
            return flat.rearrange("p (" + " ".join(names) + ") -> p " + " ".join(names),
                                  **{k: v for k, v in zip(names[1:], dims[1:])})

        flat_cat = catT[:, :, :].rearrange("p k t -> p (k t)")
        flat_u = uext[:, :, :].rearrange("p c t -> p (c t)")
        flat_s = sext[:, :, :, :].rearrange("p c b t -> p (c b t)")
        flat_z = z[:, :, :, :].rearrange("p i j n -> p (i j n)")
        flat_h = hT[:, :, :].rearrange("p k t -> p (k t)")
        x_sb = view(front, 0, (TT, D))
        states = view(front, 0, (NB, NH, HD))
        xn = view(scratch, 0, (2, D))
        h2 = [xn[:, 0, :], xn[:, 1, :]] + [front[:, n * D:(n + 1) * D] for n in range(3)]
        squares = view(scratch, 0, (CT, T))
        conv = view(cv, 0, (CT, T))
        p_sb = view(cv, 0, (TT, PLE))
        cpar_rows = flat_z[0:TAPS + 3, 0:CH]
        sq_out = flat_z[:, 4096:4096 + D]
        hist_rows = flat_z[0:120, CH:3 * CH].rearrange("p (a c) -> p a c", a=2)
        sig = flat_cat[:, 0:2 * T].rearrange("p (a t) -> p a t", a=2)
        tails = flat_cat[:, 4 * T:4 * T + 2 * CH].rearrange("p (a c) -> p a c", a=2)
        qmask = flat_u[:, 0:NH * NB * NS].rearrange("p (h b t) -> p h b t", h=NH, b=NB)
        vmask = [t.rearrange("p (b e) -> p b e", b=NB) for t in (flat_s[0:NS, 0:NB * HD], cv[0:NS, 5 * PLE:5 * PLE + NB * HD])]
        pT = flat_u[:, 0:2 * T].rearrange("p (k t) -> p k t", k=2)
        pbc = flat_s[:, 0:D]
        rt = [0]

        def work(n):
            rt[0] += n
            return flat_cat[:, rt[0] - n:rt[0]]

        logit = work(TT * 36).rearrange("p (i n) -> p i n", i=TT)
        gmx, gsum, m1, m2, e2, t1 = (work(TT) for _ in range(6))
        gexp = work(TT * NG).rearrange("p (i n) -> p i n", i=TT)
        gval = work(TT * NG).rearrange("p (i n) -> p i n", i=TT)
        gone = work(TT * NG).rearrange("p (i n) -> p i n", i=TT)
        sel = work(TT * NE).rearrange("p (i g e) -> p i g e", i=TT, g=NG)
        el = work(TT * NEG).rearrange("p (i n) -> p i n", i=TT)
        eval_ = work(TT * NEG).rearrange("p (i n) -> p i n", i=TT)
        one1 = work(TT * NEG).rearrange("p (i n) -> p i n", i=TT)
        one2 = work(TT * NEG).rearrange("p (i n) -> p i n", i=TT)
        M = [work(TT * NE).rearrange("p (i n) -> p i n", i=TT) for _ in range(2)]
        both = work(TT * NE).rearrange("p (i n) -> p i n", i=TT)
        rank = work((TT + 1) * NE).rearrange("p (i n) -> p i n", i=TT + 1)
        deep = work(TT * NE).rearrange("p (i n) -> p i n", i=TT)
        flag = work(TT * NE).rearrange("p (i n) -> p i n", i=TT)
        blk = work(TT * NE).rearrange("p (i n) -> p i n", i=TT)
        lane = work(TT * NE).rearrange("p (i n) -> p i n", i=TT)
        prod = work(TT * NE).rearrange("p (i n) -> p i n", i=TT)
        ov = work(NE)
        ovi = work(NE)
        ovb = work(NE)
        ovw = work(NE)
        zero32 = work(NE)
        posb = work(2 * TT).rearrange("p (a i) -> p a i", a=2)
        posl = work(2 * TT).rearrange("p (a i) -> p a i", a=2)
        laneone = flat_h[:, 2 * D:2 * D + 2 * TT * P].rearrange("p (a n) -> p a n", a=2 * TT)
        blockone = flat_h[:, 2 * D + 2 * TT * P:2 * D + 2 * TT * (P + NBLK)].rearrange("p (a n) -> p a n", a=2 * TT)
        tabf = work(NBLK)
        tabz = work(NBLK)
        ovt = work(2 * NOV * NE).rearrange("p (a j e) -> p a j e", a=2, j=NOV)
        ovf = work(NOV + 1)
        assert rt[0] <= KT * T, rt[0]
        junk = view(front, 4 * D, (D,))
        X = [xn[:, 0, :], xn[:, 1, :], front[:, 2 * D:3 * D], front[:, 3 * D:4 * D]]
        XT = flat_h[:, 0:2 * D].rearrange("p (a k s) -> p a k s", a=2, k=KT)
        hid = view(cv, 0, (2, FF))
        gat = view(cv, 2 * FF, (2, FF))
        hidT = view(cv, 4 * FF, (2, 2, P))
        yout = view(front, 0, (2, D))
        yin = flat_u[:, 0:2 * D].rearrange("p (a n) -> p a n", a=2)
        yin2 = flat_cat[:, 0:2 * D].rearrange("p (a n) -> p a n", a=2)
        yins = [yin, yin2]
        sg = view(scratch, 0, (2, D))
        yo = view(front, 0, (2, D))
        xt = view(front, 2 * D, (2, D))

        def C(name, r=P):
            a, n = COLS[name]
            return const[0:r, a:a + n]

        ident = C("ident")
        rope_t = C("rope").rearrange("p (i c n) -> p i c n", i=TT, c=2)

        bank = [ctx.enter_context(nc.psum_tensor(f"bank{i}", [P, 512], F32)) for i in range(8)]

        def pair(b):
            return [bank[b], bank[b + 1]]

        names = """const_in ident_in params_in hist_in states_in router_in gbc_in final_in pbc_in p_in cpar_T
            hist_T xT_ps ab_done mean_done var_done z_done qk_T s_done o_done kvs_done oT_done tail_T
            wo_done pT_ps ple_done h2T_ps logit_done rank_done table_done gu_done xt_ps hT_ps d_done cpar_sb
            hist_sb hT_sb u_done sig_done convp convs cmean csq cstd crstd cdone z_sb rope_done qT_sb qTx_sb
            kT_sb s_sb kz_done gn_var gn_rstd on_done og_done oT_sb r_upd tail_u tail_sb tail_out qm_done
            vm_done vm2_done rs_upd rs_out rp_out x1_sum x1_sq x1_std x1_rstd h2_done h2T_sb xsq xstd xrstd
            xn_done zeroed dve_order pool_order pT_sb ple_sq ple_var ple_std ple_sb logit_sb gexp_done
            picks_done laneone_done table_sb idx_done xt_sb sil_done hid_done hT_ev y_ready zero_x cur_done
            pool_codes ticks moe_out ov_load ov_gather ov_cur ov_xt ov_xtsb ov_gu ov_sil ov_hid ov_hT
            ov_hTsb ov_d ov_y ov_out ov_end x2_done x2T_ps x2T_low x2T_high pg_done sg_done x3_done x3_sq
            x3_std x3_rstd out_done cs_copy x2_order h2_out ple_raw""".split()
        S = {n: sem(n) for n in names}
        x_in = [sem(f"x_in{i}") for i in range(TT)]
        x_back = [sem(f"x_back{i}") for i in range(TT)]
        slot_in = [sem(f"slot_in{i}") for i in range(RING)]
        y_stored = [sem(f"y_stored{i}") for i in range(2)]
        gathered = [sem(f"gathered{i}") for i in range(NX)]
        scattered = [sem(f"scattered{i}") for i in range(2)]
        moe_in = [sem(f"moe_in{i}") for i in range(2)]
        block = ctx.enter_context(nc.Block())

        def before(i, q):
            return (i, q - 1) if q else (i - 1, NX - 1)

        def after(i, q):
            return (i, q + 1) if q < NX - 1 else (i + 1, 0)

        def x_rows(i):
            return x_prompt[0, i * P:(i + 1) * P, :] if i < TT - 1 else x_sample.rearrange("b t d -> (b t) d")

        def p_rows(i):
            return p_prompt[0, 0, i * P:(i + 1) * P, :] if i < TT - 1 else p_sample[0].rearrange("b t d -> (b t) d")

        def y_rows(i):
            return y_prompt[0, i * P:(i + 1) * P, :] if i < TT - 1 else y_sample.rearrange("b t d -> (b t) d")

        def tok(i):
            return slice(i * P, i * P + rows(i))

        def w_cols(w, n):
            return w.rearrange("(p k) n -> p k n", k=KT)[:, :, n * 256:(n + 1) * 256]

        def w_cols_k(w, n):
            return w.rearrange("(k p) n -> p k n", p=P)[:, :, n * 256:(n + 1) * 256]

        def slot8(s):
            return ring[:, s, :].rearrange("p (k n) -> p k n", k=KT)

        def slots8(s):
            return ring[:, s:s + 2, :].rearrange("p a (k n) -> p k a n", k=KT)

        def slot2(s):
            return ring[:, s, :].rearrange("p (k n) -> p k n", k=2)

        def gate_rows(e):
            return w_gate[0, e, :, :].rearrange("(p k) f -> p (k f)", k=KT)

        @block.sync
        def _(sp):
            W = w_in[0]

            def load(s, view_, src):
                sp.dma_start(view_, src).then_inc(slot_in[s], 16)

            for i in range(TT):
                sp.dma_start(x_sb[0:rows(i), i, :], x_rows(i)).then_inc(x_in[i], 16)
            sp.dma_start(const[:, P:NCONST], consts_d[:, P:NCONST]).then_inc(S["const_in"], 16)
            for s, n in enumerate((0, 2, 1, 3, 4, 5)):
                load(s, slot8(s), w_cols(W, n))
            sp.wait_ge(S["ab_done"], 2)
            load(0, slot8(0), w_cols(W, 6))
            load(1, slot8(1), w_cols(W, 7))
            sp.wait_ge(S["ab_done"], 4)
            load(2, slot8(2), w_cols(W, 8))
            load(3, slot8(3), w_cols(W, 9))
            sp.wait_ge(S["z_done"], TT)
            load(4, slot8(4), w_cols(W, 10))
            load(5, slot8(5), w_cols(W, 11))
            sp.wait_ge(S["z_done"], 2 * TT)
            load(0, slot8(0), w_cols_k(w_out[0], 0))
            load(1, slot8(1), w_cols_k(w_out[0], 1))
            sp.wait_ge(S["z_done"], 3 * TT)
            load(2, slot8(2), w_cols_k(w_out[0], 2))
            load(3, slot8(3), w_cols_k(w_out[0], 3))
            for i in range(TT):
                sp.wait_ge(S["og_done"], i + 1)
                sp.dma_start(z[0:rows(i), i, 0:2, :].rearrange("p a n -> p (a n)"), x_rows(i)).then_inc(x_back[i], 16)
            load(4, ring[:, 4, :], w_ple[0].rearrange("(p k) n -> p (k n)", k=2))
            sp.wait_ge(S["wo_done"], TT)
            load(0, ring[:, 0, :], gate_rows(0))
            load(1, ring[:, 1, :], w_up[0, 0, :, :].rearrange("(p k) f -> p (k f)", k=KT))
            load(2, ring[:, 2, :], w_down[0, 0, :, :].rearrange("(p k) n -> p (k n)", k=2))
            load(3, ring[:, 3, :], gate_rows(1))
            load(5, ring[:, 5, :], w_down[0, 1, :, :].rearrange("(p k) n -> p (k n)", k=2))
            sp.wait_ge(S["ple_done"], TT)
            load(4, ring[:, 4, :], w_up[0, 1, :, :].rearrange("(p k) f -> p (k f)", k=KT))
            wg3 = w_gate[0].rearrange("e (p k) f -> e p (k f)", k=KT)
            wu3 = w_up[0].rearrange("e (p k) f -> e p (k f)", k=KT)
            wd3 = w_down[0].rearrange("e (p k) n -> e p (k n)", k=2)
            with sp.Fori(1, NE // 2) as i:
                for par in range(2):
                    for m, w3 in ((0, wg3), (1, wu3), (2, wd3)):
                        s = 3 * par + m
                        if m != 1:
                            sp.wait_ge(S["gu_done" if m == 0 else "d_done"], 2 * i - 1 + par)
                        src = w3[bass.ds(2 * i + par, 1), :, :].rearrange("e p n -> (e p) n")
                        load(s, ring[:, s, :], src)
            sp.wait_ge(S["idx_done"], 3)
            n_ov = sp.value_load(ovinfo[0:1, NOV:NOV + 1], min_val=0, max_val=NOV)
            sp.wait_ge(S["d_done"], NE)
            with sp.If(n_ov > 0):
                with sp.Fori(0, NOV) as j:
                    e = sp.value_load(ovinfo[0:1, bass.ds(j, 1)], min_val=0, max_val=NE - 1)
                    sp.wait_ge(S["ov_end"], j + 1)
                    for s, w3 in ((0, wg3), (1, wu3), (2, wd3)):
                        src = w3[bass.ds(e, 1), :, :].rearrange("e p n -> (e p) n")
                        sp.dma_start(ring[:, s, :], src).then_inc(S["ov_load"], 16)
                sp.wait_ge(S["ov_end"], NOV + 1)
            sp.nop()
            for s in range(4):
                load(s, slot8(s), w_cols(w_ple_gate[0], s))

        @block.tensor
        def _(pe):
            def mm(out, lhsT, rhs, start, stop):
                return nc.tensor.matmul(out, lhsT, rhs, start=start, stop=stop, skip_group_check=True)

            def tr(out, in_):
                k = in_.shape[0]
                return nc.tensor.transpose(out, in_, ident[0:k, 0:k])

            def slot_ready(s, use):
                pe.wait_ge(slot_in[s], 16 * use)

            def rows_T(src, i, banks, done):
                r = rows(i)
                for k in range(KT):
                    m = tr(banks[k // 4][:, (k % 4) * P:(k % 4) * P + r], src[0:r, k:D:KT])
                m.then_inc(done, 1)

            pe.wait_ge(S["ident_in"], 16)
            for i in range(TT):
                pe.wait_ge(S["xn_done"], i + 1)
                if i >= 2:
                    pe.wait_ge(S["hT_sb"], 2 * (i - 1))
                rows_T(xn[:, i % 2, :], i, pair(2 * (i % 2)), S["xT_ps"])

            pe.wait_ge(S["params_in"], 80)
            for c in range(CT):
                m = tr(bank[6][:, c * 34:(c + 1) * 34], cpar_rows[:, c * P:(c + 1) * P])
            m.then_inc(S["cpar_T"], 1)
            pe.wait_ge(S["hist_in"], 32)
            for a in range(2):
                for c in range(CT):
                    m = tr(bank[4 + a][:, c * 120:(c + 1) * 120], hist_rows[:, a, c * P:(c + 1) * P])
                m.then_inc(S["hist_T"], 1)

            for c in range(CT):
                if c == 0:
                    pe.wait_ge(S["hT_sb"], 2 * TT)
                    pe.wait_ge(S["hist_sb"], 2)
                    pe.wait_ge(S["cpar_sb"], 1)
                if c >= 2:
                    pe.wait_ge(S["u_done"], 2 * (c - 1))
                for n in range(2):
                    s = 2 * (c // 2) + n
                    slot_ready(s, 1)
                    for k in range(KT):
                        w = slot8(s)[:, k, (c % 2) * P:(c % 2 + 1) * P]
                        mm(bank[2 + 2 * (c % 2) + n][:, :], w, hT[:, k, 0:SEQ], k == 0, k == KT - 1)
                    for k in range(KT):
                        w = slot8(s)[:, k, (c % 2) * P:(c % 2 + 1) * P]
                        m = mm(bank[(6, 1)[c % 2]][:, n * NS:(n + 1) * NS], w, hT[:, k, SEQ:T], k == 0, k == KT - 1)
                m.then_inc(S["ab_done"], 1)

            def z_part(j, i, k0, k1):
                n = j * TT + i
                s = (4, 0, 2, 4)[j]
                if k0 == 0:
                    if n == 1:
                        pe.wait_ge(S["sig_done"], 2 * (CT - 1))
                    if n >= 2:
                        pe.wait_ge(S["z_sb"], n - 1)
                    if i == 0:
                        for t in (s, s + 1):
                            slot_ready(t, (1, 2, 2, 2)[j])
                r = rows(i)
                for k in range(k0, k1):
                    m = mm(bank[3 * (n % 2)][0:r, :], hT[:, k, tok(i)], slots8(s)[:, k, :, :], k == 0, k == KT - 1)
                if k1 == KT:
                    m.then_inc(S["z_done"], 1)

            for j in range(2):
                for i in range(TT):
                    z_part(j, i, 0, KT)
            z_part(2, 0, 0, KT)
            z_part(2, 1, 0, KT)

            def channel_sum(src, b, done):
                for c in range(CT):
                    mm(bank[b][:, :], C("ones"), src[:, c, 0:SEQ], c == 0, c == CT - 1)
                for c in range(CT):
                    m = mm(bank[b - 1][:, 0:NS], C("ones"), src[:, c, SEQ:T], c == 0, c == CT - 1)
                m.then_inc(done, 1)

            pe.wait_ge(S["const_in"], 16)
            pe.wait_ge(S["convp"], CT * TAPS)
            pe.wait_ge(S["convs"], CT * TAPS)
            channel_sum(conv, 7, S["mean_done"])
            pe.wait_ge(S["tail_u"], CT)
            for c in range(CT):
                tr(bank[4][0:HIST, c * P:(c + 1) * P], uext[:, c, SEQ:SEQ + HIST])
            for c in range(CT):
                m = tr(bank[5][0:NS, c * P:(c + 1) * P], kTs[:, c, 0:NS])
            m.then_inc(S["tail_T"], 1)
            for i in range(2, TT):
                z_part(2, i, 0, KT)
            pe.wait_ge(S["csq"], 1)
            pe.wait_ge(S["tail_sb"], 2)
            channel_sum(squares, 5, S["var_done"])

            def retention_scores(i):
                r = rows(i)
                pe.wait_ge(S["qT_sb"], i + 1)
                pe.wait_ge(S["kT_sb"], i + 1)
                for h in range(NH):
                    m = mm(bank[4][0:r, h * P:h * P + r], kTs[:, h, 0:r], qTs[:, h, 0:r], True, True)
                m.then_inc(S["s_done"], 1)

            def retention_out(i):
                r = rows(i)
                pe.wait_ge(S["s_sb"], i + 1)
                pe.wait_ge(S["qTx_sb"], i + 1)
                if 0 < i < TT - 1:
                    pe.wait_ge(S["r_upd"], 1 + NH * (i - 1))
                if i == TT - 1:
                    pe.wait_ge(S["qm_done"], NH)
                    pe.wait_ge(S["states_in"], 16)
                if i >= 1:
                    pe.wait_ge(S["on_done"], NH * i)
                for h in range(NH):
                    o = bank[5][0:r, h * HD:(h + 1) * HD]
                    v = z[0:r, i, 2, h * HD:(h + 1) * HD]
                    if i == TT - 1:
                        for b in range(NB):
                            mm(o, qmask[:, h, b, :], states[:, b, h, :], b == 0, False)
                    elif i:
                        mm(o, qTx[:, h, 0:r], Rst[:, h, :], True, False)
                    m = mm(o, Sm[0:r, h, 0:r], v, i == 0, True)
                pe.wait_ge(S["kz_done"], i + 1)
                if i < TT - 1:
                    for h in range(NH):
                        m = mm(bank[6][:, h * HD:(h + 1) * HD], kz[:, h * HD:(h + 1) * HD],
                               z[:, i, 2, h * HD:(h + 1) * HD], True, True)
                m.then_inc(S["o_done"], 1)

            def gated_T(i):
                r = rows(i)
                pe.wait_ge(S["og_done"], i + 1)
                if i >= 1:
                    pe.wait_ge(S["oT_sb"], i)
                for h in range(NH):
                    m = tr(bank[7][:, h * P:h * P + r], z[0:r, i, 3, h * HD:(h + 1) * HD])
                m.then_inc(S["oT_done"], 1)

            for i in range(TT):
                r = rows(i)
                pe.wait_ge(S["rope_done"], TT + i + 1)
                if i == 0:
                    pe.wait_ge(S["cmean"], 2 * CT)
                for j, b in ((0, 2), (1, 1)):
                    for h in range(NH):
                        m = tr(bank[b][:, h * P:h * P + r], z[0:r, i, j, h * HD:(h + 1) * HD])
                m.then_inc(S["qk_T"], 1)
                z_part(3, i, 0, KT // 2)
                if i == 0:
                    pe.wait_ge(S["cstd"], 2)
                retention_scores(i)
                z_part(3, i, KT // 2, KT)
                retention_out(i)
                if i >= 1:
                    gated_T(i - 1)

            def sample_states(heads):
                for n in range(2 * heads[0], 2 * heads[-1] + 2):
                    h, a = n // 2, n % 2
                    pe.wait_ge(S["vm_done" if h % 2 == 0 else "vm2_done"], h // 2 + 1)
                    if n == 0:
                        pe.wait_ge(S["r_upd"], 1 + NH * (TT - 2))
                    if n >= 2:
                        pe.wait_ge(S["rs_upd"], n - 1)
                    mm(bank[(6, 4)[n % 2]][:, :], kz[0:NS, h * HD:(h + 1) * HD], vmask[h % 2][:, 4 * a:4 * a + 4, :],
                       True, True).then_inc(S["kvs_done"], 1)

            def w_out_tile(i):
                r = rows(i)
                if i == 0:
                    pe.wait_ge(S["cdone"], CT)
                    pe.wait_ge(S["z_sb"], 4 * TT)
                    for s in range(4):
                        slot_ready(s, (3, 3, 3, 3)[s])
                pe.wait_ge(S["oT_sb"], i + 1)
                if i >= 2:
                    pe.wait_ge(S["x1_sum"], 2 * (i - 1))
                for a in range(2):
                    for k in range(KT):
                        m = mm(pair(2 * (i % 2))[a][0:r, :], catT[:, k, tok(i)], slots8(2 * a)[:, k, :, :],
                               k == 0, k == KT - 1)
                m.then_inc(S["wo_done"], 1)

            def p_T(tiles):
                if tiles[0]:
                    pe.wait_ge(S["pT_sb"], tiles[0])
                else:
                    pe.wait_ge(S["oT_sb"], TT)
                for i in tiles:
                    for k in range(2):
                        c = 256 * (i % 2) + P * k
                        m = tr(bank[7][:, c:c + rows(i)], p_sb[0:rows(i), i, k:PLE:2])
                m.then_inc(S["pT_ps"], 1)

            def ple_tile(i):
                r = rows(i)
                if i == 0:
                    slot_ready(4, 3)
                    pe.wait_ge(S["pT_sb"], TT)
                if i < 2:
                    pe.wait_ge(S["x1_sum"], (2 * (TT - 1), 2 * TT)[i])
                else:
                    pe.wait_ge(S["ple_raw"], 2 * (i - 1))
                for a in range(2):
                    for k in range(2):
                        m = mm(pair(2 - 2 * (i % 2))[a][0:r, :], pT[:, k, tok(i)],
                               slot2(4)[:, k, a * 512:(a + 1) * 512], k == 0, k == 1)
                m.then_inc(S["ple_done"], 1)

            def h2_T(i):
                pe.wait_ge(S["h2_done"], i + 1)
                if i:
                    pe.wait_ge(S["h2T_sb"], 2 * i)
                else:
                    pe.wait_ge(S["rs_upd"], 2 * NH)
                rows_T(h2[i], i, pair(4), S["h2T_ps"])

            def router(i):
                if i == 0:
                    pe.wait_ge(S["router_in"], 64)
                pe.wait_ge(S["h2T_sb"], 2 * (i + 1))
                for k in range(KT):
                    m = mm(bank[6][0:rows(i), i * 36:(i + 1) * 36], hT[:, k, tok(i)], wr[:, k, :], k == 0, k == KT - 1)
                m.then_inc(S["logit_done"], 1)

            sample_states((0, 1))
            w_out_tile(0)
            gated_T(TT - 1)
            sample_states((2, 3))
            w_out_tile(1)
            pe.wait_ge(S["p_in"], 16 * TT)
            p_T((0, 1))
            w_out_tile(2)
            p_T((2, 3))
            h2_T(0)
            w_out_tile(3)
            p_T((4,))
            router(0)
            h2_T(1)
            w_out_tile(4)
            router(1)
            h2_T(2)
            ple_tile(0)
            router(2)
            h2_T(3)
            ple_tile(1)
            router(3)
            h2_T(4)
            ple_tile(2)
            router(4)
            ple_tile(3)
            pe.wait_ge(S["picks_done"], 1)
            for i in range(TT):
                for j in range(i + 1):
                    r = rows(j)
                    w = C("before", r) if j == i else C("ones", r)
                    mm(bank[7][0:rows(i), i * NE:(i + 1) * NE], w[:, 0:rows(i)], both[0:r, j, :], j == 0, j == i)
            for j in range(TT):
                r = rows(j)
                m = mm(bank[7][:, TT * NE:(TT + 1) * NE], C("ones", r), both[0:r, j, :], j == 0, j == TT - 1)
            m.then_inc(S["rank_done"], 1)
            ple_tile(4)
            for n in range(2 * TT):
                i, r = n // 2, rows(n // 2)
                pe.wait_ge(S["laneone_done"], 2 * (n + 1))
                mm(bank[5][:, 0:NBLK], laneone[0:r, n, :], blockone[0:r, n, :], n == 0,
                   n == 2 * TT - 1).then_inc(S["table_done"], 1)

            def x_T(i, q):
                pe.wait_ge(gathered[q], 16 * i + 16)
                for k in range(KT):
                    m = tr(bank[2 + k // 4][:, (k % 4) * P:(k % 4 + 1) * P], X[q][:, k:D:KT])
                m.then_inc(S["xt_ps"], 1)

            def gate_up(i, q):
                i, par = 2 * i + q // 2, q % 2
                pe.wait_ge(S["xt_sb"], 2 * (2 * i + par) + 2)
                for s in (3 * par, 3 * par + 1):
                    pe.wait_ge(slot_in[s], 16 * i + 64)
                for k in range(KT):
                    m = mm(bank[par][:, :], XT[:, par, k, :], slots8(3 * par)[:, k, :, :], k == 0, k == KT - 1)
                m.then_inc(S["gu_done"], 1)

            def hid_T(i, q):
                i, par = 2 * i + q // 2, q % 2
                pe.wait_ge(S["hid_done"], 2 * i + par + 1)
                for k in range(2):
                    m = tr(bank[4][:, k * P:(k + 1) * P], hid[:, par, k:FF:2])
                m.then_inc(S["hT_ps"], 1)

            def down(i, q):
                i, par = 2 * i + q // 2, q % 2
                pe.wait_ge(S["hT_ev"], 2 * i + par + 1)
                pe.wait_ge(slot_in[3 * par + 2], 16 * i + (64, 48)[par])
                if not (isinstance(i, int) and i == 0 and par == 0):
                    pe.wait_ge(S["y_ready"], 2 * (2 * i + par))
                for a in range(2):
                    for k in range(2):
                        m = mm(bank[5 + a][:, :], hidT[:, par, k, :],
                               slot2(3 * par + 2)[:, k, a * 512:(a + 1) * 512], k == 0, k == 1)
                m.then_inc(S["d_done"], 1)

            def step(i, q, first=False, last=False):
                gate_up(i, q)
                if not last:
                    x_T(*after(i, q))
                if not first:
                    down(*before(i, q))
                hid_T(i, q)

            pe.wait_ge(S["ple_raw"], 2 * TT)
            pe.wait_ge(S["table_sb"], 1)
            x_T(0, 0)
            step(0, 0, first=True)
            for q in range(1, NX):
                step(0, q)
            with pe.Fori(1, LOOPS - 1) as i:
                for q in range(NX):
                    step(i, q)
            for q in range(NX):
                step(LOOPS - 1, q, last=q == NX - 1)
            down(LOOPS - 1, NX - 1)

            pe.wait_ge(S["idx_done"], 3)
            n_ov = pe.value_load(ovinfo[0:1, NOV:NOV + 1], min_val=0, max_val=NOV)
            with pe.If(n_ov > 0):
                with pe.Fori(0, NOV) as j:
                    pe.wait_ge(S["ov_gather"], 16 * j + 16)
                    for k in range(KT):
                        m = tr(bank[2 + k // 4][:, (k % 4) * P:(k % 4 + 1) * P], X[0][:, k:D:KT])
                    m.then_inc(S["ov_xt"], 1)
                    pe.wait_ge(S["ov_xtsb"], 2 * j + 2)
                    pe.wait_ge(S["ov_load"], 48 * j + 48)
                    for k in range(KT):
                        m = mm(bank[0][:, :], XT[:, 0, k, :], slots8(0)[:, k, :, :], k == 0, k == KT - 1)
                    m.then_inc(S["ov_gu"], 1)
                    pe.wait_ge(S["ov_hid"], j + 1)
                    for k in range(2):
                        m = tr(bank[4][:, k * P:(k + 1) * P], hid[:, 0, k:FF:2])
                    m.then_inc(S["ov_hT"], 1)
                    pe.wait_ge(S["ov_hTsb"], j + 1)
                    for a in range(2):
                        for k in range(2):
                            m = mm(bank[5 + a][:, :], hidT[:, 0, k, :], slot2(2)[:, k, a * 512:(a + 1) * 512],
                                   k == 0, k == 1)
                    m.then_inc(S["ov_d"], 1)
            pe.nop()

            for i in range(TT + 1):
                if i < TT:
                    r = rows(i)
                    pe.wait_ge(S["x2_done"], i + 1)
                    if i >= 2:
                        pe.wait_ge(S["x2T_low"], i - 1)
                        pe.wait_ge(S["x2T_high"], i - 1)
                    else:
                        pe.wait_ge(S["y_ready"], 2 * NE)
                    rows_T(z[:, i, 0:2, :].rearrange("p a n -> p (a n)"), i, pair(2 * (i % 2)), S["x2T_ps"])
                if i >= 1:
                    t = i - 1
                    r = rows(t)
                    pe.wait_ge(S["x2T_low"], t + 1)
                    pe.wait_ge(S["x2T_high"], t + 1)
                    if t == 0:
                        for s in range(4):
                            slot_ready(s, 4 + NE // 2)
                    if t >= 2:
                        pe.wait_ge(S["sg_done"], 2 * (t - 1))
                    for a in range(2):
                        for k in range(KT):
                            m = mm(pair(4 + 2 * (t % 2))[a][0:r, :], hT[:, k, tok(t)], slots8(2 * a)[:, k, :, :],
                                   k == 0, k == KT - 1)
                    m.then_inc(S["pg_done"], 1)

        @block.vector
        def _(dve):
            V = nc.vector
            order = [0]

            def then(ins):
                order[0] += 1
                ins.then_inc(S["dve_order"], 1)
                dve.wait_ge(S["dve_order"], order[0])

            for t in (ssq, ssq2, ssq4):
                V.memset(t[:, :], 1.0).then_inc(S["zeroed"], 1)
            V.memset(ssq3[:, :, :], 1.0).then_inc(S["zeroed"], 1)
            V.memset(epsb[:, :], EPS).then_inc(S["zeroed"], 1)
            V.memset(half[:, :], -0.5).then_inc(S["zeroed"], 1)
            V.memset(mv[:, :, :], 1.0).then_inc(S["zeroed"], 1)
            def quads(i, a):
                return bank[2 * (i % 2) + a][:, :].rearrange("p (k t) -> p k t", k=4)[:, :, 0:rows(i)]

            def x_rstd(i):
                r = rows(i)
                dve.wait_ge(S["xstd"], i + 1)
                V.reciprocal(rst[0:r, i:i + 1], rst[0:r, i:i + 1]).then_inc(S["xrstd"], 1)

            def h_out(i):
                dve.wait_ge(S["xT_ps"], i + 1)
                for a in range(2):
                    g = bc(g1c[:, 4 * a:4 * a + 4], 2, rows(i))
                    V.tensor_tensor(hT[:, 4 * a:4 * a + 4, tok(i)], quads(i, a), g, ALU.mult).then_inc(S["hT_sb"], 1)

            x_rstd(0)
            dve.wait_ge(S["params_in"], 80)
            for i in range(TT):
                if i + 1 < TT:
                    x_rstd(i + 1)
                h_out(i)
            dve.wait_ge(S["cpar_T"], 1)
            V.tensor_copy(cpar[:, :, :], bank[6][:, 0:CT * 34].rearrange("p (c n) -> p c n", c=CT)).then_inc(S["cpar_sb"], 1)
            dve.wait_ge(S["const_in"], 16)

            dve.wait_ge(S["cpar_sb"], 1)
            dve.wait_ge(S["zero_x"], 1)
            dve.wait_ge(S["hist_sb"], 2)
            def glu(c):
                dve.wait_ge(S["sig_done"], 2 * (c + 1))
                V.tensor_tensor(uext[:, c, HIST:HIST + SEQ], bank[2 + 2 * (c % 2)][:, :], sig[:, c % 2, 0:SEQ],
                                ALU.mult).then_inc(S["u_done"], 1)
                V.tensor_tensor(sext[:, c, :, HIST:HIST + NL],
                                bank[(6, 1)[c % 2]][:, 0:NS].rearrange("p (b t) -> p b t", b=NB),
                                sig[:, c % 2, SEQ:T].rearrange("p (b t) -> p b t", b=NB),
                                ALU.mult).then_inc(S["u_done"], 1)

            ahead = (15, 6, 2)
            glu(0)
            for c in range(CT):
                dve.wait_ge(S["u_done"], 2 * (c + 1))
                cs = conv[:, c, SEQ:T].rearrange("p (b t) -> p b t", b=NB)
                for t in range(TAPS):
                    tap = cpar[:, c, t:t + 1]
                    out = bank[7][:, :] if t < TAPS - 1 else conv[:, c, 0:SEQ]
                    if t == 0:
                        if c:
                            dve.wait_ge(S["convp"], c * TAPS)
                        bias = cpar[:, c, TAPS:TAPS + 1]
                        V.tensor_scalar(out, uext[:, c, 0:SEQ], tap, bias, ALU.mult, ALU.add).then_inc(S["convp"], 1)
                        V.tensor_scalar(cs, sext[:, c, :, 0:NL], tap, bias, ALU.mult, ALU.add).then_inc(S["convs"], 1)
                    else:
                        dve.wait_ge(S["convp"], c * TAPS + t)
                        V.scalar_tensor_tensor(out, uext[:, c, t:t + SEQ], tap, bank[7][:, :], ALU.mult,
                                               ALU.add).then_inc(S["convp"], 1)
                        dve.wait_ge(S["convs"], c * TAPS + t)
                        V.scalar_tensor_tensor(cs, sext[:, c, :, t:t + NL], tap, cs, ALU.mult,
                                               ALU.add).then_inc(S["convs"], 1)
                    if c < CT - 1 and t == ahead[c]:
                        glu(c + 1)
            dve.wait_ge(S["convp"], CT * TAPS)
            dve.wait_ge(S["convs"], CT * TAPS)
            dve.wait_ge(S["mean_done"], 1)
            for c in range(CT):
                for b, cols in ((7, slice(0, SEQ)), (6, slice(SEQ, T))):
                    v = conv[:, c, cols]
                    V.scalar_tensor_tensor(v, bank[b][:, 0:v.shape[1]], -1.0 / CH, v, ALU.mult,
                                           ALU.add).then_inc(S["cmean"], 1)
            dve.wait_ge(S["cstd"], 2)
            cst = squares[:, 0, :]
            then(V.reciprocal(cst, cst))
            V.tensor_tensor(conv, conv, bc(cst, 1, CT), ALU.mult).then_inc(S["crstd"], 1)

            for i in range(TT):
                r = rows(i)
                dve.wait_ge(S["qT_sb"], i + 1)
                if i == 0:
                    dve.wait_ge(S["rope_done"], 2 * TT)
                if i < TT - 1:
                    V.tensor_tensor(qTx[:, :, :], qTs[:, :, :],
                                    C("xi").rearrange("p (h t) -> p h t", h=NH), ALU.mult).then_inc(S["qTx_sb"], 1)
                    decay = C("decay").rearrange("p (h t) -> p h t", h=NH)
                else:
                    for h in range(NH):
                        m = V.tensor_tensor(qTx[:, h, 0:NS].rearrange("p (b t) -> p b t", b=NB),
                                            qTs[:, h, 0:NS].rearrange("p (b t) -> p b t", b=NB),
                                            bc(C("xi")[:, h * P:h * P + NL], 1, NB), ALU.mult)
                        if h == NH - 1:
                            m.then_inc(S["qTx_sb"], 1)
                    decay = C("decay_s", NS).rearrange("p (h t) -> p h t", h=NH)
                dve.wait_ge(S["s_done"], i + 1)
                V.tensor_tensor(Sm[0:r, :, 0:r], bank[4][0:r, :].rearrange("p (h t) -> p h t", h=NH)[:, :, 0:r],
                                decay, ALU.mult).then_inc(S["s_sb"], 1)
                dve.wait_ge(S["o_done"], i + 1)
                if i == 0:
                    V.tensor_copy(Rst[:, :, :], bank[6][:, :].rearrange("p (h e) -> p h e", h=NH)).then_inc(S["r_upd"], 1)
                elif i < TT - 1:
                    for h in range(NH):
                        V.scalar_tensor_tensor(Rst[:, h, :], Rst[:, h, :], float(np.exp(P * np.log(GAMMA[h]))),
                                               bank[6][:, h * HD:(h + 1) * HD], ALU.mult, ALU.add).then_inc(S["r_upd"], 1)
                for h in range(NH):
                    m = V.bn_stats(bns[0:r, h, :], bank[5][0:r, h * HD:(h + 1) * HD])
                then(m)
                for h in range(NH):
                    m = V.bn_aggr(mv[0:r, h, :], bns[0:r, h, :])
                then(m)
                V.tensor_scalar(mv[0:r, :, 1], mv[0:r, :, 1], EPS, None, ALU.add).then_inc(S["gn_var"], 1)
                dve.wait_ge(S["gn_rstd"], i + 1)
                for h in range(NH):
                    V.tensor_scalar(z[0:r, i, 0, h * HD:(h + 1) * HD], bank[5][0:r, h * HD:(h + 1) * HD],
                                    mv[0:r, h, 0:1], grs[0:r, h:h + 1], ALU.subtract, ALU.mult).then_inc(S["on_done"], 1)

            def v_masks(h):
                if h > 1:
                    dve.wait_ge(S["kvs_done"], 2 * h - 2)
                V.tensor_tensor(vmask[1], bc(z[0:NS, TT - 1, 2, h * HD:(h + 1) * HD], 1, NB),
                                bc(C("row8", NS), 2, HD), ALU.mult).then_inc(S["vm2_done"], 1)

            v_masks(1)
            for n in range(2 * NH):
                h, a = n // 2, n % 2
                if n == 4:
                    v_masks(3)
                dve.wait_ge(S["kvs_done"], n + 1)
                st = states[:, 4 * a:4 * a + 4, h, :]
                V.scalar_tensor_tensor(st, st, float(np.exp(NL * np.log(GAMMA[h]))),
                                       bank[(6, 4)[n % 2]][:, :].rearrange("p (b e) -> p b e", b=4), ALU.mult,
                                       ALU.add).then_inc(S["rs_upd"], 1)

            def x1(i, a=None):
                v = z[0:rows(i), i, 0:2, :]
                return v.rearrange("p a n -> p (a n)") if a is None else v[:, a, :]

            def ple(i, a=None):
                v = z[0:rows(i), i, 2:4, :]
                return v.rearrange("p a n -> p (a n)") if a is None else v[:, a, :]

            def norm2(i):
                r = rows(i)
                dve.wait_ge(S["x1_std"], i + 1)
                V.reciprocal(rst2[0:r, i:i + 1], rst2[0:r, i:i + 1]).then_inc(S["x1_rstd"], 1)
                dve.wait_ge(S["x1_rstd"], i + 1)
                if i == 0:
                    dve.wait_ge(S["gbc_in"], 16)
                if i == 2:
                    dve.wait_ge(S["rs_out"], 16)
                V.scalar_tensor_tensor(h2[i][0:r, :], x1(i), rst2[0:r, i:i + 1], gbc[0:r, :], ALU.mult,
                                       ALU.mult).then_inc(S["h2_done"], 1)

            def add_x(i):
                dve.wait_ge(x_back[i], 16)
                dve.wait_ge(S["wo_done"], i + 1)
                for a in range(2):
                    V.tensor_tensor(x1(i, a), pair(2 * (i % 2))[a][0:rows(i), :], x1(i, a), ALU.add).then_inc(S["x1_sum"], 1)

            def h2_out_high(i):
                dve.wait_ge(S["h2T_ps"], i + 1)
                V.tensor_copy(hT[:, 4:8, tok(i)],
                              bank[5][:, :].rearrange("p (k t) -> p k t", k=4)[:, :, 0:rows(i)]).then_inc(S["h2T_sb"], 1)

            add_x(0)
            for i in range(1, TT):
                add_x(i)
                norm2(i - 1)
                if i >= 2:
                    h2_out_high(i - 2)
            norm2(TT - 1)
            h2_out_high(TT - 2)
            h2_out_high(TT - 1)

            dve.wait_ge(S["wo_done"], TT)
            then(V.memset(logit, 0.0))
            V.memset(tabz, 0.0).then_inc(S["zeroed"], 1)
            V.memset(zero32, 0.0).then_inc(S["zeroed"], 1)
            dve.wait_ge(S["logit_done"], TT)
            dve.wait_ge(S["router_in"], 64)
            ps = bank[6][:, 0:TT * 36].rearrange("p (i n) -> p i n", i=TT)
            V.tensor_tensor(logit[:, 0:TT - 1, :], ps[:, 0:TT - 1, :], bc(rbias[:, :], 1, TT - 1), ALU.add).then_inc(S["logit_sb"], 1)
            V.tensor_tensor(logit[0:NS, TT - 1, :], ps[0:NS, TT - 1, :], rbias[0:NS, :], ALU.add).then_inc(S["logit_sb"], 1)
            dve.wait_ge(S["logit_sb"], 2)
            lg = logit[:, :, 0:NG]
            then(V.tensor_reduce(gmx, lg, AX.X, ALU.max))
            V.tensor_tensor(gexp, lg, bc(gmx, 2, NG), ALU.subtract).then_inc(S["logit_sb"], 1)

            def first_of(one, values, mx, tmp, n):
                then(V.tensor_tensor(one, values, bc(mx, 2, n), ALU.is_equal))
                then(V.tensor_tensor(tmp, one, bc(C("rev")[:, 0:n], 1, TT), ALU.mult))
                then(V.tensor_reduce(t1, tmp, AX.X, ALU.max))
                then(V.tensor_tensor(one, tmp, bc(t1, 2, n), ALU.is_equal))

            first_of(gone, lg, gmx, gval, NG)
            then(V.tensor_tensor(sel, logit[:, :, NG:].rearrange("p i (g e) -> p i g e", g=NG),
                                 bc(gone, 3, NEG), ALU.mult))
            then(V.tensor_reduce(el, sel.rearrange("p i g e -> p i e g"), AX.X, ALU.add))
            then(V.tensor_reduce(m1, el, AX.X, ALU.max))
            first_of(one1, el, m1, eval_, NEG)
            then(V.tensor_scalar(eval_, one1, -3.0e38, None, ALU.mult))
            then(V.tensor_tensor(el, el, eval_, ALU.add))
            then(V.tensor_reduce(m2, el, AX.X, ALU.max))
            V.tensor_tensor(e2, m2, m1, ALU.subtract).then_inc(S["logit_sb"], 1)
            first_of(one2, el, m2, eval_, NEG)
            for k, one in ((0, one1), (1, one2)):
                for i in range(TT):
                    m = V.tensor_tensor(M[k][:, i, :].rearrange("p (g e) -> p g e", g=NG), bc(gone[:, i, :], 2, NEG),
                                        bc(one[:, i, :], 1, NG), ALU.mult)
                then(m)
            V.tensor_tensor(both, M[0], M[1], ALU.add).then_inc(S["picks_done"], 1)
            dve.wait_ge(S["rank_done"], 1)
            then(V.memset(rank, 0.0))
            rp = bank[7][:, 0:(TT + 1) * NE].rearrange("p (i n) -> p i n", i=TT + 1)
            V.tensor_copy(rank[:, 0:TT - 1, :], rp[:, 0:TT - 1, :])
            V.tensor_copy(rank[0:NS, TT - 1, :], rp[0:NS, TT - 1, :])
            then(V.tensor_copy(rank[:, TT, :], rp[:, TT, :]))
            total = rank[:, TT, :]
            then(V.tensor_scalar(ov, total, float(SLOTS), None, ALU.is_gt))
            for n in range(2, DEEP):
                then(V.scalar_tensor_tensor(ov, total, float(SLOTS * n), ov, ALU.is_gt, ALU.add))
            then(V.tensor_tensor_scan(ovi, zero32, ov, 0.0, ALU.add, ALU.add))
            then(V.tensor_tensor(ovb, ovi, ov, ALU.subtract))
            then(V.tensor_tensor(ovw, ovb, C("expert"), ALU.subtract))
            then(V.tensor_scalar(ovw, ovw, float(NE - 1), None, ALU.add))
            rk = rank[:, 0:TT, :]
            then(V.tensor_scalar(flag, rk, float(SLOTS), None, ALU.is_ge))
            then(V.tensor_copy(deep, flag))
            for n in range(2, DEEP):
                then(V.scalar_tensor_tensor(deep, rk, float(SLOTS * n), deep, ALU.is_ge, ALU.add))
            then(V.tensor_tensor(blk, deep, bc(ovw, 1, TT), ALU.add))
            then(V.tensor_tensor(blk, blk, flag, ALU.mult))
            then(V.tensor_tensor(blk, blk, bc(C("expert"), 1, TT), ALU.add))
            then(V.scalar_tensor_tensor(lane, deep, -float(SLOTS), rk, ALU.mult, ALU.add))
            for k in range(2):
                for pos, what in ((posb, blk), (posl, lane)):
                    then(V.tensor_tensor(prod, what, M[k], ALU.mult))
                    then(V.tensor_reduce(pos[:, k, :], prod, AX.X, ALU.add))
            code = C("code").rearrange("p (i k) -> p i k", i=TT)
            for n in range(2 * TT):
                i, k = n // 2, n % 2
                V.tensor_scalar(laneone[:, n, :], C("lane"), posl[:, k, i:i + 1], None,
                                ALU.is_equal).then_inc(S["laneone_done"], 1)
                V.tensor_scalar(blockone[:, n, :], C("block"), posb[:, k, i:i + 1], code[:, i, k:k + 1],
                                ALU.is_equal, ALU.mult).then_inc(S["laneone_done"], 1)
            dve.wait_ge(S["table_done"], 2 * TT)
            V.tensor_copy(tabf, bank[5][:, 0:NBLK]).then_inc(S["table_sb"], 1)
            dve.wait_ge(S["table_sb"], 1)
            then(V.tensor_scalar(tabz, tabf, 0.0, float(1 << 20), ALU.is_equal, ALU.mult))
            then(V.scalar_tensor_tensor(tabf, tabf, -1.0, tabz, ALU.add, ALU.add))
            V.tensor_copy(codes[:, :], tabf).then_inc(S["idx_done"], 1)
            dve.wait_ge(S["idx_done"], 1)
            V.tensor_scalar(tokidx[:, :], codes[:, :], 1, None, ALU.arith_shift_right).then_inc(S["idx_done"], 1)
            jj = bc(C("ovj", 1), 2, NE)
            then(V.tensor_tensor(ovt[0:1, 0, :, :], bc(ovb[0:1, :], 1, NOV), jj, ALU.is_le))
            then(V.tensor_tensor(ovt[0:1, 1, :, :], bc(ovi[0:1, :], 1, NOV), jj, ALU.is_le))
            then(V.tensor_tensor(ovt[0:1, 0, :, :], ovt[0:1, 0, :, :], ovt[0:1, 1, :, :], ALU.subtract))
            then(V.tensor_tensor(ovt[0:1, 0, :, :], ovt[0:1, 0, :, :], bc(C("expert", 1), 1, NOV), ALU.mult))
            then(V.tensor_reduce(ovf[0:1, 0:NOV], ovt[0:1, 0, :, :], AX.X, ALU.add))
            then(V.tensor_copy(ovf[0:1, NOV:NOV + 1], ovi[0:1, NE - 1:NE]))
            V.tensor_copy(ovinfo[:, :], ovf[0:1, :]).then_inc(S["idx_done"], 1)

            dve.wait_ge(S["gexp_done"], 2)
            then(V.tensor_reduce(gsum, gexp, AX.X, ALU.add))
            then(V.tensor_scalar(t1, e2, 1.0, None, ALU.add))
            then(V.tensor_tensor(t1, t1, gsum, ALU.mult))
            then(V.reciprocal(gates[:, :, 0], t1))
            then(V.tensor_tensor(gates[:, :, 1], gates[:, :, 0], e2, ALU.mult))
            dve.wait_ge(S["ple_sq"], 2 * TT)
            V.tensor_tensor(rst3[:, :], ssq3[:, :, 0], ssq3[:, :, 1], ALU.add).then_inc(S["ple_var"], 1)

            def ple_rstd():
                dve.wait_ge(S["ple_std"], 1)
                then(V.reciprocal(rst3[:, :], rst3[:, :]))
                dve.wait_ge(S["pbc_in"], 16)

            def ple_norm(i):
                V.scalar_tensor_tensor(ple(i), ple(i), rst3[0:rows(i), i:i + 1], pbc[0:rows(i), :], ALU.mult,
                                       ALU.mult).then_inc(S["ple_sb"], 1)

            def xt_half(par):
                return XT[:, par, 4:8, :], bank[3][:, :].rearrange("p (k s) -> p k s", k=4)

            def x_out(i, q):
                i, par = 2 * i + q // 2, q % 2
                dve.wait_ge(S["xt_ps"], 2 * i + par + 1)
                V.tensor_copy(*xt_half(par)).then_inc(S["xt_sb"], 1)

            def hidden(i, q):
                i, par = 2 * i + q // 2, q % 2
                dve.wait_ge(S["sil_done"], 2 * i + par + 1)
                V.tensor_tensor(hid[:, par, :], bank[par][:, FF:2 * FF], gat[:, par, :], ALU.mult).then_inc(S["hid_done"], 1)

            def hid_out(i, q):
                i, par = 2 * i + q // 2, q % 2
                dve.wait_ge(S["hT_ps"], 2 * i + par + 1)
                V.tensor_copy(hidT[:, par, :, :], bank[4][:, 0:2 * P].rearrange("p (k s) -> p k s", k=2)).then_inc(S["hT_ev"], 1)

            def y_out(i, q):
                i, par = 2 * i + q // 2, q % 2
                dve.wait_ge(S["d_done"], 2 * i + par + 1)
                if isinstance(i, int):
                    if i == 0 and par == 0:
                        dve.wait_ge(S["rs_out"], 16)
                    if i:
                        dve.wait_ge(scattered[par], 16 * i)
                else:
                    dve.wait_ge(scattered[par], 16 * i)
                V.tensor_copy(yout[:, par, 512:1024], bank[6][:, :]).then_inc(S["y_ready"], 1)

            def step(i, q, first=False, last=False):
                hidden(i, q)
                if not last:
                    x_out(*after(i, q))
                if not first:
                    y_out(*before(i, q))
                hid_out(i, q)

            x_out(0, 0)
            step(0, 0, first=True)
            ple_rstd()
            for q in range(1, NX):
                step(0, q)
                ple_norm(q - 1)
            with dve.Fori(1, LOOPS - 1) as i:
                for q in range(NX):
                    step(i, q)
            for q in range(NX):
                step(LOOPS - 1, q, last=q == NX - 1)
                if q < 2:
                    ple_norm(NX - 1 + q)
            y_out(LOOPS - 1, NX - 1)

            dve.wait_ge(S["idx_done"], 3)
            n_ov = dve.value_load(ovinfo[0:1, NOV:NOV + 1], min_val=0, max_val=NOV)
            with dve.If(n_ov > 0):
                with dve.Fori(0, NOV) as j:
                    dve.wait_ge(S["ov_xt"], j + 1)
                    V.tensor_copy(*xt_half(0)).then_inc(S["ov_xtsb"], 1)
                    dve.wait_ge(S["ov_sil"], j + 1)
                    V.tensor_tensor(hid[:, 0, :], bank[0][:, FF:2 * FF], gat[:, 0, :], ALU.mult).then_inc(S["ov_hid"], 1)
                    dve.wait_ge(S["ov_hT"], j + 1)
                    V.tensor_copy(hidT[:, 0, :, :], bank[4][:, 0:2 * P].rearrange("p (k s) -> p k s", k=2)).then_inc(S["ov_hTsb"], 1)
                    dve.wait_ge(S["ov_d"], j + 1)
                    V.tensor_copy(yout[:, 0, 512:1024], bank[6][:, :]).then_inc(S["ov_y"], 1)
            dve.nop()

            def x2(i):
                r = rows(i)
                dve.wait_ge(moe_in[i % 2], 16 * (i // 2 + 1))
                y = yins[i % 2]
                V.scalar_tensor_tensor(x1(i), y[0:r, 0, :], gates[0:r, i, 0:1], x1(i), ALU.mult,
                                       ALU.add).then_inc(S["x2_order"], 1)
                dve.wait_ge(S["x2_order"], i + 1)
                V.scalar_tensor_tensor(x1(i), y[0:r, 1, :], gates[0:r, i, 1:2], x1(i), ALU.mult,
                                       ALU.add).then_inc(S["x2_done"], 1)
                dve.wait_ge(S["x2T_ps"], i + 1)
                V.tensor_copy(hT[:, 4:8, tok(i)], quads(i, 1)).then_inc(S["x2T_high"], 1)

            dve.wait_ge(S["ple_sb"], TT)

            def x3(i):
                r = rows(i)
                dve.wait_ge(S["sg_done"], 2 * (i + 1))
                if i >= 2:
                    dve.wait_ge(S["x3_sq"], i - 1)
                t = xt[0:r, i % 2, :]
                then(V.tensor_tensor(t, sg[0:r, i % 2, :], ple(i), ALU.mult))
                V.tensor_tensor(t, t, x1(i), ALU.add).then_inc(S["x3_done"], 1)

            def final(i):
                r = rows(i)
                dve.wait_ge(S["x3_std"], i + 1)
                V.reciprocal(rst4[0:r, i:i + 1], rst4[0:r, i:i + 1]).then_inc(S["x3_rstd"], 1)
                dve.wait_ge(S["x3_rstd"], i + 1)
                if i == 0:
                    dve.wait_ge(S["final_in"], 16)
                if i >= 2:
                    dve.wait_ge(y_stored[i % 2], 16 * (i // 2))
                V.scalar_tensor_tensor(yo[0:r, i % 2, :], xt[0:r, i % 2, :], rst4[0:r, i:i + 1], gbc[0:r, :],
                                       ALU.mult, ALU.mult).then_inc(S["out_done"], 1)

            x2(0)
            for i in range(TT + 2):
                if i + 1 < TT:
                    x2(i + 1)
                if 1 <= i <= TT:
                    x3(i - 1)
                if i >= 2:
                    final(i - 2)

        @block.scalar
        def _(act):
            A = nc.scalar
            act.dma_start(const[:, 0:P], consts_d[:, 0:P]).then_inc(S["ident_in"], 16)
            act.dma_start(cpar_rows[0:TAPS, :], conv_w[0]).then_inc(S["params_in"], 16)
            for n, v in enumerate((conv_b, conv_ln_g, conv_ln_b)):
                act.dma_start(cpar_rows[TAPS + n:TAPS + n + 1, :], v).then_inc(S["params_in"], 16)
            act.dma_start(g1c[:, :], norm1_g[0].rearrange("(p k) -> p k", k=KT)).then_inc(S["params_in"], 16)
            for a in range(2):
                act.dma_start(hist_rows[:, a, :], state_conv[0, 4 * a:4 * a + 4, :, :].rearrange("b t c -> (b t) c")
                              ).then_inc(S["hist_in"], 16)

            def scaled(i):
                r = rows(i)
                act.wait_ge(S["xrstd"], i + 1)
                if i >= 2:
                    act.wait_ge(S["xT_ps"], i - 1)
                A.activation(xn[0:r, i % 2, :], x_sb[0:r, i, :], ACT.Copy, scale=rst[0:r, i:i + 1]).then_inc(S["xn_done"], 1)

            act.wait_ge(S["zeroed"], 7)
            for i in range(TT):
                r = rows(i)
                act.wait_ge(x_in[i], 16)
                if i:
                    act.wait_ge(S["xsq"], i)
                A.activation(sq_out[0:r, :], x_sb[0:r, i, :], ACT.Square, accum_out=ssq[0:r, i:i + 1]).then_inc(S["xsq"], 1)
                act.wait_ge(S["xsq"], i + 1)
                A.activation(rst[0:r, i:i + 1], ssq[0:r, i:i + 1], ACT.Sqrt, bias=epsb[0:r, :],
                             scale=1.0 / D).then_inc(S["xstd"], 1)
                if i:
                    scaled(i - 1)
            scaled(TT - 1)
            for i in range(2):
                act.wait_ge(S["hist_T"], i + 1)
                A.activation(sext[:, :, 4 * i:4 * i + 4, 0:HIST],
                             bank[4 + i][:, 0:CT * 120].rearrange("p (c b t) -> p c b t", c=CT, b=4),
                             ACT.Copy).then_inc(S["hist_sb"], 1)
            act.wait_ge(S["xn_done"], TT)
            act.dma_start(states, state_ret[0].rearrange("b h d e -> d b h e")).then_inc(S["states_in"], 16)
            act.dma_start(conv_s[0, :, 0:HIST - NL, :], state_conv[0, :, NL:HIST, :]).then_inc(S["cs_copy"], 16)
            act.dma_start(wr[:, :, 0:NG], rg_w[0].rearrange("(p k) n -> p k n", k=KT)).then_inc(S["router_in"], 16)
            act.dma_start(wr[:, :, NG:], re_w[0].rearrange("(p k) n -> p k n", k=KT)).then_inc(S["router_in"], 16)
            act.dma_start(rbias[:, 0:NG], rg_b[0].partition_broadcast(P)).then_inc(S["router_in"], 16)
            act.dma_start(rbias[:, NG:], re_b[0].partition_broadcast(P)).then_inc(S["router_in"], 16)
            act.dma_start(gbc[:, :], norm2_g[0].partition_broadcast(P)).then_inc(S["gbc_in"], 16)

            for c in range(CT):
                act.wait_ge(S["ab_done"], c + 1)
                if c >= 2:
                    act.wait_ge(S["u_done"], 2 * (c - 1))
                A.activation(sig[:, c % 2, 0:SEQ], bank[3 + 2 * (c % 2)][:, :], ACT.Sigmoid).then_inc(S["sig_done"], 1)
                A.activation(sig[:, c % 2, SEQ:T], bank[(6, 1)[c % 2]][:, NS:2 * NS], ACT.Sigmoid).then_inc(S["sig_done"], 1)

            def z_out(n):
                j, i = n // TT, n % TT
                act.wait_ge(S["z_done"], n + 1)
                A.activation(z[0:rows(i), i, j, :], bank[3 * (n % 2)][0:rows(i), :],
                             ACT.Silu if j == 3 else ACT.Copy).then_inc(S["z_sb"], 1)

            for n in range(12):
                z_out(n)
            act.wait_ge(S["tail_T"], 1)
            A.activation(tails[0:HIST, 0, :], bank[4][0:HIST, :], ACT.Copy).then_inc(S["tail_sb"], 1)
            A.activation(tails[0:NS, 1, :], bank[5][0:NS, :], ACT.Copy).then_inc(S["tail_sb"], 1)
            act.wait_ge(S["cmean"], 2 * CT)
            A.activation(squares, conv, ACT.Square).then_inc(S["csq"], 1)
            act.wait_ge(S["tail_sb"], 2)
            act.dma_start(conv_p[0, 0], tails[0:HIST, 0, :]).then_inc(S["tail_out"], 16)
            for b in range(NB):
                act.dma_start(conv_s[0, b, HIST - NL:HIST, :], tails[b * NL:(b + 1) * NL, 1, :]).then_inc(S["tail_out"], 16)
            for n in range(12, 15):
                z_out(n)
            act.wait_ge(S["var_done"], 1)
            A.activation(squares[:, 0, 0:SEQ], bank[5][:, :], ACT.Sqrt, bias=epsb[:, :], scale=1.0 / CH).then_inc(S["cstd"], 1)
            A.activation(squares[:, 0, SEQ:T], bank[4][:, 0:NS], ACT.Sqrt, bias=epsb[:, :], scale=1.0 / CH).then_inc(S["cstd"], 1)

            def gated_out(i):
                r = rows(i)
                act.wait_ge(S["oT_done"], i + 1)
                if i == 0:
                    act.wait_ge(S["tail_out"], 16 * (1 + NB))
                A.activation(catT[:, 4:8, tok(i)], bank[7][:, :].rearrange("p (h t) -> p h t", h=NH)[:, :, 0:r],
                             ACT.Copy).then_inc(S["oT_sb"], 1)

            for i in range(TT):
                r = rows(i)
                act.wait_ge(S["qk_T"], i + 1)
                for t, b, done in ((kTs, 1, "kT_sb"), (qTs, 2, "qT_sb")):
                    A.activation(t[:, :, 0:r], bank[b][:, :].rearrange("p (h t) -> p h t", h=NH)[:, :, 0:r],
                                 ACT.Copy).then_inc(S[done], 1)
                z_out(15 + i)
                if i == 0:
                    act.wait_ge(S["crstd"], 1)
                    for c in range(CT):
                        A.activation(catT[:, c, :], conv[:, c, :], ACT.Silu, bias=cpar[:, c, TAPS + 2:TAPS + 3],
                                     scale=cpar[:, c, TAPS + 1:TAPS + 2]).then_inc(S["cdone"], 1)
                    act.wait_ge(S["cdone"], CT)
                    for n in range(TT):
                        act.dma_start(p_sb[0:rows(n), n, :], p_rows(n)).then_inc(S["p_in"], 16)
                if i >= 1:
                    gated_out(i - 1)
            act.wait_ge(S["r_upd"], 1 + NH * (TT - 2))
            act.dma_start(ret_p[0, 0].rearrange("h d e -> d h e"), Rst[:, :, :]).then_inc(S["rp_out"], 16)
            act.wait_ge(S["rs_upd"], 2 * NH)
            act.dma_start(pbc, ple_norm_g[0].partition_broadcast(P)).then_inc(S["pbc_in"], 16)
            act.dma_start(ret_s[0].rearrange("b h d e -> d b h e"), states).then_inc(S["rs_out"], 16)
            gated_out(TT - 1)

            def x1_sq(i):
                r = rows(i)
                act.wait_ge(S["x1_sum"], 2 * (i + 1))
                if i >= 1:
                    act.wait_ge(S["x1_sq"], i)
                A.activation(junk[0:r, :], z[0:r, i, 0:2, :].rearrange("p a n -> p (a n)"), ACT.Square,
                             accum_out=ssq2[0:r, i:i + 1]).then_inc(S["x1_sq"], 1)
                act.wait_ge(S["x1_sq"], i + 1)
                A.activation(rst2[0:r, i:i + 1], ssq2[0:r, i:i + 1], ACT.Sqrt, bias=epsb[0:r, :],
                             scale=1.0 / D).then_inc(S["x1_std"], 1)

            def h2_store(i):
                r = rows(i)
                act.wait_ge(S["h2_done"], i + 1)
                act.dma_start(h2_d[i * P:i * P + r, :], h2[i][0:r, :]).then_inc(S["h2_out"], 16)

            def h2_out_low(i):
                act.wait_ge(S["h2T_ps"], i + 1)
                A.activation(hT[:, 0:4, tok(i)], bank[4][:, :].rearrange("p (k t) -> p k t", k=4)[:, :, 0:rows(i)],
                             ACT.Copy).then_inc(S["h2T_sb"], 1)

            def pT_out(turn, tiles):
                act.wait_ge(S["pT_ps"], turn)
                for i in tiles:
                    A.activation(pT[:, :, tok(i)], bank[7][:, 256 * (i % 2):256 * (i % 2) + 256].rearrange(
                        "p (k t) -> p k t", k=2)[:, :, 0:rows(i)], ACT.Copy).then_inc(S["pT_sb"], 1)

            def ple_out(i):
                r = rows(i)
                act.wait_ge(S["ple_done"], i + 1)
                for a in range(2):
                    A.activation(z[0:r, i, 2 + a, :], pair(2 - 2 * (i % 2))[a][0:r, :], ACT.Copy).then_inc(S["ple_raw"], 1)
                    act.wait_ge(S["x1_sq"], TT)
                    act.wait_ge(S["ple_raw"], 2 * i + a + 1)
                    if 2 * i + a:
                        act.wait_ge(S["ple_sq"], 2 * i + a)
                    A.activation(junk[0:r, 0:512], z[0:r, i, 2 + a, :], ACT.Square,
                                 accum_out=ssq3[0:r, i, a:a + 1]).then_inc(S["ple_sq"], 1)

            x1_sq(0)
            pT_out(1, (0, 1))
            x1_sq(1)
            h2_store(0)
            pT_out(2, (2, 3))
            x1_sq(2)
            h2_store(1)
            h2_out_low(0)
            pT_out(3, (4,))
            x1_sq(3)
            h2_store(2)
            h2_out_low(1)
            x1_sq(4)
            h2_store(3)
            h2_out_low(2)
            ple_out(0)
            h2_store(4)
            h2_out_low(3)
            act.dma_start(gbc[:, :], final_norm_g.partition_broadcast(P)).then_inc(S["final_in"], 16)
            ple_out(1)
            h2_out_low(4)
            for i in range(2, TT):
                ple_out(i)
            act.wait_ge(S["logit_sb"], 3)
            A.activation(gexp, gexp, ACT.Exp).then_inc(S["gexp_done"], 1)
            act.wait_ge(S["logit_sb"], 4)
            A.activation(e2, e2, ACT.Exp).then_inc(S["gexp_done"], 1)
            act.wait_ge(S["ple_var"], 1)
            A.activation(rst3[:, :], rst3[:, :], ACT.Sqrt, bias=epsb[:, :], scale=1.0 / D).then_inc(S["ple_std"], 1)

            def xt_half(par):
                return XT[:, par, 0:4, :], bank[2][:, :].rearrange("p (k s) -> p k s", k=4)

            def x_out(i, q):
                i, par = 2 * i + q // 2, q % 2
                act.wait_ge(S["xt_ps"], 2 * i + par + 1)
                A.activation(*xt_half(par), ACT.Copy).then_inc(S["xt_sb"], 1)

            def silu(i, q):
                i, par = 2 * i + q // 2, q % 2
                act.wait_ge(S["gu_done"], 2 * i + par + 1)
                A.activation(gat[:, par, :], bank[par][:, 0:FF], ACT.Silu).then_inc(S["sil_done"], 1)

            def y_copy(i, q):
                i, par = 2 * i + q // 2, q % 2
                act.wait_ge(S["d_done"], 2 * i + par + 1)
                if isinstance(i, int):
                    if i == 0 and par == 0:
                        act.wait_ge(S["rs_out"], 16)
                    if i:
                        act.wait_ge(scattered[par], 16 * i)
                else:
                    act.wait_ge(scattered[par], 16 * i)
                A.activation(yout[:, par, 0:512], bank[5][:, :], ACT.Copy).then_inc(S["y_ready"], 1)

            def step(i, q, first=False, last=False):
                silu(i, q)
                if not last:
                    x_out(*after(i, q))
                if not first:
                    y_copy(*before(i, q))

            x_out(0, 0)
            step(0, 0, first=True)
            for q in range(1, NX):
                step(0, q)
            with act.Fori(1, LOOPS - 1) as i:
                for q in range(NX):
                    step(i, q)
            for q in range(NX):
                step(LOOPS - 1, q, last=q == NX - 1)
            y_copy(LOOPS - 1, NX - 1)

            act.wait_ge(S["idx_done"], 3)
            n_ov = act.value_load(ovinfo[0:1, NOV:NOV + 1], min_val=0, max_val=NOV)
            with act.If(n_ov > 0):
                with act.Fori(0, NOV) as j:
                    act.wait_ge(S["ov_xt"], j + 1)
                    A.activation(*xt_half(0), ACT.Copy).then_inc(S["ov_xtsb"], 1)
                    act.wait_ge(S["ov_gu"], j + 1)
                    A.activation(gat[:, 0, :], bank[0][:, 0:FF], ACT.Silu).then_inc(S["ov_sil"], 1)
                    act.wait_ge(S["ov_d"], j + 1)
                    A.activation(yout[:, 0, 0:512], bank[5][:, :], ACT.Copy).then_inc(S["ov_y"], 1)
            act.nop()

            act.wait_ge(S["moe_out"], 1)
            moe2 = moe_d.rearrange("(t k) d -> t k d", k=2)
            for i in range(2):
                act.dma_start(yins[i], moe2[i * P:(i + 1) * P, :, :]).then_inc(moe_in[i], 16)
            for i in range(TT + 1):
                if i < TT:
                    r = rows(i)
                    act.wait_ge(S["x2T_ps"], i + 1)
                    A.activation(hT[:, 0:4, tok(i)],
                                 bank[2 * (i % 2)][:, :].rearrange("p (k t) -> p k t", k=4)[:, :, 0:r],
                                 ACT.Copy).then_inc(S["x2T_low"], 1)
                    if i + 2 < TT:
                        n = i + 2
                        act.wait_ge(S["x2_done"], i + 1)
                        act.dma_start(yins[i % 2][0:rows(n), :, :],
                                      moe2[n * P:n * P + rows(n), :, :]).then_inc(moe_in[i % 2], 16)
                if i >= 1:
                    t = i - 1
                    r = rows(t)
                    act.wait_ge(S["pg_done"], t + 1)
                    if t >= 2:
                        act.wait_ge(S["x3_done"], t - 1)
                    for a in range(2):
                        A.activation(sg[0:r, t % 2, a * 512:(a + 1) * 512], pair(4 + 2 * (t % 2))[a][0:r, :],
                                     ACT.Sigmoid).then_inc(S["sg_done"], 1)
                    act.wait_ge(S["x3_done"], t + 1)
                    if t >= 1:
                        act.wait_ge(S["x3_sq"], t)
                    A.activation(junk[0:r, :], xt[0:r, t % 2, :], ACT.Square,
                                 accum_out=ssq4[0:r, t:t + 1]).then_inc(S["x3_sq"], 1)
                    act.wait_ge(S["x3_sq"], t + 1)
                    A.activation(rst4[0:r, t:t + 1], ssq4[0:r, t:t + 1], ACT.Sqrt, bias=epsb[0:r, :],
                                 scale=1.0 / D).then_inc(S["x3_std"], 1)
                    if t >= 1:
                        act.wait_ge(S["out_done"], t)
                        act.dma_start(y_rows(t - 1), yo[0:rows(t - 1), (t - 1) % 2, :]).then_inc(y_stored[(t - 1) % 2], 16)
            act.wait_ge(S["out_done"], TT)
            act.dma_start(y_rows(TT - 1), yo[0:NS, (TT - 1) % 2, :]).then_inc(y_stored[0], 16)
            act.wait_ge(y_stored[0], 48)
            act.wait_ge(y_stored[1], 32)
            act.wait_ge(S["tail_out"], 16 * (1 + NB))
            act.wait_ge(S["cs_copy"], 16)
            act.wait_ge(S["rp_out"], 16)
            act.wait_ge(S["rs_out"], 16)

        @block.gpsimd
        def _(pool):
            G = nc.gpsimd
            order = [0]

            def then(ins):
                order[0] += 1
                ins.then_inc(S["pool_order"], 1)
                pool.wait_ge(S["pool_order"], order[0])

            G.memset(uext[:, :, 0:HIST], 0.0).then_inc(S["zero_x"], 1)
            pool.wait_ge(S["const_in"], 16)
            ta = Sm[:, :, :]
            tb = qTx[:, :, :]
            for j in range(2):
                for i in range(TT):
                    r = rows(i)
                    pool.wait_ge(S["z_sb"], j * TT + i + 1)
                    v = z[0:r, i, j, :].rearrange("p (h a n) -> p h a n", h=NH, a=2)
                    aa = ta[0:r].rearrange("p h (a n) -> p h a n", a=2)
                    bb = tb[0:r].rearrange("p h (a n) -> p h a n", a=2)
                    cos = bc(bc(rope_t[0:r, i, 0, :], 1, 2), 1, NH)
                    sin = bc(bc(rope_t[0:r, i, 1, :], 1, 2), 1, NH)
                    then(G.tensor_tensor(aa, v, cos, ALU.mult))
                    then(G.tensor_tensor(bb, v, sin, ALU.mult))
                    then(G.tensor_tensor(v[:, :, 0, :], aa[:, :, 0, :], bb[:, :, 1, :], ALU.subtract))
                    G.tensor_tensor(v[:, :, 1, :], bb[:, :, 0, :], aa[:, :, 1, :], ALU.add).then_inc(S["rope_done"], 1)
                    pool.wait_ge(S["rope_done"], j * TT + i + 1)
                if j == 0:
                    pool.wait_ge(S["u_done"], 2 * CT)
                    for c in range(CT):
                        G.tensor_copy(kTs[:, c, 0:NS].rearrange("p (b t) -> p b t", b=NB),
                                      sext[:, c, :, HIST:HIST + NL]).then_inc(S["tail_u"], 1)

            def k_decay(i):
                r = rows(i)
                if i:
                    pool.wait_ge(S["o_done"], i)
                zeta = C("zeta" if i < TT - 1 else "zeta_s", r)
                G.tensor_tensor(kz[0:r, :].rearrange("p (h d) -> p h d", h=NH),
                                z[0:r, i, 1, :].rearrange("p (h d) -> p h d", h=NH), bc(zeta, 2, HD),
                                ALU.mult).then_inc(S["kz_done"], 1)

            def v_masks(h):
                if h:
                    pool.wait_ge(S["kvs_done"], 2 * h - 2)
                G.tensor_tensor(vmask[0], bc(z[0:NS, TT - 1, 2, h * HD:(h + 1) * HD], 1, NB),
                                bc(C("row8", NS), 2, HD), ALU.mult).then_inc(S["vm_done"], 1)

            k_decay(0)
            for i in range(TT):
                r = rows(i)
                if i == TT - 1:
                    pool.wait_ge(S["qTx_sb"], TT)
                    eye = C("eye8").rearrange("p (b c) -> p b c", b=NB)
                    for h in range(NH):
                        G.tensor_tensor(qmask[:, h, :, :].rearrange("p b (c t) -> p b c t", c=NB),
                                        bc(qTx[:, h, 0:NS].rearrange("p (c t) -> p c t", c=NB), 1, NB),
                                        bc(eye, 3, NL), ALU.mult).then_inc(S["qm_done"], 1)
                if i == 1:
                    v_masks(0)
                pool.wait_ge(S["gn_var"], i + 1)
                G.tensor_tensor(grs[0:r, :], mv[0:r, :, 1], half[0:r, :], ALU.pow).then_inc(S["gn_rstd"], 1)
                if i < TT - 1:
                    k_decay(i + 1)
                pool.wait_ge(S["on_done"], NH * (i + 1))
                pool.wait_ge(S["z_sb"], 16 + i)
                G.tensor_tensor(z[0:r, i, 3, :], z[0:r, i, 3, :], z[0:r, i, 0, :], ALU.mult).then_inc(S["og_done"], 1)
            v_masks(2)

            pool.wait_ge(S["idx_done"], 2)
            pool.wait_ge(S["h2_out"], 16 * TT)
            pool.wait_ge(S["h2T_ps"], TT)

            def wait(on, value):
                pool.wait_ge(on, value)
                pool.sem_inc(S["ticks"], 1)

            def column(dst, src, n, done, count):
                G.tensor_copy(dst, src[:, bass.ds(n, 1)]).then_inc(done, 1)
                wait(done, count)

            def gather(i, q):
                if not (isinstance(i, int) and i == 0):
                    wait(S["xt_ps"], NX * i + q - (NX - 1))
                column(cur_tok[:, q:q + 1], tokidx, NX * i + q, S["cur_done"], NX * i + q + 1)
                G.indirect_dma_start(X[q], None, h2_d, bass.IndirectOffsetOnAxis(ap=cur_tok[:, q:q + 1], axis=0),
                                     bounds_check=T - 1, oob_is_err=False).then_inc(gathered[q], 16)

            def scatter(i, q):
                i, par = 2 * i + q // 2, q % 2
                if not (isinstance(i, int) and i == 0):
                    wait(scattered[par], 16 * i)
                column(cur_code[:, par:par + 1], codes, 2 * i + par, S["pool_codes"], 2 * i + par + 1)
                wait(S["y_ready"], 2 * (2 * i + par) + 2)
                G.indirect_dma_start(moe_d, bass.IndirectOffsetOnAxis(ap=cur_code[:, par:par + 1], axis=0),
                                     yout[:, par, :], None, bounds_check=2 * T - 1,
                                     oob_is_err=False).then_inc(scattered[par], 16)

            wait(S["rs_out"], 16)
            for q in range(NX):
                gather(0, q)
            for q in range(NX):
                gather(1, q)
                scatter(0, q)
            with pool.Fori(1, LOOPS - 1) as i:
                for q in range(NX):
                    gather(i + 1, q)
                    scatter(i, q)
            for q in range(NX):
                scatter(LOOPS - 1, q)

            pool.wait_ge(scattered[0], 8 * NE)
            pool.wait_ge(scattered[1], 8 * NE)
            pool.sem_inc(S["ov_end"], 1)
            pool.wait_ge(S["idx_done"], 3)
            n_ov = pool.value_load(ovinfo[0:1, NOV:NOV + 1], min_val=0, max_val=NOV)
            with pool.If(n_ov > 0):
                with pool.Fori(0, NOV) as j:
                    G.tensor_copy(cur_tok[:, 0:1], tokidx[:, bass.ds(j + NE, 1)]).then_inc(S["ov_cur"], 1)
                    G.tensor_copy(cur_code[:, 0:1], codes[:, bass.ds(j + NE, 1)]).then_inc(S["ov_cur"], 1)
                    wait(S["ov_cur"], 2 * j + 2)
                    G.indirect_dma_start(X[0], None, h2_d, bass.IndirectOffsetOnAxis(ap=cur_tok[:, 0:1], axis=0),
                                         bounds_check=T - 1, oob_is_err=False).then_inc(S["ov_gather"], 16)
                    wait(S["ov_y"], 2 * j + 2)
                    G.indirect_dma_start(moe_d, bass.IndirectOffsetOnAxis(ap=cur_code[:, 0:1], axis=0),
                                         yout[:, 0, :], None, bounds_check=2 * T - 1,
                                         oob_is_err=False).then_inc(S["ov_out"], 16)
                    wait(S["ov_out"], 16 * j + 16)
                    pool.sem_inc(S["ov_end"], 1)
            pool.nop()
            pool.sem_inc(S["moe_out"], 1)


_INS = ["x_prompt", "x_sample", "p_prompt", "p_sample", "state_conv", "state_ret", "w_in", "conv_w", "conv_b",
        "conv_ln_g", "conv_ln_b", "w_out", "norm1_g", "norm2_g", "router_group_w", "router_group_b",
        "router_expert_w", "router_expert_b", "w_expert_gate", "w_expert_up", "w_expert_down", "w_ple",
        "ple_norm_g", "w_ple_gate", "final_norm_g"]
_OUTS = [(1, SEQ, D), (NB, NL, D), (1, 1, HIST, CH), (1, 1, NH, HD, HD), (1, NB, HIST, CH), (1, NB, NH, HD, HD)]


def kernel(**inputs):
    import concourse.bacc as _bacc
    from concourse.bass_utils import run_bass_kernel_spmd as _run

    nc = _bacc.Bacc("TRN2", target_bir_lowering=False, num_devices=1)
    arrays, args = {}, []
    for name in _INS:
        a = np.ascontiguousarray(inputs[name])
        arrays[f"in_{name}"] = a
        args.append(nc.dram_tensor(f"in_{name}", a.shape, mybir.dt.from_np(a.dtype), kind="ExternalInput").ap())
    arrays["constants"] = constants()
    args.append(nc.dram_tensor("constants", (P, NCONST), F32, kind="ExternalInput").ap())
    outs = [nc.dram_tensor(f"out_{i}", shape, F32, kind="ExternalOutput").ap() for i, shape in enumerate(_OUTS)]
    build(nc, args, outs)
    r = _run(nc, [arrays], core_ids=[0])
    return tuple(r.results[0][f"out_{i}"] for i in range(len(_OUTS)))
```

```python
from contextlib import ExitStack

import numpy as np

import concourse.bass as bass
from concourse import mybir

F32 = mybir.dt.float32
F32R = mybir.dt.float32r
I32 = mybir.dt.int32
ALU = mybir.AluOpType
ACT = mybir.ActivationFunctionType
AX = mybir.AxisListType

P = 128
D = 1024
KT = D // P
SEQ = 512
NB, NL = 8, 8
NS = NB * NL
T = SEQ + NS
TT = 5
CH, CT = 512, 4
TAPS = 31
HIST = TAPS - 1
NH, HD = 4, 128
PLE = 256
NG, NEG = 4, 8
NE = NG * NEG
FF = 256
EPS = 1e-6
SLOTS = 128
HALF = SLOTS // 2
DEEP = -(-T // SLOTS)
NOV = (2 * T - NE) // SLOTS if SLOTS < 128 else 8
NBLK = NE + NOV
RING = 6
NX = 4
LOOPS = NE // NX
CHUNK = 2048
GAMMA = [1.0 - 2.0 ** (-5.0 - h) for h in range(NH)]

COLS = {}
_at = 0
for _name, _n in (("ident", P), ("ones", P), ("before", P), ("decay", NH * P), ("xi", NH * P), ("zeta", NH),
                  ("decay_s", NH * NS), ("zeta_s", NH), ("eye8", NB * NB), ("row8", NB), ("rope", TT * 2 * 64),
                  ("lane", P), ("block", NBLK), ("expert", NE), ("code", TT * 2), ("rev", NEG), ("ovj", NOV)):
    COLS[_name] = (_at, _n)
    _at += _n
NCONST = _at


def rows(i):
    return P if i < TT - 1 else NS


def constants():
    c = np.zeros((P, NCONST), np.float64)

    def put(name, value):
        a, n = COLS[name]
        v = np.asarray(value, np.float64)
        c[: v.shape[0], a:a + n] = v.reshape(v.shape[0], n)

    lg = np.array([np.log(g) for g in GAMMA])
    p = np.arange(P)
    put("ident", np.eye(P))
    put("ones", np.ones((P, P)))
    put("before", p[:, None] < p[None, :])
    scale = HD ** -0.5
    rel = p[None, :] - p[:, None]
    put("decay", np.stack([np.where(rel >= 0, np.exp(np.maximum(rel, 0) * g), 0.0) * scale for g in lg], 1))
    put("xi", np.broadcast_to(np.stack([np.exp((p + 1) * g) for g in lg])[None], (P, NH, P)))
    put("zeta", np.stack([np.exp((P - 1 - p) * g) * scale for g in lg], 1))
    s = np.arange(NS)
    rs = s[None, :] - s[:, None]
    same = (s[None, :] // NL == s[:, None] // NL) & (rs >= 0)
    put("decay_s", np.stack([np.where(same, np.exp(np.maximum(rs, 0) * g), 0.0) * scale for g in lg], 1))
    put("zeta_s", np.stack([np.exp((NL - 1 - s % NL) * g) * scale for g in lg], 1))
    put("eye8", np.broadcast_to(np.eye(NB).reshape(1, -1), (P, NB * NB)))
    put("row8", (s[:, None] // NL == np.arange(NB)[None, :]))
    inv = (10000.0 ** (-np.arange(64, dtype=np.float64) / 64)).astype(np.float32)
    pos = np.zeros((P, TT), np.float32)
    for i in range(TT - 1):
        pos[:, i] = i * P + p
    pos[:NS, TT - 1] = 4096 + s % NL
    ang = (pos[:, :, None] * inv[None, None, :]).astype(np.float64)
    put("rope", np.stack([np.cos(ang), np.sin(ang)], 2))
    put("lane", np.broadcast_to(p[None].astype(float), (P, P)))
    put("block", np.broadcast_to(np.arange(NBLK)[None].astype(float), (P, NBLK)))
    put("expert", np.broadcast_to(np.arange(NE)[None].astype(float), (P, NE)))
    tok = np.arange(TT)[None, :] * P + p[:, None]
    put("code", np.stack([2 * tok + 1, 2 * tok + 2], 2))
    put("rev", np.broadcast_to((NEG - np.arange(NEG))[None].astype(float), (P, NEG)))
    put("ovj", np.broadcast_to(np.arange(NOV)[None].astype(float), (P, NOV)))
    return c.astype(np.float32)


def bc(ap, axis, n):
    a = ap.unsqueeze(axis)
    shape = list(a.shape)
    shape[axis] = n
    return a.to_broadcast(shape)


def build(nc, ins, outs):
    (x_prompt, x_sample, p_prompt, p_sample, state_conv, state_ret, w_in, conv_w, conv_b, conv_ln_g, conv_ln_b,
     w_out, norm1_g, norm2_g, rg_w, rg_b, re_w, re_b, w_gate, w_up, w_down, w_ple, ple_norm_g, w_ple_gate,
     final_norm_g, consts_d) = ins
    y_prompt, y_sample, conv_p, ret_p, conv_s, ret_s = outs
    h2_d = nc.dram_tensor("h2_rows", (T, D), F32, kind="Internal").ap()
    moe_d = nc.dram_tensor("expert_rows", (2 * T, D), F32, kind="Internal").ap()
    moe2 = moe_d.rearrange("(t k) d -> t k d", k=2)

    with ExitStack() as ctx:
        def sb(name, shape, dt=F32):
            return ctx.enter_context(nc.sbuf_tensor(name, shape, dt))

        def sem(name):
            return ctx.enter_context(nc.semaphore(name))

        def place(name, shape):
            with nc.sbuf_tensor(name, shape, F32R) as t:
                return t

        ring_r = place("ring_parts", [P, RING, CHUNK])
        ring = sb("ring", [P, RING, CHUNK])
        const = sb("const", [P, NCONST])
        h_hi = place("hT_high", [P, KT, T])
        hT = sb("hT", [P, KT, T])
        h_lo = place("hT_low", [P, TT, KT, P])
        front = sb("front", [P, TT * D])
        conv_hi = place("conv_high", [P, CT, T])
        scratch = sb("scratch", [P, CT * T])
        z = sb("z", [P, TT, 4, 512])
        uext = sb("uext", [P, CT, HIST + SEQ])
        sext = sb("sext", [P, CT, NB, HIST + NL])
        cv_r = place("cv_parts", [P, CHUNK])
        cv = sb("cv", [P, CT * T])
        cat_r = place("catT_parts", [P, KT * T])
        catT = sb("catT", [P, KT, T])
        x2_lo = place("x2T_low_parts", [P, 2, KT, P])
        kz = sb("kz", [P, 512])
        Rst = sb("Rst", [P, NH, HD])
        qTs = sb("qTs", [P, NH, P])
        qTx = sb("qTx", [P, NH, P])
        kTs = sb("kTs", [P, NH, P])
        Sm = sb("Sm", [P, NH, P])
        gbc = sb("gbc", [P, D])
        cpar = sb("cpar", [P, CT, TAPS + 3])
        ssq = sb("ssq", [P, TT])
        rst = sb("rst", [P, TT])
        ssq2 = sb("ssq2", [P, TT])
        rst2 = sb("rst2", [P, TT])
        ssq3 = sb("ssq3", [P, TT, 2])
        rst3 = sb("rst3", [P, TT])
        ssq4 = sb("ssq4", [P, TT, 2])
        rst4 = sb("rst4", [P, TT])
        bns = sb("bns", [P, NH, 6])
        mv = sb("mv", [P, NH, 2])
        grs = sb("grs", [P, NH])
        half = sb("half", [P, NH])
        epsb = sb("epsb", [P, 1])
        tokidx = sb("tokidx", [P, NBLK], I32)
        codes = sb("codes", [P, NBLK], I32)
        cur_tok = sb("cur_tok", [P, NX], I32)
        cur_code = sb("cur_code", [P, 2], I32)
        ovinfo = sb("ovinfo", [1, NOV + 1 + NE], I32)
        gates = sb("gates", [P, TT, 2])
        wr = sb("wr", [P, KT, NG + NE])
        rbias = sb("rbias", [P, NG + NE])

        def view(t, off, dims):
            n = int(np.prod(dims))
            flat = t[:, off:off + n]
            if len(dims) == 1:
                return flat
            names = "abcd"[: len(dims)]
            return flat.rearrange("p (" + " ".join(names) + ") -> p " + " ".join(names),
                                  **{k: v for k, v in zip(names[1:], dims[1:])})

        flat_cat = catT[:, :, :].rearrange("p k t -> p (k t)")
        flat_u = uext[:, :, :].rearrange("p c t -> p (c t)")
        flat_s = sext[:, :, :, :].rearrange("p c b t -> p (c b t)")
        flat_z = z[:, :, :, :].rearrange("p i j n -> p (i j n)")
        flat_h = hT[:, :, :].rearrange("p k t -> p (k t)")
        x_sb = view(front, 0, (TT, D))
        states = view(front, 0, (NB, NH, HD))
        xn = view(scratch, 0, (2, D))
        h2 = [front[:, n * D:(n + 1) * D] for n in range(4)] + [xn[:, 0, :]]
        squares = view(scratch, 0, (CT, T))
        conv = view(cv, 0, (CT, T))
        p_sb = view(cv, 0, (TT, PLE))
        cpar_rows = flat_z[0:TAPS + 3, 0:CH]
        sq_out = flat_z[:, 4096:4096 + D]
        hist_rows = flat_z[0:120, CH:3 * CH].rearrange("p (a c) -> p a c", a=2)
        sig = flat_cat[:, 0:2 * T].rearrange("p (a t) -> p a t", a=2)
        tails = flat_cat[:, 4 * T:4 * T + 2 * CH].rearrange("p (a c) -> p a c", a=2)
        qmask = flat_u[:, 0:NH * NB * NS].rearrange("p (h b t) -> p h b t", h=NH, b=NB)
        vmask = [t.rearrange("p (b e) -> p b e", b=NB) for t in (flat_s[0:NS, 0:NB * HD], cv[0:NS, 5 * PLE:5 * PLE + NB * HD])]
        pT = flat_u[:, 0:2 * T].rearrange("p (k t) -> p k t", k=2)
        pbc = flat_s[:, 0:D]
        rt = [0]

        def work(n):
            rt[0] += n
            return flat_cat[:, rt[0] - n:rt[0]]

        logit = work(TT * 36).rearrange("p (i n) -> p i n", i=TT)
        gmx, gsum, m1, m2, e2, t1 = (work(TT) for _ in range(6))
        gexp = work(TT * NG).rearrange("p (i n) -> p i n", i=TT)
        gval = work(TT * NG).rearrange("p (i n) -> p i n", i=TT)
        gone = work(TT * NG).rearrange("p (i n) -> p i n", i=TT)
        sel = work(TT * NE).rearrange("p (i g e) -> p i g e", i=TT, g=NG)
        el = work(TT * NEG).rearrange("p (i n) -> p i n", i=TT)
        eval_ = work(TT * NEG).rearrange("p (i n) -> p i n", i=TT)
        one1 = work(TT * NEG).rearrange("p (i n) -> p i n", i=TT)
        one2 = work(TT * NEG).rearrange("p (i n) -> p i n", i=TT)
        M = [work(TT * NE).rearrange("p (i n) -> p i n", i=TT) for _ in range(2)]
        both = work(TT * NE).rearrange("p (i n) -> p i n", i=TT)
        rank = work((TT + 1) * NE).rearrange("p (i n) -> p i n", i=TT + 1)
        deep = work(TT * NE).rearrange("p (i n) -> p i n", i=TT)
        flag = work(TT * NE).rearrange("p (i n) -> p i n", i=TT)
        blk = work(TT * NE).rearrange("p (i n) -> p i n", i=TT)
        lane = work(TT * NE).rearrange("p (i n) -> p i n", i=TT)
        prod = work(TT * NE).rearrange("p (i n) -> p i n", i=TT)
        ov = work(NE)
        ovi = work(NE)
        ovb = work(NE)
        ovw = work(NE)
        zero32 = work(NE)
        posb = work(2 * TT).rearrange("p (a i) -> p a i", a=2)
        posl = work(2 * TT).rearrange("p (a i) -> p a i", a=2)
        laneone = flat_h[:, 2 * D:2 * D + 2 * TT * P].rearrange("p (a n) -> p a n", a=2 * TT)
        blockone = flat_h[:, 2 * D + 2 * TT * P:2 * D + 2 * TT * (P + NBLK)].rearrange("p (a n) -> p a n", a=2 * TT)
        tabf = work(NBLK)
        tabz = work(NBLK)
        ovt = work(2 * NOV * NE).rearrange("p (a j e) -> p a j e", a=2, j=NOV)
        ovf = work(NOV + 1)
        assert rt[0] <= KT * T, rt[0]
        junk = view(front, 4 * D, (D,))
        X = [xn[:, 0, :], xn[:, 1, :], front[:, 2 * D:3 * D], front[:, 3 * D:4 * D]]
        XT = flat_h[:, 0:2 * D].rearrange("p (a k s) -> p a k s", a=2, k=KT)
        cat_lo = cat_r[:, :].rearrange("p (k t) -> p k t", k=KT)
        flat_hi = h_hi[:, :, :].rearrange("p k t -> p (k t)")
        XT_hi, XT_lo = (flat_hi[:, n * 2 * D:(n + 1) * 2 * D].rearrange("p (a k s) -> p a k s", a=2, k=KT) for n in range(2))
        hid = view(cv, 0, (2, FF))
        gat = view(cv, 2 * FF, (2, FF))
        hidT = view(cv, 4 * FF, (2, 2, P))
        yout = view(front, 0, (2, D))
        yin = flat_u[:, 0:2 * D].rearrange("p (a n) -> p a n", a=2)
        yin2 = flat_cat[:, 0:2 * D].rearrange("p (a n) -> p a n", a=2)
        yins = [yin, yin2]
        sg = view(scratch, 0, (2, D))
        yo = view(front, 0, (2, D))
        xt = view(front, 2 * D, (2, D))

        def C(name, r=P):
            a, n = COLS[name]
            return const[0:r, a:a + n]

        ident = C("ident")
        rope_t = C("rope").rearrange("p (i c n) -> p i c n", i=TT, c=2)

        bank = [ctx.enter_context(nc.psum_tensor(f"bank{i}", [P, 512], F32)) for i in range(8)]

        def pair(b):
            return [bank[b], bank[b + 1]]

        names = """const_in ident_in params_in hist_in states_in router_in gbc_in final_in pbc_in p_in cpar_T
            hist_T xT_ps ab_done mean_done var_done z_done qk_T s_done o_done kvs_done oT_done tail_T
            wo_done pT_ps ple_done h2T_ps logit_done rank_done table_done gu_done xt_ps hT_ps d_done cpar_sb
            hist_sb hT_sb u_done sig_done convp convs cmean csq cstd crstd cdone z_sb rope_done qT_sb qTx_sb
            kT_sb s_sb kz_done gn_var gn_rstd on_done og_done oT_sb r_upd tail_u tail_sb tail_out qm_done
            vm_done vm2_done rs_upd rs_out rp_out x1_sum x1_sq x1_std h2_done h2T_sb xsq xstd
            xn_done zeroed dve_order pool_order pT_sb ple_sq ple_var ple_std ple_sb logit_sb gexp_done
            picks_done laneone_done table_sb idx_done xt_sb sil_done hid_done hT_ev y_ready zero_x cur_done
            pool_codes ticks moe_out ov_load ov_gather ov_cur ov_xt ov_xtsb ov_gu ov_sil ov_hid ov_hT
            ov_hTsb ov_d ov_y ov_out ov_end x2_done x2T_ps x2T_low x2T_high pg_done sg_done x3_done x3_sq
            x3_rstd out_done cs_copy h2_out ple_raw w_hi w_lo hlo_sb""".split()
        S = {n: sem(n) for n in names}
        x_in = [sem(f"x_in{i}") for i in range(TT)]
        x_back = [sem(f"x_back{i}") for i in range(TT)]
        slot_in = [sem(f"slot_in{i}") for i in range(RING)]
        y_stored = [sem(f"y_stored{i}") for i in range(2)]
        gathered = [sem(f"gathered{i}") for i in range(NX)]
        scattered = [sem(f"scattered{i}") for i in range(2)]
        moe_in = [sem(f"moe_in{i}") for i in range(2)]
        block = ctx.enter_context(nc.Block())

        def before(i, q):
            return (i, q - 1) if q else (i - 1, NX - 1)

        def after(i, q):
            return (i, q + 1) if q < NX - 1 else (i + 1, 0)

        def x_rows(i):
            return x_prompt[0, i * P:(i + 1) * P, :] if i < TT - 1 else x_sample.rearrange("b t d -> (b t) d")

        def p_rows(i):
            return p_prompt[0, 0, i * P:(i + 1) * P, :] if i < TT - 1 else p_sample[0].rearrange("b t d -> (b t) d")

        def y_rows(i):
            return y_prompt[0, i * P:(i + 1) * P, :] if i < TT - 1 else y_sample.rearrange("b t d -> (b t) d")

        def tok(i):
            return slice(i * P, i * P + rows(i))

        def w_cols(w, n):
            return w.rearrange("(p k) n -> p k n", k=KT)[:, :, n * 256:(n + 1) * 256]

        def w_cols_k(w, n):
            return w.rearrange("(k p) n -> p k n", p=P)[:, :, n * 256:(n + 1) * 256]

        def slot8(s):
            return ring[:, s, :].rearrange("p (k n) -> p k n", k=KT)

        def slots8(s):
            return ring[:, s:s + 2, :].rearrange("p a (k n) -> p k a n", k=KT)

        def slot2(s):
            return ring[:, s, :].rearrange("p (k n) -> p k n", k=2)

        def gate_rows(e):
            return w_gate[0, e, :, :].rearrange("(p k) f -> p (k f)", k=KT)

        def quads(i, a):
            return bank[2 * (i % 2) + a][:, :].rearrange("p (k t) -> p k t", k=4)[:, :, 0:rows(i)]

        WO = [(c, i) for c in (12, 13) for i in range(TT - 1)] + [(12, TT - 1), (13, TT - 1)]
        WO += [(c, i) for c in (14, 15) for i in range(TT)]
        LOWS = 2 * TT + 1

        def used(c):
            if c < 4:
                return S["ab_done"], (3, 4, 7, 8)[c]
            if c < 12:
                return S["z_done"], TT * (c - 3) if c < 10 else 8 * TT - 11 + c
            return S["wo_done"], WO.index((c, TT - 1)) + 1

        def gate_high(c):
            return (cat_r[:, CHUNK:2 * CHUNK], cv_r[:, :], ring_r[:, 4, :], ring_r[:, 5, :])[c]

        LOADS = (4, 4, 4, 4, 1, 0)

        @block.sync
        def _(sp):
            W = w_in[0]

            def load(s, view_, src):
                sp.dma_start(view_, src).then_inc(slot_in[s], 16)

            for i in range(TT):
                sp.dma_start(x_sb[0:rows(i), i, :], x_rows(i)).then_inc(x_in[i], 16)
            for s, n in enumerate((0, 2, 1, 3)):
                load(s, slot8(s), w_cols(W, n))
                if s == 1:
                    sp.dma_start(cpar_rows[0:TAPS, :], conv_w[0]).then_inc(S["params_in"], 16)
                    for m, v in enumerate((conv_b, conv_ln_g, conv_ln_b)):
                        sp.dma_start(cpar_rows[TAPS + m:TAPS + m + 1, :], v).then_inc(S["params_in"], 16)
                    for a in range(2):
                        sp.dma_start(hist_rows[:, a, :], state_conv[0, 4 * a:4 * a + 4, :, :].rearrange(
                            "b t c -> (b t) c")).then_inc(S["hist_in"], 16)
                if s == 3:
                    sp.dma_start(const[:, P:NCONST], consts_d[:, P:NCONST]).then_inc(S["const_in"], 16)
            for c in range(4, 16):
                sp.wait_ge(*used(c - 4))
                load(c % 4, slot8(c % 4), w_cols(W, c) if c < 12 else w_cols_k(w_out[0], c - 12))
            sp.dma_start(states, state_ret[0].rearrange("b h d e -> d b h e")).then_inc(S["states_in"], 16)
            sp.wait_ge(S["cdone"], CT)
            for n in range(TT):
                sp.dma_start(p_sb[0:rows(n), n, :], p_rows(n)).then_inc(S["p_in"], 16)
            for i in range(TT):
                sp.wait_ge(S["og_done"], i + 1)
                sp.dma_start(z[0:rows(i), i, 0:2, :].rearrange("p a n -> p (a n)"), x_rows(i)).then_inc(x_back[i], 16)
            sp.wait_ge(*used(14))
            load(4, ring[:, 4, :], w_ple[0].rearrange("(p k) n -> p (k n)", k=2))
            load(0, ring[:, 0, :], gate_rows(0))
            load(1, ring[:, 1, :], w_up[0, 0, :, :].rearrange("(p k) f -> p (k f)", k=KT))
            load(2, ring[:, 2, :], w_down[0, 0, :, :].rearrange("(p k) n -> p (k n)", k=2))
            sp.wait_ge(*used(15))
            load(3, ring[:, 3, :], gate_rows(1))
            load(5, ring[:, 5, :], w_down[0, 1, :, :].rearrange("(p k) n -> p (k n)", k=2))
            sp.wait_ge(S["ple_done"], TT)
            load(4, ring[:, 4, :], w_up[0, 1, :, :].rearrange("(p k) f -> p (k f)", k=KT))
            wg3 = w_gate[0].rearrange("e (p k) f -> e p (k f)", k=KT)
            wu3 = w_up[0].rearrange("e (p k) f -> e p (k f)", k=KT)
            wd3 = w_down[0].rearrange("e (p k) n -> e p (k n)", k=2)
            def gate_up_in(i, par):
                e = 2 * i + par
                sp.wait_ge(S["gu_done"], e - 1)
                for s, w3 in ((3 * par, wg3), (3 * par + 1, wu3)):
                    load(s, ring[:, s, :], w3[bass.ds(e, 1), :, :].rearrange("e p n -> (e p) n"))

            def down_in(i, par):
                e = 2 * i + par
                sp.wait_ge(S["d_done"], e - 1)
                load(3 * par + 2, ring[:, 3 * par + 2, :], wd3[bass.ds(e, 1), :, :].rearrange("e p n -> (e p) n"))

            gate_up_in(1, 0)
            gate_up_in(1, 1)
            down_in(1, 0)
            with sp.Fori(2, NE // 2) as i:
                gate_up_in(i, 0)
                down_in(i - 1, 1)
                gate_up_in(i, 1)
                down_in(i, 0)
            down_in(NE // 2 - 1, 1)
            for s in range(3):
                if s != 1:
                    sp.wait_ge(S["gu_done" if s == 0 else "d_done"], NE - 1)
                load(s, slot8(s), w_cols(w_ple_gate[0], s))
            sp.wait_ge(S["idx_done"], 3)
            n_ov = sp.value_load(ovinfo[0:1, NOV:NOV + 1], min_val=0, max_val=NOV)
            sp.wait_ge(S["gu_done"], NE)
            with sp.If(n_ov > 0):
                sp.wait_ge(S["d_done"], NE)
                with sp.Fori(0, NOV) as j:
                    e = sp.value_load(ovinfo[0:1, bass.ds(j, 1)], min_val=0, max_val=NE - 1)
                    sp.wait_ge(S["ov_end"], j + 1)
                    for s, w3 in ((3, wg3), (4, wu3), (5, wd3)):
                        src = w3[bass.ds(e, 1), :, :].rearrange("e p n -> (e p) n")
                        sp.dma_start(ring[:, s, :], src).then_inc(S["ov_load"], 16)
                sp.wait_ge(S["ov_end"], NOV + 1)
            sp.nop()
            sp.wait_ge(S["moe_out"], 1)
            for i in range(2):
                sp.dma_start(yins[i], moe2[i * P:(i + 1) * P, :, :]).then_inc(moe_in[i], 16)
                if i == 0:
                    load(3, slot8(3), w_cols(w_ple_gate[0], 3))

        @block.tensor
        def _(pe):
            def mm(out, lhsT, rhs, start, stop):
                return nc.tensor.matmul(out, lhsT, rhs, start=start, stop=stop, skip_group_check=True)

            def tr(out, in_):
                k = in_.shape[0]
                return nc.tensor.transpose(out, in_, ident[0:k, 0:k])

            def slot_ready(s, use):
                pe.wait_ge(slot_in[s], 16 * use)

            def rows_T(src, i, banks, done):
                r = rows(i)
                for k in range(KT):
                    m = tr(banks[k // 4][:, (k % 4) * P:(k % 4) * P + r], src[0:r, k:D:KT])
                m.then_inc(done, 1)

            pe.wait_ge(S["ident_in"], 16)
            for i in range(TT):
                pe.wait_ge(S["xn_done"], i + 1)
                if i >= 2:
                    pe.wait_ge(S["hlo_sb"], i - 1)
                rows_T(xn[:, i % 2, :], i, pair(2 * (i % 2)), S["xT_ps"])

            pe.wait_ge(S["params_in"], 64)
            for c in range(CT):
                m = tr(bank[6][:, c * 34:(c + 1) * 34], cpar_rows[:, c * P:(c + 1) * P])
            m.then_inc(S["cpar_T"], 1)
            pe.wait_ge(S["hist_in"], 32)
            for a in range(2):
                for c in range(CT):
                    m = tr(bank[4 + a][:, c * 120:(c + 1) * 120], hist_rows[:, a, c * P:(c + 1) * P])
                m.then_inc(S["hist_T"], 1)

            PARTS = ((0, 0), (0, 1), (1, 0))

            def part8(c, low):
                return ring_r[:, c % 4 if low else 4 + c % 2, :].rearrange("p (k n) -> p k n", k=KT)

            def x_parts(i, low, k):
                return h_lo[:, i, k, 0:rows(i)] if low else h_hi[:, k, tok(i)]

            for c in range(CT):
                if c == 0:
                    pe.wait_ge(S["hT_sb"], 2 * TT)
                    pe.wait_ge(S["cpar_sb"], 1)
                if c == 1:
                    pe.wait_ge(S["hist_sb"], 2)
                if c >= 2:
                    pe.wait_ge(S["u_done"], 2 * (c - 1))
                for n in range(2):
                    s = 2 * (c // 2) + n
                    for which, (w_part, x_part) in enumerate(PARTS):
                        if c % 2 == 0 and which == 0:
                            pe.wait_ge(S["w_hi"], s + 1)
                        if c == 0 and n == 0 and which == 1:
                            pe.wait_ge(S["hlo_sb"], TT)
                        if c % 2 == 0 and which == 2:
                            pe.wait_ge(S["w_lo"], s + 1)
                        for k in range(KT):
                            w = part8(s, w_part)[:, k, (c % 2) * P:(c % 2 + 1) * P]
                            x = h_lo[:, 0:TT - 1, k, :] if x_part else h_hi[:, k, 0:SEQ].rearrange("p (i t) -> p i t", i=TT - 1)
                            mm(bank[2 + 2 * (c % 2) + n][:, :].rearrange("p (i t) -> p i t", i=TT - 1), w, x,
                               which == 0 and k == 0, which == 2 and k == KT - 1)
                    for which, (w_part, x_part) in enumerate(PARTS):
                        for k in range(KT):
                            w = part8(s, w_part)[:, k, (c % 2) * P:(c % 2 + 1) * P]
                            m = mm(bank[(6, 1)[c % 2]][:, n * NS:(n + 1) * NS], w, x_parts(TT - 1, x_part, k),
                                   which == 0 and k == 0, which == 2 and k == KT - 1)
                    m.then_inc(S["ab_done"], 1)

            def z_part(c, i):
                n = (c - 4) * TT + i if c < 10 else 6 * TT + 2 * i + c - 10
                if n == 1:
                    pe.wait_ge(S["sig_done"], 2 * (CT - 1))
                if n >= 2:
                    pe.wait_ge(S["z_sb"], n - 1)
                for which, (w_part, x_part) in enumerate(PARTS):
                    if i == 0 and which in (0, 2):
                        pe.wait_ge(S["w_hi" if which == 0 else "w_lo"], c + 1)
                    for k in range(KT):
                        m = mm(bank[3 * (n % 2)][0:rows(i), 0:256], x_parts(i, x_part, k), part8(c, w_part)[:, k, :],
                               which == 0 and k == 0, which == 2 and k == KT - 1)
                m.then_inc(S["z_done"], 1)

            for c in range(4, 10):
                for i in range(TT):
                    z_part(c, i)

            def channel_sum(src, b, done):
                for c in range(CT):
                    mm(bank[b][:, :], C("ones"), src[:, c, 0:SEQ], c == 0, c == CT - 1)
                for c in range(CT):
                    m = mm(bank[b - 1][:, 0:NS], C("ones"), src[:, c, SEQ:T], c == 0, c == CT - 1)
                m.then_inc(done, 1)

            pe.wait_ge(S["const_in"], 16)
            pe.wait_ge(S["convp"], CT * TAPS)
            pe.wait_ge(S["convs"], CT * TAPS)
            channel_sum(conv, 7, S["mean_done"])
            pe.wait_ge(S["tail_u"], CT)
            for c in range(CT):
                tr(bank[4][0:HIST, c * P:(c + 1) * P], uext[:, c, SEQ:SEQ + HIST])
            for c in range(CT):
                m = tr(bank[5][0:NS, c * P:(c + 1) * P], kTs[:, c, 0:NS])
            m.then_inc(S["tail_T"], 1)
            def retention_scores(i):
                r = rows(i)
                pe.wait_ge(S["qT_sb"], i + 1)
                pe.wait_ge(S["kT_sb"], i + 1)
                for h in range(NH):
                    m = mm(bank[4][0:r, h * P:h * P + r], kTs[:, h, 0:r], qTs[:, h, 0:r], True, True)
                m.then_inc(S["s_done"], 1)

            def retention_out(i):
                r = rows(i)
                pe.wait_ge(S["s_sb"], i + 1)
                pe.wait_ge(S["qTx_sb"], i + 1)
                if 0 < i < TT - 1:
                    pe.wait_ge(S["r_upd"], 1 + NH * (i - 1))
                if i == TT - 1:
                    pe.wait_ge(S["qm_done"], NH)
                    pe.wait_ge(S["states_in"], 16)
                if i >= 1:
                    pe.wait_ge(S["on_done"], NH * i)
                for h in range(NH):
                    o = bank[5][0:r, h * HD:(h + 1) * HD]
                    v = z[0:r, i, 2, h * HD:(h + 1) * HD]
                    if i == TT - 1:
                        for b in range(NB):
                            mm(o, qmask[:, h, b, :], states[:, b, h, :], b == 0, False)
                    elif i:
                        mm(o, qTx[:, h, 0:r], Rst[:, h, :], True, False)
                    m = mm(o, Sm[0:r, h, 0:r], v, i == 0, True)
                pe.wait_ge(S["kz_done"], i + 1)
                if i < TT - 1:
                    for h in range(NH):
                        m = mm(bank[6][:, h * HD:(h + 1) * HD], kz[:, h * HD:(h + 1) * HD],
                               z[:, i, 2, h * HD:(h + 1) * HD], True, True)
                m.then_inc(S["o_done"], 1)

            def gated_T(i):
                r = rows(i)
                pe.wait_ge(S["og_done"], i + 1)
                if i >= 1:
                    pe.wait_ge(S["oT_sb"], i)
                for h in range(NH):
                    m = tr(bank[7][:, h * P:h * P + r], z[0:r, i, 3, h * HD:(h + 1) * HD])
                m.then_inc(S["oT_done"], 1)

            def q_k_T(i):
                pe.wait_ge(S["rope_done"], TT + i + 1)
                if i == 0:
                    pe.wait_ge(S["cmean"], 2 * CT)
                for j, b in ((0, 2), (1, 1)):
                    for h in range(NH):
                        m = tr(bank[b][:, h * P:h * P + rows(i)], z[0:rows(i), i, j, h * HD:(h + 1) * HD])
                m.then_inc(S["qk_T"], 1)

            def sample_states(heads):
                for n in range(2 * heads[0], 2 * heads[-1] + 2):
                    h, a = n // 2, n % 2
                    pe.wait_ge(S["vm_done" if h % 2 == 0 else "vm2_done"], h // 2 + 1)
                    if n == 0:
                        pe.wait_ge(S["r_upd"], 1 + NH * (TT - 2))
                    if n >= 2:
                        pe.wait_ge(S["rs_upd"], n - 1)
                    mm(bank[(6, 4)[n % 2]][:, :], kz[0:NS, h * HD:(h + 1) * HD], vmask[h % 2][:, 4 * a:4 * a + 4, :],
                       True, True).then_inc(S["kvs_done"], 1)

            def w_out_part(c, i):
                n = WO.index((c, i))
                if n == 0:
                    pe.wait_ge(S["z_sb"], 8 * TT)
                if n >= 4:
                    pe.wait_ge(S["x1_sum"], n - 3)
                for which, (w_part, x_part) in enumerate(PARTS):
                    if i == 0 and which in (0, 2):
                        pe.wait_ge(S["w_hi" if which == 0 else "w_lo"], c + 1)
                    if c == 12 and which == 0:
                        pe.wait_ge(S["hT_sb"], 2 * TT + 2 + i)
                    if c == 12 and which == 1:
                        pe.wait_ge(S["hlo_sb"], TT + 2 + i)
                    for k in range(KT):
                        x = cat_lo[:, k, tok(i)] if x_part else (conv_hi if k < CT else h_hi)[:, k, tok(i)]
                        m = mm(bank[n % 4][0:rows(i), 0:256], x, part8(c, w_part)[:, k, :],
                               which == 0 and k == 0, which == 2 and k == KT - 1)
                m.then_inc(S["wo_done"], 1)

            def p_T(tiles):
                if tiles[0]:
                    pe.wait_ge(S["pT_sb"], tiles[0])
                else:
                    pe.wait_ge(S["oT_sb"], TT)
                for i in tiles:
                    for k in range(2):
                        c = 256 * (i % 2) + P * k
                        m = tr(bank[7][:, c:c + rows(i)], p_sb[0:rows(i), i, k:PLE:2])
                m.then_inc(S["pT_ps"], 1)

            def ple_tile(i):
                r = rows(i)
                if i == 0:
                    slot_ready(4, 1)
                    pe.wait_ge(S["pT_sb"], TT)
                if i < 2:
                    pe.wait_ge(S["x1_sum"], len(WO))
                else:
                    pe.wait_ge(S["ple_raw"], 2 * (i - 1))
                for a in range(2):
                    for k in range(2):
                        m = mm(pair(2 - 2 * (i % 2))[a][0:r, :], pT[:, k, tok(i)],
                               slot2(4)[:, k, a * 512:(a + 1) * 512], k == 0, k == 1)
                m.then_inc(S["ple_done"], 1)

            def h2_T(i):
                pe.wait_ge(S["h2_done"], i + 1)
                if i:
                    pe.wait_ge(S["h2T_sb"], 2 * i)
                else:
                    pe.wait_ge(S["rs_upd"], 2 * NH)
                rows_T(h2[i], i, pair(4), S["h2T_ps"])

            def router(i):
                if i == 0:
                    pe.wait_ge(S["router_in"], 64)
                pe.wait_ge(S["h2T_sb"], 2 * (i + 1))
                for k in range(KT):
                    m = mm(bank[6][0:rows(i), i * 36:(i + 1) * 36], hT[:, k, tok(i)], wr[:, k, :], k == 0, k == KT - 1)
                m.then_inc(S["logit_done"], 1)

            for i in range(TT):
                if i == 0:
                    z_part(10, 0)
                q_k_T(i)
                z_part(11, i)
                if i == 0:
                    pe.wait_ge(S["csq"], 1)
                    pe.wait_ge(S["tail_sb"], 2)
                    channel_sum(squares, 5, S["var_done"])
                    pe.wait_ge(S["cstd"], 2)
                retention_scores(i)
                if i < TT - 1:
                    z_part(10, i + 1)
                    retention_out(i)
                    if i >= 1:
                        gated_T(i - 1)
            for i in range(TT - 1):
                w_out_part(12, i)
                if i == 0:
                    gated_T(TT - 2)
            retention_out(TT - 1)
            for i in range(TT - 1):
                w_out_part(13, i)
            gated_T(TT - 1)
            sample_states((0, 1))
            w_out_part(12, TT - 1)
            w_out_part(13, TT - 1)
            sample_states((2, 3))
            pe.wait_ge(S["p_in"], 16 * TT)
            p_T((0, 1))
            for i in range(TT):
                w_out_part(14, i)
                if i == 2:
                    p_T((2, 3))
            p_T((4,))
            for i in range(TT):
                w_out_part(15, i)
                if i == 2:
                    h2_T(0)
                if i == 3:
                    router(0)
                    h2_T(1)
            router(1)
            h2_T(2)
            ple_tile(0)
            router(2)
            h2_T(3)
            ple_tile(1)
            router(3)
            h2_T(4)
            ple_tile(2)
            router(4)
            ple_tile(3)
            pe.wait_ge(S["picks_done"], 1)
            for i in range(TT):
                for j in range(i + 1):
                    r = rows(j)
                    w = C("before", r) if j == i else C("ones", r)
                    mm(bank[7][0:rows(i), i * NE:(i + 1) * NE], w[:, 0:rows(i)], both[0:r, j, :], j == 0, j == i)
            for j in range(TT):
                r = rows(j)
                m = mm(bank[7][:, TT * NE:(TT + 1) * NE], C("ones", r), both[0:r, j, :], j == 0, j == TT - 1)
            m.then_inc(S["rank_done"], 1)
            ple_tile(4)
            for n in range(2 * TT):
                i, r = n // 2, rows(n // 2)
                pe.wait_ge(S["laneone_done"], 2 * (n + 1))
                mm(bank[5][:, 0:NBLK], laneone[0:r, n, :], blockone[0:r, n, :], n == 0,
                   n == 2 * TT - 1).then_inc(S["table_done"], 1)

            def x_T(i, q):
                pe.wait_ge(gathered[q], 16 * i + 16)
                for k in range(KT):
                    m = tr(bank[2 + k // 4][:, (k % 4) * P:(k % 4 + 1) * P], X[q][:, k:D:KT])
                m.then_inc(S["xt_ps"], 1)

            def gate_up(i, q):
                i, par = 2 * i + q // 2, q % 2
                high = cat_r[:, 0:2 * CHUNK].rearrange("p (a k n) -> p k a n", a=2, k=KT)
                low = ring_r[:, 3 * par:3 * par + 2, :].rearrange("p a (k n) -> p k a n", k=KT)
                pe.wait_ge(S["xt_sb"], 2 * (2 * i + par) + 2)
                pe.wait_ge(S["w_hi"], 16 + 2 * (2 * i + par) + 2)
                for k in range(KT):
                    mm(bank[par][:, :], XT_hi[:, par, k, :], high[:, k, :, :], k == 0, False)
                pe.wait_ge(S["hlo_sb"], LOWS + 2 * i + par + 1)
                for k in range(KT):
                    mm(bank[par][:, :], XT_lo[:, par, k, :], high[:, k, :, :], False, False)
                pe.wait_ge(S["w_lo"], 16 + 2 * (2 * i + par) + 2)
                for k in range(KT):
                    m = mm(bank[par][:, :], XT_hi[:, par, k, :], low[:, k, :, :], False, k == KT - 1)
                m.then_inc(S["gu_done"], 1)

            def hid_T(i, q):
                i, par = 2 * i + q // 2, q % 2
                pe.wait_ge(S["hid_done"], 2 * i + par + 1)
                for k in range(2):
                    m = tr(bank[4][:, k * P:(k + 1) * P], hid[:, par, k:FF:2])
                m.then_inc(S["hT_ps"], 1)

            def down(i, q):
                i, par = 2 * i + q // 2, q % 2
                pe.wait_ge(S["hT_ev"], 2 * i + par + 1)
                pe.wait_ge(slot_in[3 * par + 2], 16 * i + 16 * (LOADS[3 * par + 2] + 1))
                if not (isinstance(i, int) and i == 0 and par == 0):
                    pe.wait_ge(S["y_ready"], 2 * (2 * i + par))
                for a in range(2):
                    for k in range(2):
                        m = mm(bank[5 + a][:, :], hidT[:, par, k, :],
                               slot2(3 * par + 2)[:, k, a * 512:(a + 1) * 512], k == 0, k == 1)
                m.then_inc(S["d_done"], 1)

            def step(i, q, first=False, last=False):
                gate_up(i, q)
                if not last:
                    x_T(*after(i, q))
                if not first:
                    down(*before(i, q))
                hid_T(i, q)

            pe.wait_ge(S["ple_raw"], 2 * TT)
            pe.wait_ge(S["table_sb"], 1)
            x_T(0, 0)
            step(0, 0, first=True)
            for q in range(1, NX):
                step(0, q)
            with pe.Fori(1, LOOPS - 1) as i:
                for q in range(NX):
                    step(i, q)
            for q in range(NX):
                step(LOOPS - 1, q, last=q == NX - 1)
            down(LOOPS - 1, NX - 1)

            pe.wait_ge(S["idx_done"], 3)
            n_ov = pe.value_load(ovinfo[0:1, NOV:NOV + 1], min_val=0, max_val=NOV)
            with pe.If(n_ov > 0):
                with pe.Fori(0, NOV) as j:
                    pe.wait_ge(S["ov_gather"], 16 * j + 16)
                    for k in range(KT):
                        m = tr(bank[2 + k // 4][:, (k % 4) * P:(k % 4 + 1) * P], X[0][:, k:D:KT])
                    m.then_inc(S["ov_xt"], 1)
                    pe.wait_ge(S["ov_xtsb"], 2 * j + 2)
                    pe.wait_ge(S["ov_load"], 48 * j + 48)
                    for k in range(KT):
                        m = mm(bank[0][:, :], XT[:, 0, k, :], slots8(3)[:, k, :, :], k == 0, k == KT - 1)
                    m.then_inc(S["ov_gu"], 1)
                    pe.wait_ge(S["ov_hid"], j + 1)
                    for k in range(2):
                        m = tr(bank[4][:, k * P:(k + 1) * P], hid[:, 0, k:FF:2])
                    m.then_inc(S["ov_hT"], 1)
                    pe.wait_ge(S["ov_hTsb"], j + 1)
                    for a in range(2):
                        for k in range(2):
                            m = mm(bank[5 + a][:, :], hidT[:, 0, k, :], slot2(5)[:, k, a * 512:(a + 1) * 512],
                                   k == 0, k == 1)
                    m.then_inc(S["ov_d"], 1)
            pe.nop()

            def x2_T(i):
                pe.wait_ge(S["x2_done"], i + 1)
                if i >= 2:
                    pe.wait_ge(S["hlo_sb"], LOWS + NE + i - 1)
                else:
                    pe.wait_ge(S["y_ready"], 2 * NE)
                rows_T(z[:, i, 0:2, :].rearrange("p a n -> p (a n)"), i, pair(2 * (i % 2)), S["x2T_ps"])

            def gate_half(i, a):
                for c in (2 * a, 2 * a + 1):
                    for which, (w_part, x_part) in enumerate(((0, 0), (1, 0), (0, 1))):
                        if i == 0 and which < 2:
                            pe.wait_ge(S["w_hi" if which == 0 else "w_lo"], 16 + 2 * NE + c + 1)
                        if c == 0 and which == 2:
                            pe.wait_ge(S["hlo_sb"], LOWS + NE + i + 1)
                        w = (ring_r[:, c, :] if w_part else gate_high(c)).rearrange("p (k n) -> p k n", k=KT)
                        for k in range(KT):
                            x = x2_lo[:, i % 2, k, 0:rows(i)] if x_part else h_hi[:, k, tok(i)]
                            m = mm(pair(4 + 2 * (i % 2))[a][0:rows(i), 256 * (c % 2):256 * (c % 2 + 1)], x, w[:, k, :],
                                   which == 0 and k == 0, which == 2 and k == KT - 1)
                m.then_inc(S["pg_done"], 1)

            x2_T(0)
            for i in range(TT):
                pe.wait_ge(S["x2T_low"], i + 1)
                pe.wait_ge(S["x2T_high"], i + 1)
                if i >= 2:
                    pe.wait_ge(S["sg_done"], 2 * (i - 1))
                gate_half(i, 0)
                if i + 1 < TT:
                    x2_T(i + 1)
                gate_half(i, 1)

        @block.vector
        def _(dve):
            V = nc.vector
            order = [0]

            def then(ins):
                order[0] += 1
                ins.then_inc(S["dve_order"], 1)
                dve.wait_ge(S["dve_order"], order[0])

            for t in (ssq, ssq2):
                V.memset(t[:, :], 1.0).then_inc(S["zeroed"], 1)
            for t in (ssq3, ssq4):
                V.memset(t[:, :, :], 1.0).then_inc(S["zeroed"], 1)
            V.memset(epsb[:, :], EPS).then_inc(S["zeroed"], 1)
            V.memset(half[:, :], -0.5).then_inc(S["zeroed"], 1)
            V.memset(mv[:, :, :], 1.0).then_inc(S["zeroed"], 1)
            def x_norm(i):
                r = rows(i)
                dve.wait_ge(S["xstd"], i + 1)
                then(V.reciprocal(rst[0:r, i:i + 1], rst[0:r, i:i + 1]))
                if i == 0:
                    dve.wait_ge(S["gbc_in"], 16)
                if i >= 2:
                    dve.wait_ge(S["xT_ps"], i - 1)
                V.scalar_tensor_tensor(xn[0:r, i % 2, :], x_sb[0:r, i, :], rst[0:r, i:i + 1], gbc[0:r, :], ALU.mult,
                                       ALU.mult).then_inc(S["xn_done"], 1)

            def h_low(i):
                dve.wait_ge(S["hT_sb"], 2 * i + 2)
                for a in range(2):
                    m = V.tensor_tensor(h_lo[:, i, 4 * a:4 * a + 4, 0:rows(i)], quads(i, a),
                                        h_hi[:, 4 * a:4 * a + 4, tok(i)].bitcast(F32), ALU.subtract)
                m.then_inc(S["hlo_sb"], 1)

            x_norm(0)
            x_norm(1)
            for i in range(TT):
                h_low(i)
                if i + 2 < TT:
                    x_norm(i + 2)
            dve.wait_ge(S["cpar_T"], 1)
            V.tensor_copy(cpar[:, :, :], bank[6][:, 0:CT * 34].rearrange("p (c n) -> p c n", c=CT)).then_inc(S["cpar_sb"], 1)
            dve.wait_ge(S["const_in"], 16)

            dve.wait_ge(S["cpar_sb"], 1)
            dve.wait_ge(S["zero_x"], 1)
            dve.wait_ge(S["hist_sb"], 2)
            def glu(c):
                dve.wait_ge(S["sig_done"], 2 * (c + 1))
                V.tensor_tensor(uext[:, c, HIST:HIST + SEQ], bank[2 + 2 * (c % 2)][:, :], sig[:, c % 2, 0:SEQ],
                                ALU.mult).then_inc(S["u_done"], 1)
                V.tensor_tensor(sext[:, c, :, HIST:HIST + NL],
                                bank[(6, 1)[c % 2]][:, 0:NS].rearrange("p (b t) -> p b t", b=NB),
                                sig[:, c % 2, SEQ:T].rearrange("p (b t) -> p b t", b=NB),
                                ALU.mult).then_inc(S["u_done"], 1)

            ahead = (15, 6, 2)
            glu(0)
            for c in range(CT):
                dve.wait_ge(S["u_done"], 2 * (c + 1))
                cs = conv[:, c, SEQ:T].rearrange("p (b t) -> p b t", b=NB)
                for t in range(TAPS):
                    tap = cpar[:, c, t:t + 1]
                    out = bank[7][:, :] if t < TAPS - 1 else conv[:, c, 0:SEQ]
                    if t == 0:
                        if c:
                            dve.wait_ge(S["convp"], c * TAPS)
                        bias = cpar[:, c, TAPS:TAPS + 1]
                        V.tensor_scalar(out, uext[:, c, 0:SEQ], tap, bias, ALU.mult, ALU.add).then_inc(S["convp"], 1)
                        V.tensor_scalar(cs, sext[:, c, :, 0:NL], tap, bias, ALU.mult, ALU.add).then_inc(S["convs"], 1)
                    else:
                        dve.wait_ge(S["convp"], c * TAPS + t)
                        V.scalar_tensor_tensor(out, uext[:, c, t:t + SEQ], tap, bank[7][:, :], ALU.mult,
                                               ALU.add).then_inc(S["convp"], 1)
                        dve.wait_ge(S["convs"], c * TAPS + t)
                        V.scalar_tensor_tensor(cs, sext[:, c, :, t:t + NL], tap, cs, ALU.mult,
                                               ALU.add).then_inc(S["convs"], 1)
                    if c < CT - 1 and t == ahead[c]:
                        glu(c + 1)
            dve.wait_ge(S["convp"], CT * TAPS)
            dve.wait_ge(S["convs"], CT * TAPS)
            dve.wait_ge(S["mean_done"], 1)
            for c in range(CT):
                for b, cols in ((7, slice(0, SEQ)), (6, slice(SEQ, T))):
                    v = conv[:, c, cols]
                    V.scalar_tensor_tensor(v, bank[b][:, 0:v.shape[1]], -1.0 / CH, v, ALU.mult,
                                           ALU.add).then_inc(S["cmean"], 1)
            def x1(i, a=None):
                v = z[0:rows(i), i, 0:2, :]
                return v.rearrange("p a n -> p (a n)") if a is None else v[:, a, :]

            def add_x(c, i):
                n = WO.index((c, i))
                if c == 12:
                    dve.wait_ge(x_back[i], 16)
                dve.wait_ge(S["wo_done"], n + 1)
                v = x1(i)[:, 256 * (c - 12):256 * (c - 11)]
                V.tensor_tensor(v, bank[n % 4][0:rows(i), 0:256], v, ALU.add).then_inc(S["x1_sum"], 1)

            def heads_low(i):
                dve.wait_ge(S["hT_sb"], 2 * TT + 2 + i)
                V.tensor_tensor(cat_lo[:, CT:KT, tok(i)], catT[:, CT:KT, tok(i)],
                                h_hi[:, CT:KT, tok(i)].bitcast(F32), ALU.subtract).then_inc(S["hlo_sb"], 1)

            def v_masks(h):
                if h > 1:
                    dve.wait_ge(S["kvs_done"], 2 * h - 2)
                V.tensor_tensor(vmask[1], bc(z[0:NS, TT - 1, 2, h * HD:(h + 1) * HD], 1, NB),
                                bc(C("row8", NS), 2, HD), ALU.mult).then_inc(S["vm2_done"], 1)

            for i in range(TT):
                r = rows(i)
                dve.wait_ge(S["qT_sb"], i + 1)
                if i == 0:
                    dve.wait_ge(S["rope_done"], 2 * TT)
                if i < TT - 1:
                    V.tensor_tensor(qTx[:, :, :], qTs[:, :, :],
                                    C("xi").rearrange("p (h t) -> p h t", h=NH), ALU.mult).then_inc(S["qTx_sb"], 1)
                    decay = C("decay").rearrange("p (h t) -> p h t", h=NH)
                else:
                    for h in range(NH):
                        m = V.tensor_tensor(qTx[:, h, 0:NS].rearrange("p (b t) -> p b t", b=NB),
                                            qTs[:, h, 0:NS].rearrange("p (b t) -> p b t", b=NB),
                                            bc(C("xi")[:, h * P:h * P + NL], 1, NB), ALU.mult)
                        if h == NH - 1:
                            m.then_inc(S["qTx_sb"], 1)
                    decay = C("decay_s", NS).rearrange("p (h t) -> p h t", h=NH)
                dve.wait_ge(S["s_done"], i + 1)
                V.tensor_tensor(Sm[0:r, :, 0:r], bank[4][0:r, :].rearrange("p (h t) -> p h t", h=NH)[:, :, 0:r],
                                decay, ALU.mult).then_inc(S["s_sb"], 1)
                if i == 0:
                    dve.wait_ge(S["cstd"], 2)
                    cst = squares[:, 0, :]
                    then(V.reciprocal(cst, cst))
                    V.tensor_tensor(conv, conv, bc(cst, 1, CT), ALU.mult).then_inc(S["crstd"], 1)
                if i == 2:
                    dve.wait_ge(S["cdone"], CT)
                    dve.wait_ge(S["z_sb"], 6 * TT)
                    v_masks(1)
                    dve.wait_ge(S["hT_sb"], 2 * TT + 1)
                    V.tensor_tensor(cat_lo[:, 0:CT, :], catT[:, 0:CT, :], conv_hi[:, :, :].bitcast(F32),
                                    ALU.subtract).then_inc(S["hlo_sb"], 1)
                if i == TT - 1:
                    for t in range(TT - 1):
                        heads_low(t)
                    for t in range(TT - 1):
                        add_x(12, t)
                dve.wait_ge(S["o_done"], i + 1)
                if i == 0:
                    V.tensor_copy(Rst[:, :, :], bank[6][:, :].rearrange("p (h e) -> p h e", h=NH)).then_inc(S["r_upd"], 1)
                elif i < TT - 1:
                    for h in range(NH):
                        V.scalar_tensor_tensor(Rst[:, h, :], Rst[:, h, :], float(np.exp(P * np.log(GAMMA[h]))),
                                               bank[6][:, h * HD:(h + 1) * HD], ALU.mult, ALU.add).then_inc(S["r_upd"], 1)
                for h in range(NH):
                    m = V.bn_stats(bns[0:r, h, :], bank[5][0:r, h * HD:(h + 1) * HD])
                then(m)
                for h in range(NH):
                    m = V.bn_aggr(mv[0:r, h, :], bns[0:r, h, :])
                then(m)
                V.tensor_scalar(mv[0:r, :, 1], mv[0:r, :, 1], EPS, None, ALU.add).then_inc(S["gn_var"], 1)
                dve.wait_ge(S["gn_rstd"], i + 1)
                for h in range(NH):
                    V.tensor_scalar(z[0:r, i, 0, h * HD:(h + 1) * HD], bank[5][0:r, h * HD:(h + 1) * HD],
                                    mv[0:r, h, 0:1], grs[0:r, h:h + 1], ALU.subtract, ALU.mult).then_inc(S["on_done"], 1)

            for i in range(TT - 1):
                add_x(13, i)
            for n in range(2 * NH):
                h, a = n // 2, n % 2
                if n == 4:
                    heads_low(TT - 1)
                    add_x(12, TT - 1)
                    add_x(13, TT - 1)
                    v_masks(3)
                dve.wait_ge(S["kvs_done"], n + 1)
                st = states[:, 4 * a:4 * a + 4, h, :]
                V.scalar_tensor_tensor(st, st, float(np.exp(NL * np.log(GAMMA[h]))),
                                       bank[(6, 4)[n % 2]][:, :].rearrange("p (b e) -> p b e", b=4), ALU.mult,
                                       ALU.add).then_inc(S["rs_upd"], 1)

            def ple(i, a=None):
                v = z[0:rows(i), i, 2:4, :]
                return v.rearrange("p a n -> p (a n)") if a is None else v[:, a, :]

            def norm2(i):
                r = rows(i)
                dve.wait_ge(S["x1_std"], i + 1)
                then(V.reciprocal(rst2[0:r, i:i + 1], rst2[0:r, i:i + 1]))
                if i == 0:
                    dve.wait_ge(S["gbc_in"], 32)
                if i == 0:
                    dve.wait_ge(S["rs_out"], 16)
                V.scalar_tensor_tensor(h2[i][0:r, :], x1(i), rst2[0:r, i:i + 1], gbc[0:r, :], ALU.mult,
                                       ALU.mult).then_inc(S["h2_done"], 1)

            def h2_out_high(i):
                dve.wait_ge(S["h2T_ps"], i + 1)
                V.tensor_copy(hT[:, 4:8, tok(i)],
                              bank[5][:, :].rearrange("p (k t) -> p k t", k=4)[:, :, 0:rows(i)]).then_inc(S["h2T_sb"], 1)

            for i in range(TT):
                add_x(14, i)
            add_x(15, 0)
            for i in range(1, TT):
                add_x(15, i)
                norm2(i - 1)
                if i >= 2:
                    h2_out_high(i - 2)
            norm2(TT - 1)
            h2_out_high(TT - 2)
            h2_out_high(TT - 1)

            dve.wait_ge(S["wo_done"], len(WO))
            then(V.memset(logit, 0.0))
            V.memset(tabz, 0.0).then_inc(S["zeroed"], 1)
            V.memset(zero32, 0.0).then_inc(S["zeroed"], 1)
            dve.wait_ge(S["logit_done"], TT)
            dve.wait_ge(S["router_in"], 64)
            ps = bank[6][:, 0:TT * 36].rearrange("p (i n) -> p i n", i=TT)
            V.tensor_tensor(logit[:, 0:TT - 1, :], ps[:, 0:TT - 1, :], bc(rbias[:, :], 1, TT - 1), ALU.add).then_inc(S["logit_sb"], 1)
            V.tensor_tensor(logit[0:NS, TT - 1, :], ps[0:NS, TT - 1, :], rbias[0:NS, :], ALU.add).then_inc(S["logit_sb"], 1)
            dve.wait_ge(S["logit_sb"], 2)
            lg = logit[:, :, 0:NG]
            then(V.tensor_reduce(gmx, lg, AX.X, ALU.max))
            V.tensor_tensor(gexp, lg, bc(gmx, 2, NG), ALU.subtract).then_inc(S["logit_sb"], 1)

            def first_of(one, values, mx, tmp, n):
                then(V.tensor_tensor(one, values, bc(mx, 2, n), ALU.is_equal))
                then(V.tensor_tensor(tmp, one, bc(C("rev")[:, 0:n], 1, TT), ALU.mult))
                then(V.tensor_reduce(t1, tmp, AX.X, ALU.max))
                then(V.tensor_tensor(one, tmp, bc(t1, 2, n), ALU.is_equal))

            first_of(gone, lg, gmx, gval, NG)
            then(V.tensor_tensor(sel, logit[:, :, NG:].rearrange("p i (g e) -> p i g e", g=NG),
                                 bc(gone, 3, NEG), ALU.mult))
            then(V.tensor_reduce(el, sel.rearrange("p i g e -> p i e g"), AX.X, ALU.add))
            then(V.tensor_reduce(m1, el, AX.X, ALU.max))
            first_of(one1, el, m1, eval_, NEG)
            then(V.tensor_scalar(eval_, one1, -3.0e38, None, ALU.mult))
            then(V.tensor_tensor(el, el, eval_, ALU.add))
            then(V.tensor_reduce(m2, el, AX.X, ALU.max))
            V.tensor_tensor(e2, m2, m1, ALU.subtract).then_inc(S["logit_sb"], 1)
            first_of(one2, el, m2, eval_, NEG)
            for k, one in ((0, one1), (1, one2)):
                for i in range(TT):
                    m = V.tensor_tensor(M[k][:, i, :].rearrange("p (g e) -> p g e", g=NG), bc(gone[:, i, :], 2, NEG),
                                        bc(one[:, i, :], 1, NG), ALU.mult)
                then(m)
            V.tensor_tensor(both, M[0], M[1], ALU.add).then_inc(S["picks_done"], 1)
            dve.wait_ge(S["rank_done"], 1)
            then(V.memset(rank, 0.0))
            rp = bank[7][:, 0:(TT + 1) * NE].rearrange("p (i n) -> p i n", i=TT + 1)
            V.tensor_copy(rank[:, 0:TT - 1, :], rp[:, 0:TT - 1, :])
            V.tensor_copy(rank[0:NS, TT - 1, :], rp[0:NS, TT - 1, :])
            then(V.tensor_copy(rank[:, TT, :], rp[:, TT, :]))
            total = rank[:, TT, :]
            then(V.tensor_copy(ovinfo[:, NOV + 1:], total[0:1, :]))
            then(V.tensor_scalar(ov, total, float(SLOTS), None, ALU.is_gt))
            for n in range(2, DEEP):
                then(V.scalar_tensor_tensor(ov, total, float(SLOTS * n), ov, ALU.is_gt, ALU.add))
            then(V.tensor_tensor_scan(ovi, zero32, ov, 0.0, ALU.add, ALU.add))
            then(V.tensor_tensor(ovb, ovi, ov, ALU.subtract))
            then(V.tensor_tensor(ovw, ovb, C("expert"), ALU.subtract))
            then(V.tensor_scalar(ovw, ovw, float(NE - 1), None, ALU.add))
            rk = rank[:, 0:TT, :]
            then(V.tensor_scalar(flag, rk, float(SLOTS), None, ALU.is_ge))
            then(V.tensor_copy(deep, flag))
            for n in range(2, DEEP):
                then(V.scalar_tensor_tensor(deep, rk, float(SLOTS * n), deep, ALU.is_ge, ALU.add))
            then(V.tensor_tensor(blk, deep, bc(ovw, 1, TT), ALU.add))
            then(V.tensor_tensor(blk, blk, flag, ALU.mult))
            then(V.tensor_tensor(blk, blk, bc(C("expert"), 1, TT), ALU.add))
            then(V.scalar_tensor_tensor(lane, deep, -float(SLOTS), rk, ALU.mult, ALU.add))
            for k in range(2):
                for pos, what in ((posb, blk), (posl, lane)):
                    then(V.tensor_tensor(prod, what, M[k], ALU.mult))
                    then(V.tensor_reduce(pos[:, k, :], prod, AX.X, ALU.add))
            code = C("code").rearrange("p (i k) -> p i k", i=TT)
            for n in range(2 * TT):
                i, k = n // 2, n % 2
                V.tensor_scalar(laneone[:, n, :], C("lane"), posl[:, k, i:i + 1], None,
                                ALU.is_equal).then_inc(S["laneone_done"], 1)
                V.tensor_scalar(blockone[:, n, :], C("block"), posb[:, k, i:i + 1], code[:, i, k:k + 1],
                                ALU.is_equal, ALU.mult).then_inc(S["laneone_done"], 1)
            dve.wait_ge(S["table_done"], 2 * TT)
            V.tensor_copy(tabf, bank[5][:, 0:NBLK]).then_inc(S["table_sb"], 1)
            dve.wait_ge(S["table_sb"], 1)
            then(V.tensor_scalar(tabz, tabf, 0.0, float(1 << 20), ALU.is_equal, ALU.mult))
            then(V.scalar_tensor_tensor(tabf, tabf, -1.0, tabz, ALU.add, ALU.add))
            V.tensor_copy(codes[:, :], tabf).then_inc(S["idx_done"], 1)
            dve.wait_ge(S["idx_done"], 1)
            V.tensor_scalar(tokidx[:, :], codes[:, :], 1, None, ALU.arith_shift_right).then_inc(S["idx_done"], 1)
            jj = bc(C("ovj", 1), 2, NE)
            then(V.tensor_tensor(ovt[0:1, 0, :, :], bc(ovb[0:1, :], 1, NOV), jj, ALU.is_le))
            then(V.tensor_tensor(ovt[0:1, 1, :, :], bc(ovi[0:1, :], 1, NOV), jj, ALU.is_le))
            then(V.tensor_tensor(ovt[0:1, 0, :, :], ovt[0:1, 0, :, :], ovt[0:1, 1, :, :], ALU.subtract))
            then(V.tensor_tensor(ovt[0:1, 0, :, :], ovt[0:1, 0, :, :], bc(C("expert", 1), 1, NOV), ALU.mult))
            then(V.tensor_reduce(ovf[0:1, 0:NOV], ovt[0:1, 0, :, :], AX.X, ALU.add))
            then(V.tensor_copy(ovf[0:1, NOV:NOV + 1], ovi[0:1, NE - 1:NE]))
            V.tensor_copy(ovinfo[:, 0:NOV + 1], ovf[0:1, :]).then_inc(S["idx_done"], 1)

            dve.wait_ge(S["gexp_done"], 2)
            then(V.tensor_reduce(gsum, gexp, AX.X, ALU.add))
            then(V.tensor_scalar(t1, e2, 1.0, None, ALU.add))
            then(V.tensor_tensor(t1, t1, gsum, ALU.mult))
            then(V.reciprocal(gates[:, :, 0], t1))
            then(V.tensor_tensor(gates[:, :, 1], gates[:, :, 0], e2, ALU.mult))
            dve.wait_ge(S["ple_sq"], 2 * TT)
            V.tensor_tensor(rst3[:, :], ssq3[:, :, 0], ssq3[:, :, 1], ALU.add).then_inc(S["ple_var"], 1)

            def ple_rstd():
                dve.wait_ge(S["ple_std"], 1)
                then(V.reciprocal(rst3[:, :], rst3[:, :]))
                dve.wait_ge(S["pbc_in"], 16)

            def ple_norm(i):
                V.scalar_tensor_tensor(ple(i), ple(i), rst3[0:rows(i), i:i + 1], pbc[0:rows(i), :], ALU.mult,
                                       ALU.mult).then_inc(S["ple_sb"], 1)

            def xt_half(par):
                return XT[:, par, 4:8, :], bank[3][:, :].rearrange("p (k s) -> p k s", k=4)

            def x_out(i, q):
                i, par = 2 * i + q // 2, q % 2
                dve.wait_ge(S["xt_ps"], 2 * i + par + 1)
                V.tensor_copy(XT_hi[:, par, 4:8, :], xt_half(par)[1]).then_inc(S["xt_sb"], 1)

            def x_low(i, q):
                i, par = 2 * i + q // 2, q % 2
                dve.wait_ge(S["xt_sb"], 2 * (2 * i + par) + 2)
                for a in range(2):
                    m = V.tensor_tensor(XT_lo[:, par, 4 * a:4 * a + 4, :],
                                        bank[2 + a][:, :].rearrange("p (k s) -> p k s", k=4),
                                        XT_hi[:, par, 4 * a:4 * a + 4, :].bitcast(F32), ALU.subtract)
                m.then_inc(S["hlo_sb"], 1)

            def w_low(i, q, m):
                i, par = 2 * i + q // 2, q % 2
                dve.wait_ge(S["w_hi"], 16 + 2 * (2 * i + par) + m + 1)
                V.tensor_tensor(ring_r[:, 3 * par + m, :], ring[:, 3 * par + m, :],
                                cat_r[:, m * CHUNK:(m + 1) * CHUNK].bitcast(F32), ALU.subtract).then_inc(S["w_lo"], 1)

            def hidden(i, q):
                i, par = 2 * i + q // 2, q % 2
                dve.wait_ge(S["sil_done"], 2 * i + par + 1)
                V.tensor_tensor(hid[:, par, :], bank[par][:, FF:2 * FF], gat[:, par, :], ALU.mult).then_inc(S["hid_done"], 1)

            def hid_out(i, q):
                i, par = 2 * i + q // 2, q % 2
                dve.wait_ge(S["hT_ps"], 2 * i + par + 1)
                V.tensor_copy(hidT[:, par, :, :], bank[4][:, 0:2 * P].rearrange("p (k s) -> p k s", k=2)).then_inc(S["hT_ev"], 1)

            def y_out(i, q):
                i, par = 2 * i + q // 2, q % 2
                dve.wait_ge(S["d_done"], 2 * i + par + 1)
                if isinstance(i, int):
                    if i == 0 and par == 0:
                        dve.wait_ge(S["rs_out"], 16)
                    if i:
                        dve.wait_ge(scattered[par], 16 * i)
                else:
                    dve.wait_ge(scattered[par], 16 * i)
                V.tensor_copy(yout[:, par, 512:1024], bank[6][:, :]).then_inc(S["y_ready"], 1)

            def x_and_weights(i, q):
                x_out(i, q)
                w_low(i, q, 0)
                x_low(i, q)
                w_low(i, q, 1)

            def step(i, q, first=False, last=False):
                hidden(i, q)
                if not last:
                    x_and_weights(*after(i, q))
                hid_out(i, q)
                if not first:
                    y_out(*before(i, q))

            x_and_weights(0, 0)
            step(0, 0, first=True)
            ple_rstd()
            for q in range(1, NX):
                step(0, q)
                ple_norm(q - 1)
            with dve.Fori(1, LOOPS - 1) as i:
                for q in range(NX):
                    step(i, q)
            for q in range(NX):
                step(LOOPS - 1, q, last=q == NX - 1)
                if q < 2:
                    ple_norm(NX - 1 + q)
            y_out(LOOPS - 1, NX - 1)

            dve.wait_ge(S["idx_done"], 3)
            n_ov = dve.value_load(ovinfo[0:1, NOV:NOV + 1], min_val=0, max_val=NOV)
            with dve.If(n_ov > 0):
                with dve.Fori(0, NOV) as j:
                    dve.wait_ge(S["ov_xt"], j + 1)
                    V.tensor_copy(*xt_half(0)).then_inc(S["ov_xtsb"], 1)
                    dve.wait_ge(S["ov_sil"], j + 1)
                    V.tensor_tensor(hid[:, 0, :], bank[0][:, FF:2 * FF], gat[:, 0, :], ALU.mult).then_inc(S["ov_hid"], 1)
                    dve.wait_ge(S["ov_hT"], j + 1)
                    V.tensor_copy(hidT[:, 0, :, :], bank[4][:, 0:2 * P].rearrange("p (k s) -> p k s", k=2)).then_inc(S["ov_hTsb"], 1)
                    dve.wait_ge(S["ov_d"], j + 1)
                    V.tensor_copy(yout[:, 0, 512:1024], bank[6][:, :]).then_inc(S["ov_y"], 1)
            dve.nop()

            def x2(i):
                r = rows(i)
                dve.wait_ge(moe_in[i % 2], 16 * (i // 2 + 1))
                y = yins[i % 2]
                then(V.scalar_tensor_tensor(x1(i), y[0:r, 0, :], gates[0:r, i, 0:1], x1(i), ALU.mult, ALU.add))
                V.scalar_tensor_tensor(x1(i), y[0:r, 1, :], gates[0:r, i, 1:2], x1(i), ALU.mult,
                                       ALU.add).then_inc(S["x2_done"], 1)

            def x2_out(i):
                dve.wait_ge(S["x2T_ps"], i + 1)
                if i == 0:
                    dve.wait_ge(S["rp_out"], 16)
                if i >= 2:
                    dve.wait_ge(S["pg_done"], 2 * (i - 1))
                V.tensor_copy(h_hi[:, 4:8, tok(i)], quads(i, 1)).then_inc(S["x2T_high"], 1)
                dve.wait_ge(S["x2T_low"], i + 1)
                V.tensor_tensor(x2_lo[:, i % 2, 0:4, 0:rows(i)], quads(i, 0), h_hi[:, 0:4, tok(i)].bitcast(F32),
                                ALU.subtract)
                dve.wait_ge(S["x2T_high"], i + 1)
                V.tensor_tensor(x2_lo[:, i % 2, 4:8, 0:rows(i)], quads(i, 1), h_hi[:, 4:8, tok(i)].bitcast(F32),
                                ALU.subtract).then_inc(S["hlo_sb"], 1)

            def gate_low(c):
                dve.wait_ge(S["w_hi"], 16 + 2 * NE + c + 1)
                V.tensor_tensor(ring_r[:, c, :], ring[:, c, :], gate_high(c).bitcast(F32),
                                ALU.subtract).then_inc(S["w_lo"], 1)

            def x3(i, a):
                r = rows(i)
                dve.wait_ge(S["sg_done"], 2 * i + a + 1)
                if i >= 2:
                    dve.wait_ge(S["x3_sq"], 2 * (i - 1))
                t = xt[0:r, i % 2, a * 512:(a + 1) * 512]
                then(V.tensor_tensor(t, sg[0:r, i % 2, a * 512:(a + 1) * 512], ple(i, a), ALU.mult))
                V.tensor_tensor(t, t, x1(i, a), ALU.add).then_inc(S["x3_done"], 1)

            def final(i):
                r = rows(i)
                dve.wait_ge(S["x3_rstd"], i + 1)
                if i == 0:
                    dve.wait_ge(S["final_in"], 16)
                if i >= 2:
                    dve.wait_ge(y_stored[i % 2], 16 * (i // 2))
                V.scalar_tensor_tensor(yo[0:r, i % 2, :], xt[0:r, i % 2, :], rst4[0:r, i:i + 1], gbc[0:r, :],
                                       ALU.mult, ALU.mult).then_inc(S["out_done"], 1)

            for c in range(3):
                gate_low(c)
            x2(0)
            dve.wait_ge(S["ple_sb"], TT)
            x2_out(0)
            x2(1)
            gate_low(3)
            for i in range(TT):
                if i + 1 < TT:
                    x2_out(i + 1)
                if i + 2 < TT:
                    x2(i + 2)
                for a in range(2):
                    x3(i, a)
                final(i)

        @block.scalar
        def _(act):
            A = nc.scalar
            act.dma_start(const[:, 0:P], consts_d[:, 0:P]).then_inc(S["ident_in"], 16)
            act.dma_start(gbc[:, :], norm1_g[0].partition_broadcast(P)).then_inc(S["gbc_in"], 16)

            def h_high(i):
                act.wait_ge(S["xT_ps"], i + 1)
                for a in range(2):
                    A.activation(h_hi[:, 4 * a:4 * a + 4, tok(i)], quads(i, a), ACT.Copy).then_inc(S["hT_sb"], 1)

            act.wait_ge(S["zeroed"], 7)
            A.activation(rst4[:, 0:1], epsb[:, :], ACT.Sqrt)
            for i in range(TT):
                r = rows(i)
                act.wait_ge(x_in[i], 16)
                if i:
                    act.wait_ge(S["xsq"], i)
                A.activation(sq_out[0:r, :], x_sb[0:r, i, :], ACT.Square, accum_out=ssq[0:r, i:i + 1]).then_inc(S["xsq"], 1)
                act.wait_ge(S["xsq"], i + 1)
                A.activation(rst[0:r, i:i + 1], ssq[0:r, i:i + 1], ACT.Sqrt, bias=epsb[0:r, :],
                             scale=1.0 / D).then_inc(S["xstd"], 1)
                if i:
                    h_high(i - 1)
            h_high(TT - 1)

            def w_high(c):
                act.wait_ge(slot_in[c % 4], 16 * (c // 4 + 1))
                if c >= 2:
                    act.wait_ge(*used(c - 2))
                A.activation(ring_r[:, 4 + c % 2, :], ring[:, c % 4, :], ACT.Copy).then_inc(S["w_hi"], 1)

            act.wait_ge(S["w_hi"], 1)
            w_high(1)
            for i in range(2):
                act.wait_ge(S["hist_T"], i + 1)
                A.activation(sext[:, :, 4 * i:4 * i + 4, 0:HIST],
                             bank[4 + i][:, 0:CT * 120].rearrange("p (c b t) -> p c b t", c=CT, b=4),
                             ACT.Copy).then_inc(S["hist_sb"], 1)
            act.wait_ge(S["xn_done"], TT)
            act.dma_start(conv_s[0, :, 0:HIST - NL, :], state_conv[0, :, NL:HIST, :]).then_inc(S["cs_copy"], 16)
            act.dma_start(wr[:, :, 0:NG], rg_w[0].rearrange("(p k) n -> p k n", k=KT)).then_inc(S["router_in"], 16)
            act.dma_start(wr[:, :, NG:], re_w[0].rearrange("(p k) n -> p k n", k=KT)).then_inc(S["router_in"], 16)
            act.dma_start(rbias[:, 0:NG], rg_b[0].partition_broadcast(P)).then_inc(S["router_in"], 16)
            act.dma_start(rbias[:, NG:], re_b[0].partition_broadcast(P)).then_inc(S["router_in"], 16)
            act.dma_start(gbc[:, :], norm2_g[0].partition_broadcast(P)).then_inc(S["gbc_in"], 16)

            for c in range(CT):
                act.wait_ge(S["ab_done"], 2 * c + 2)
                if c >= 2:
                    act.wait_ge(S["u_done"], 2 * (c - 1))
                A.activation(sig[:, c % 2, 0:SEQ], bank[3 + 2 * (c % 2)][:, :], ACT.Sigmoid).then_inc(S["sig_done"], 1)
                A.activation(sig[:, c % 2, SEQ:T], bank[(6, 1)[c % 2]][:, NS:2 * NS], ACT.Sigmoid).then_inc(S["sig_done"], 1)
                w_high(c + 2)

            def z_out(c, i):
                n = (c - 4) * TT + i if c < 10 else 6 * TT + 2 * i + c - 10
                act.wait_ge(S["z_done"], n + 1)
                A.activation(z[0:rows(i), i, c // 2 - 2, 256 * (c % 2):256 * (c % 2 + 1)],
                             bank[3 * (n % 2)][0:rows(i), 0:256], ACT.Silu if c >= 10 else ACT.Copy).then_inc(S["z_sb"], 1)

            for c in range(4, 10):
                for i in range(TT):
                    z_out(c, i)
                w_high(c + 2)
            act.wait_ge(S["tail_T"], 1)
            A.activation(tails[0:HIST, 0, :], bank[4][0:HIST, :], ACT.Copy).then_inc(S["tail_sb"], 1)
            A.activation(tails[0:NS, 1, :], bank[5][0:NS, :], ACT.Copy).then_inc(S["tail_sb"], 1)
            act.wait_ge(S["cmean"], 2 * CT)
            A.activation(squares, conv, ACT.Square).then_inc(S["csq"], 1)
            act.wait_ge(S["tail_sb"], 2)
            act.dma_start(conv_p[0, 0], tails[0:HIST, 0, :]).then_inc(S["tail_out"], 16)
            for b in range(NB):
                act.dma_start(conv_s[0, b, HIST - NL:HIST, :], tails[b * NL:(b + 1) * NL, 1, :]).then_inc(S["tail_out"], 16)
            def gated_out(i):
                r = rows(i)
                act.wait_ge(S["oT_done"], i + 1)
                if i == 0:
                    act.wait_ge(S["tail_out"], 16 * (1 + NB))
                A.activation(catT[:, 4:8, tok(i)], bank[7][:, :].rearrange("p (h t) -> p h t", h=NH)[:, :, 0:r],
                             ACT.Copy).then_inc(S["oT_sb"], 1)

            z_out(10, 0)
            def heads_high(i):
                act.wait_ge(S["z_done"], 8 * TT)
                act.wait_ge(S["oT_sb"], i + 1)
                A.activation(h_hi[:, CT:KT, tok(i)], catT[:, CT:KT, tok(i)], ACT.Copy).then_inc(S["hT_sb"], 1)

            for i in range(TT):
                r = rows(i)
                act.wait_ge(S["qk_T"], i + 1)
                for t, b, done in ((kTs, 1, "kT_sb"), (qTs, 2, "qT_sb")):
                    A.activation(t[:, :, 0:r], bank[b][:, :].rearrange("p (h t) -> p h t", h=NH)[:, :, 0:r],
                                 ACT.Copy).then_inc(S[done], 1)
                z_out(11, i)
                if i == 0:
                    act.wait_ge(S["var_done"], 1)
                    A.activation(squares[:, 0, 0:SEQ], bank[5][:, :], ACT.Sqrt, bias=epsb[:, :],
                                 scale=1.0 / CH).then_inc(S["cstd"], 1)
                    A.activation(squares[:, 0, SEQ:T], bank[4][:, 0:NS], ACT.Sqrt, bias=epsb[:, :],
                                 scale=1.0 / CH).then_inc(S["cstd"], 1)
                if i < TT - 1:
                    z_out(10, i + 1)
                if i == 1:
                    act.wait_ge(S["crstd"], 1)
                    for c in range(CT):
                        A.activation(catT[:, c, :], conv[:, c, :], ACT.Silu, bias=cpar[:, c, TAPS + 2:TAPS + 3],
                                     scale=cpar[:, c, TAPS + 1:TAPS + 2]).then_inc(S["cdone"], 1)
                    act.wait_ge(S["cdone"], CT)
                    A.activation(conv_hi[:, :, :], catT[:, 0:CT, :], ACT.Copy).then_inc(S["hT_sb"], 1)
                if i == TT - 2:
                    w_high(12)
                if i == TT - 1:
                    heads_high(0)
                    w_high(13)
                    heads_high(1)
                    heads_high(2)
                if i >= 1:
                    gated_out(i - 1)
            heads_high(TT - 2)
            act.wait_ge(S["r_upd"], 1 + NH * (TT - 2))
            act.dma_start(ret_p[0, 0].rearrange("h d e -> d h e"), Rst[:, :, :]).then_inc(S["rp_out"], 16)
            gated_out(TT - 1)
            heads_high(TT - 1)
            w_high(14)
            w_high(15)
            act.wait_ge(S["rs_upd"], 2 * NH)
            act.dma_start(pbc, ple_norm_g[0].partition_broadcast(P)).then_inc(S["pbc_in"], 16)
            act.dma_start(ret_s[0].rearrange("b h d e -> d b h e"), states).then_inc(S["rs_out"], 16)

            def x1_sq(i):
                r = rows(i)
                act.wait_ge(S["x1_sum"], WO.index((15, i)) + 1)
                if i >= 1:
                    act.wait_ge(S["x1_sq"], i)
                A.activation(junk[0:r, :], z[0:r, i, 0:2, :].rearrange("p a n -> p (a n)"), ACT.Square,
                             accum_out=ssq2[0:r, i:i + 1]).then_inc(S["x1_sq"], 1)
                act.wait_ge(S["x1_sq"], i + 1)
                A.activation(rst2[0:r, i:i + 1], ssq2[0:r, i:i + 1], ACT.Sqrt, bias=epsb[0:r, :],
                             scale=1.0 / D).then_inc(S["x1_std"], 1)

            def h2_store(i):
                r = rows(i)
                act.wait_ge(S["h2_done"], i + 1)
                act.dma_start(h2_d[i * P:i * P + r, :], h2[i][0:r, :]).then_inc(S["h2_out"], 16)

            def h2_out_low(i):
                act.wait_ge(S["h2T_ps"], i + 1)
                A.activation(hT[:, 0:4, tok(i)], bank[4][:, :].rearrange("p (k t) -> p k t", k=4)[:, :, 0:rows(i)],
                             ACT.Copy).then_inc(S["h2T_sb"], 1)

            def pT_out(turn, tiles):
                act.wait_ge(S["pT_ps"], turn)
                for i in tiles:
                    A.activation(pT[:, :, tok(i)], bank[7][:, 256 * (i % 2):256 * (i % 2) + 256].rearrange(
                        "p (k t) -> p k t", k=2)[:, :, 0:rows(i)], ACT.Copy).then_inc(S["pT_sb"], 1)

            def ple_out(i):
                r = rows(i)
                act.wait_ge(S["ple_done"], i + 1)
                for a in range(2):
                    A.activation(z[0:r, i, 2 + a, :], pair(2 - 2 * (i % 2))[a][0:r, :], ACT.Copy).then_inc(S["ple_raw"], 1)
                    act.wait_ge(S["x1_sq"], TT)
                    act.wait_ge(S["ple_raw"], 2 * i + a + 1)
                    if 2 * i + a:
                        act.wait_ge(S["ple_sq"], 2 * i + a)
                    A.activation(junk[0:r, 0:512], z[0:r, i, 2 + a, :], ACT.Square,
                                 accum_out=ssq3[0:r, i, a:a + 1]).then_inc(S["ple_sq"], 1)

            pT_out(1, (0, 1))
            pT_out(2, (2, 3))
            pT_out(3, (4,))
            x1_sq(0)
            x1_sq(1)
            h2_store(0)
            x1_sq(2)
            h2_store(1)
            h2_out_low(0)
            x1_sq(3)
            h2_store(2)
            h2_out_low(1)
            x1_sq(4)
            h2_store(3)
            h2_out_low(2)
            ple_out(0)
            h2_store(4)
            h2_out_low(3)
            act.dma_start(gbc[:, :], final_norm_g.partition_broadcast(P)).then_inc(S["final_in"], 16)
            ple_out(1)
            h2_out_low(4)
            for i in range(2, TT):
                ple_out(i)
            act.wait_ge(S["logit_sb"], 3)
            A.activation(gexp, gexp, ACT.Exp).then_inc(S["gexp_done"], 1)
            act.wait_ge(S["logit_sb"], 4)
            A.activation(e2, e2, ACT.Exp).then_inc(S["gexp_done"], 1)
            act.wait_ge(S["ple_var"], 1)
            A.activation(rst3[:, :], rst3[:, :], ACT.Sqrt, bias=epsb[:, :], scale=1.0 / D).then_inc(S["ple_std"], 1)

            def xt_half(par):
                return XT[:, par, 0:4, :], bank[2][:, :].rearrange("p (k s) -> p k s", k=4)

            def x_out(i, q):
                i, par = 2 * i + q // 2, q % 2
                act.wait_ge(S["xt_ps"], 2 * i + par + 1)
                A.activation(XT_hi[:, par, 0:4, :], xt_half(par)[1], ACT.Copy).then_inc(S["xt_sb"], 1)

            def w_high_part(i, q, m):
                if not (isinstance(i, int) and i == 0 and q == 0):
                    act.wait_ge(S["gu_done"], NX * i + q)
                i, par = 2 * i + q // 2, q % 2
                s = 3 * par + m
                act.wait_ge(slot_in[s], 16 * i + 16 * (LOADS[s] + 1))
                A.activation(cat_r[:, m * CHUNK:(m + 1) * CHUNK], ring[:, s, :], ACT.Copy).then_inc(S["w_hi"], 1)

            def silu(i, q):
                i, par = 2 * i + q // 2, q % 2
                act.wait_ge(S["gu_done"], 2 * i + par + 1)
                A.activation(gat[:, par, :], bank[par][:, 0:FF], ACT.Silu).then_inc(S["sil_done"], 1)

            def y_copy(i, q):
                i, par = 2 * i + q // 2, q % 2
                act.wait_ge(S["d_done"], 2 * i + par + 1)
                if isinstance(i, int):
                    if i == 0 and par == 0:
                        act.wait_ge(S["rs_out"], 16)
                    if i:
                        act.wait_ge(scattered[par], 16 * i)
                else:
                    act.wait_ge(scattered[par], 16 * i)
                A.activation(yout[:, par, 0:512], bank[5][:, :], ACT.Copy).then_inc(S["y_ready"], 1)

            def step(i, q, first=False, last=False):
                silu(i, q)
                if not last:
                    w_high_part(*after(i, q), 0)
                    x_out(*after(i, q))
                    w_high_part(*after(i, q), 1)
                if not first:
                    y_copy(*before(i, q))

            w_high_part(0, 0, 0)
            w_high_part(0, 0, 1)
            x_out(0, 0)
            step(0, 0, first=True)
            for q in range(1, NX):
                step(0, q)
            with act.Fori(1, LOOPS - 1) as i:
                for q in range(NX):
                    step(i, q)
            for q in range(NX):
                step(LOOPS - 1, q, last=q == NX - 1)
            y_copy(LOOPS - 1, NX - 1)

            act.wait_ge(S["idx_done"], 3)
            n_ov = act.value_load(ovinfo[0:1, NOV:NOV + 1], min_val=0, max_val=NOV)
            with act.If(n_ov > 0):
                with act.Fori(0, NOV) as j:
                    act.wait_ge(S["ov_xt"], j + 1)
                    A.activation(*xt_half(0), ACT.Copy).then_inc(S["ov_xtsb"], 1)
                    act.wait_ge(S["ov_gu"], j + 1)
                    A.activation(gat[:, 0, :], bank[0][:, 0:FF], ACT.Silu).then_inc(S["ov_sil"], 1)
                    act.wait_ge(S["ov_d"], j + 1)
                    A.activation(yout[:, 0, 0:512], bank[5][:, :], ACT.Copy).then_inc(S["ov_y"], 1)
            act.nop()

            def gate_high_part(c):
                act.wait_ge(slot_in[c], 16 * (LOADS[c] + NE // 2 + 1))
                A.activation(gate_high(c), ring[:, c, :], ACT.Copy).then_inc(S["w_hi"], 1)

            for c in range(3):
                gate_high_part(c)
            for i in range(TT + 1):
                if i < TT:
                    r = rows(i)
                    act.wait_ge(S["x2T_ps"], i + 1)
                    A.activation(h_hi[:, 0:4, tok(i)],
                                 bank[2 * (i % 2)][:, :].rearrange("p (k t) -> p k t", k=4)[:, :, 0:r],
                                 ACT.Copy).then_inc(S["x2T_low"], 1)
                    if i == 0:
                        gate_high_part(3)
                    if i + 2 < TT:
                        n = i + 2
                        act.wait_ge(S["x2_done"], i + 1)
                        act.dma_start(yins[i % 2][0:rows(n), :, :],
                                      moe2[n * P:n * P + rows(n), :, :]).then_inc(moe_in[i % 2], 16)
                if i >= 1:
                    t = i - 1
                    r = rows(t)
                    if t >= 2:
                        act.wait_ge(S["x3_done"], 2 * (t - 1))
                    for a in range(2):
                        act.wait_ge(S["pg_done"], 2 * t + a + 1)
                        A.activation(sg[0:r, t % 2, a * 512:(a + 1) * 512], pair(4 + 2 * (t % 2))[a][0:r, :],
                                     ACT.Sigmoid).then_inc(S["sg_done"], 1)
                    for a in range(2):
                        act.wait_ge(S["x3_done"], 2 * t + a + 1)
                        if 2 * t + a:
                            act.wait_ge(S["x3_sq"], 2 * t + a)
                        A.activation(junk[0:r, 0:512], xt[0:r, t % 2, a * 512:(a + 1) * 512], ACT.Square,
                                     accum_out=ssq4[0:r, t, a:a + 1]).then_inc(S["x3_sq"], 1)
                    act.wait_ge(S["out_done"], t + 1)
                    if t < TT - 1:
                        act.dma_start(y_rows(t), yo[0:r, t % 2, :]).then_inc(y_stored[t % 2], 16)
            act.wait_ge(S["out_done"], TT)
            act.dma_start(y_rows(TT - 1), yo[0:NS, (TT - 1) % 2, :]).then_inc(y_stored[0], 16)
            act.wait_ge(y_stored[0], 48)
            act.wait_ge(y_stored[1], 32)
            act.wait_ge(S["tail_out"], 16 * (1 + NB))
            act.wait_ge(S["cs_copy"], 16)
            act.wait_ge(S["rp_out"], 16)
            act.wait_ge(S["rs_out"], 16)

        @block.gpsimd
        def _(pool):
            G = nc.gpsimd
            order = [0]

            def then(ins):
                order[0] += 1
                ins.then_inc(S["pool_order"], 1)
                pool.wait_ge(S["pool_order"], order[0])

            G.memset(uext[:, :, 0:HIST], 0.0).then_inc(S["zero_x"], 1)
            ta = Sm[:, :, :]
            tb = qTx[:, :, :]

            def w_low(c):
                pool.wait_ge(S["w_hi"], c + 1)
                G.tensor_tensor(ring_r[:, c % 4, :], ring[:, c % 4, :], ring_r[:, 4 + c % 2, :].bitcast(F32),
                                ALU.subtract).then_inc(S["w_lo"], 1)

            def rotate(j, i):
                r = rows(i)
                pool.wait_ge(S["z_sb"], 2 * j * TT + TT + i + 1)
                v = z[0:r, i, j, :].rearrange("p (h a n) -> p h a n", h=NH, a=2)
                aa = ta[0:r].rearrange("p h (a n) -> p h a n", a=2)
                bb = tb[0:r].rearrange("p h (a n) -> p h a n", a=2)
                cos = bc(bc(rope_t[0:r, i, 0, :], 1, 2), 1, NH)
                sin = bc(bc(rope_t[0:r, i, 1, :], 1, 2), 1, NH)
                then(G.tensor_tensor(aa, v, cos, ALU.mult))
                then(G.tensor_tensor(bb, v, sin, ALU.mult))
                then(G.tensor_tensor(v[:, :, 0, :], aa[:, :, 0, :], bb[:, :, 1, :], ALU.subtract))
                G.tensor_tensor(v[:, :, 1, :], bb[:, :, 0, :], aa[:, :, 1, :], ALU.add).then_inc(S["rope_done"], 1)
                pool.wait_ge(S["rope_done"], j * TT + i + 1)

            pool.wait_ge(slot_in[0], 16)
            G.tensor_copy(ring_r[:, 4, :], ring[:, 0, :]).then_inc(S["w_hi"], 1)
            for c in range(7):
                w_low(c)
                if c == 0:
                    pool.wait_ge(S["const_in"], 16)
            for j in range(2):
                for i in range(3):
                    rotate(j, i)
                w_low(7 + 2 * j)
                rotate(j, 3)
                rotate(j, 4)
                w_low(8 + 2 * j)
            pool.wait_ge(S["u_done"], 2 * CT)
            for c in range(CT):
                G.tensor_copy(kTs[:, c, 0:NS].rearrange("p (b t) -> p b t", b=NB),
                              sext[:, c, :, HIST:HIST + NL]).then_inc(S["tail_u"], 1)
            w_low(11)

            def k_decay(i):
                r = rows(i)
                if i:
                    pool.wait_ge(S["o_done"], i)
                zeta = C("zeta" if i < TT - 1 else "zeta_s", r)
                G.tensor_tensor(kz[0:r, :].rearrange("p (h d) -> p h d", h=NH),
                                z[0:r, i, 1, :].rearrange("p (h d) -> p h d", h=NH), bc(zeta, 2, HD),
                                ALU.mult).then_inc(S["kz_done"], 1)

            def v_masks(h):
                if h:
                    pool.wait_ge(S["kvs_done"], 2 * h - 2)
                G.tensor_tensor(vmask[0], bc(z[0:NS, TT - 1, 2, h * HD:(h + 1) * HD], 1, NB),
                                bc(C("row8", NS), 2, HD), ALU.mult).then_inc(S["vm_done"], 1)

            k_decay(0)
            for i in range(TT):
                r = rows(i)
                if i == TT - 1:
                    pool.wait_ge(S["qTx_sb"], TT)
                    eye = C("eye8").rearrange("p (b c) -> p b c", b=NB)
                    for h in range(NH):
                        G.tensor_tensor(qmask[:, h, :, :].rearrange("p b (c t) -> p b c t", c=NB),
                                        bc(qTx[:, h, 0:NS].rearrange("p (c t) -> p c t", c=NB), 1, NB),
                                        bc(eye, 3, NL), ALU.mult).then_inc(S["qm_done"], 1)
                    w_low(13)
                if i == 1:
                    v_masks(0)
                pool.wait_ge(S["gn_var"], i + 1)
                G.tensor_tensor(grs[0:r, :], mv[0:r, :, 1], half[0:r, :], ALU.pow).then_inc(S["gn_rstd"], 1)
                if i == TT - 2:
                    w_low(12)
                if i < TT - 1:
                    k_decay(i + 1)
                pool.wait_ge(S["on_done"], NH * (i + 1))
                pool.wait_ge(S["z_sb"], 6 * TT + 2 * i + 2)
                G.tensor_tensor(z[0:r, i, 3, :], z[0:r, i, 3, :], z[0:r, i, 0, :], ALU.mult).then_inc(S["og_done"], 1)
            v_masks(2)
            w_low(14)
            w_low(15)

            pool.wait_ge(S["idx_done"], 2)
            pool.wait_ge(S["h2_out"], 16 * TT)
            pool.wait_ge(S["h2T_ps"], TT)

            def wait(on, value):
                pool.wait_ge(on, value)
                pool.sem_inc(S["ticks"], 1)

            def column(dst, src, n, done, count):
                G.tensor_copy(dst, src[:, bass.ds(n, 1)]).then_inc(done, 1)
                wait(done, count)

            def sizes(e):
                n = pool.value_load(ovinfo[0:1, bass.ds(e + NOV + 1, 1)], min_val=0, max_val=T)
                return n <= HALF, n > HALF

            def gather(i, q):
                if not (isinstance(i, int) and i == 0):
                    wait(S["xt_ps"], NX * i + q - (NX - 1))
                column(cur_tok[:, q:q + 1], tokidx, NX * i + q, S["cur_done"], NX * i + q + 1)
                few, many = sizes(NX * i + q)
                for case, r in ((many, P), (few, HALF)):
                    with pool.If(case):
                        G.indirect_dma_start(X[q][0:r, :], None, h2_d,
                                             bass.IndirectOffsetOnAxis(ap=cur_tok[0:r, q:q + 1], axis=0),
                                             bounds_check=T - 1, oob_is_err=False).then_inc(gathered[q], 16)

            def scatter(i, q):
                i, par = 2 * i + q // 2, q % 2
                if not (isinstance(i, int) and i == 0):
                    wait(scattered[par], 16 * i)
                column(cur_code[:, par:par + 1], codes, 2 * i + par, S["pool_codes"], 2 * i + par + 1)
                few, many = sizes(2 * i + par)
                wait(S["y_ready"], 2 * (2 * i + par) + 2)
                for case, r in ((many, P), (few, HALF)):
                    with pool.If(case):
                        G.indirect_dma_start(moe_d, bass.IndirectOffsetOnAxis(ap=cur_code[0:r, par:par + 1], axis=0),
                                             yout[0:r, par, :], None, bounds_check=2 * T - 1,
                                             oob_is_err=False).then_inc(scattered[par], 16)

            wait(S["rs_out"], 16)
            for q in range(NX):
                gather(0, q)
            for q in range(NX):
                gather(1, q)
                scatter(0, q)
            with pool.Fori(1, LOOPS - 1) as i:
                for q in range(NX):
                    gather(i + 1, q)
                    scatter(i, q)
            for q in range(NX):
                scatter(LOOPS - 1, q)

            pool.wait_ge(S["idx_done"], 3)
            n_ov = pool.value_load(ovinfo[0:1, NOV:NOV + 1], min_val=0, max_val=NOV)
            pool.wait_ge(scattered[0], 8 * NE)
            pool.wait_ge(scattered[1], 8 * NE)
            pool.sem_inc(S["ov_end"], 1)
            with pool.If(n_ov > 0):
                with pool.Fori(0, NOV) as j:
                    G.tensor_copy(cur_tok[:, 0:1], tokidx[:, bass.ds(j + NE, 1)]).then_inc(S["ov_cur"], 1)
                    G.tensor_copy(cur_code[:, 0:1], codes[:, bass.ds(j + NE, 1)]).then_inc(S["ov_cur"], 1)
                    wait(S["ov_cur"], 2 * j + 2)
                    G.indirect_dma_start(X[0], None, h2_d, bass.IndirectOffsetOnAxis(ap=cur_tok[:, 0:1], axis=0),
                                         bounds_check=T - 1, oob_is_err=False).then_inc(S["ov_gather"], 16)
                    wait(S["ov_y"], 2 * j + 2)
                    G.indirect_dma_start(moe_d, bass.IndirectOffsetOnAxis(ap=cur_code[:, 0:1], axis=0),
                                         yout[:, 0, :], None, bounds_check=2 * T - 1,
                                         oob_is_err=False).then_inc(S["ov_out"], 16)
                    wait(S["ov_out"], 16 * j + 16)
                    pool.sem_inc(S["ov_end"], 1)
            pool.nop()
            pool.sem_inc(S["moe_out"], 1)

            for i in range(TT):
                r = rows(i)
                v = rst4[0:r, i:i + 1]
                pool.wait_ge(S["x3_sq"], 2 * i + 2)
                then(G.tensor_tensor(v, ssq4[0:r, i, 0:1], ssq4[0:r, i, 1:2], ALU.add))
                then(G.tensor_scalar(v, v, 1.0 / D, EPS, ALU.mult, ALU.add))
                G.tensor_tensor(v, v, half[0:r, 0:1], ALU.pow).then_inc(S["x3_rstd"], 1)


_INS = ["x_prompt", "x_sample", "p_prompt", "p_sample", "state_conv", "state_ret", "w_in", "conv_w", "conv_b",
        "conv_ln_g", "conv_ln_b", "w_out", "norm1_g", "norm2_g", "router_group_w", "router_group_b",
        "router_expert_w", "router_expert_b", "w_expert_gate", "w_expert_up", "w_expert_down", "w_ple",
        "ple_norm_g", "w_ple_gate", "final_norm_g"]
_OUTS = [(1, SEQ, D), (NB, NL, D), (1, 1, HIST, CH), (1, 1, NH, HD, HD), (1, NB, HIST, CH), (1, NB, NH, HD, HD)]


def kernel(**inputs):
    import concourse.bacc as _bacc
    from concourse.bass_utils import run_bass_kernel_spmd as _run

    nc = _bacc.Bacc("TRN2", target_bir_lowering=False, num_devices=1)
    arrays, args = {}, []
    for name in _INS:
        a = np.ascontiguousarray(inputs[name])
        arrays[f"in_{name}"] = a
        args.append(nc.dram_tensor(f"in_{name}", a.shape, mybir.dt.from_np(a.dtype), kind="ExternalInput").ap())
    arrays["constants"] = constants()
    args.append(nc.dram_tensor("constants", (P, NCONST), F32, kind="ExternalInput").ap())
    outs = [nc.dram_tensor(f"out_{i}", shape, F32, kind="ExternalOutput").ap() for i, shape in enumerate(_OUTS)]
    build(nc, args, outs)
    r = _run(nc, [arrays], core_ids=[0])
    return tuple(r.results[0][f"out_{i}"] for i in range(len(_OUTS)))
```
